# Optimizing a Trainium2 kernel written in Bass

```python
import math
import jax
import jax.numpy as jnp
from jax import lax
import numpy as np

D_MODEL = 1024
BATCH = 1
SEQ = 512
DEPTH = 2

LRU_WIDTH = D_MODEL
LRU_BLOCKS = 8
LRU_BLOCK = LRU_WIDTH // LRU_BLOCKS
CONV_WIDTH = 4
LRU_C = 8.0
FOX_HEADS = 16
FOX_HEAD_DIM = D_MODEL // FOX_HEADS
FOX_WIDTH = FOX_HEADS * FOX_HEAD_DIM
FOX_BLOCK = 128
MLSTM_HEADS = 8
MLSTM_HEAD_DIM = D_MODEL // MLSTM_HEADS
MLSTM_WIDTH = MLSTM_HEADS * MLSTM_HEAD_DIM
MLSTM_CHUNK = 64
N_BRANCHES = 3
PEER_HEADS = 8
PEER_TOPK = 16
N_KEYS = 128
N_EXPERTS = N_KEYS * N_KEYS
PEER_QDIM = 256
PEER_HALF = PEER_QDIM // 2
PEER_BLOCK = 64
NORM_EPS = 1e-6
IN_SIZES = (LRU_WIDTH, 3 * FOX_WIDTH, FOX_HEADS, 3 * MLSTM_WIDTH, 2 * MLSTM_HEADS, MLSTM_WIDTH, N_BRANCHES * D_MODEL)
IN_COLS = LRU_WIDTH + 3 * FOX_WIDTH + FOX_HEADS + 3 * MLSTM_WIDTH + 2 * MLSTM_HEADS + MLSTM_WIDTH + N_BRANCHES * D_MODEL

kernel_name = 'hybrid_rglru_fox_mlstm_peer'

def rms_norm(x, w):
    xf = x.astype(jnp.float32)
    y = xf * lax.rsqrt(jnp.mean(xf * xf, axis=-1, keepdims=True) + NORM_EPS)
    return (y * w.astype(jnp.float32)).astype(x.dtype)

def head_layer_norm(h, w):
    mu = jnp.mean(h, axis=-1, keepdims=True)
    hc = h - mu
    var = jnp.mean(hc * hc, axis=-1, keepdims=True)
    return hc * lax.rsqrt(var + NORM_EPS) * w.astype(jnp.float32)

def split_columns(proj):
    cuts = []
    acc = 0
    for s in IN_SIZES[:-1]:
        acc += s
        cuts.append(acc)
    return jnp.split(proj, cuts, axis=-1)

def causal_depthwise_conv(x, w, b):
    S = x.shape[1]
    xp = jnp.pad(x, ((0, 0), (CONV_WIDTH - 1, 0), (0, 0)))
    y = xp[:, 0:S] * w[0] + b
    for k in range(1, CONV_WIDTH):
        y = y + xp[:, k:k + S] * w[k]
    return y

def rg_lru(x, wa, ba, wx, bx, lam):
    B, S, W = x.shape
    xb = x.reshape(B, S, LRU_BLOCKS, LRU_BLOCK)
    r = jax.nn.sigmoid(jnp.einsum('bsgi,gij->bsgj', xb, wa).reshape(B, S, W) + ba)
    i = jax.nn.sigmoid(jnp.einsum('bsgi,gij->bsgj', xb, wx).reshape(B, S, W) + bx)
    log_a = (-LRU_C * r * jax.nn.softplus(-lam)).astype(jnp.float32)
    a = jnp.exp(log_a)
    u = jnp.sqrt(-jnp.expm1(2.0 * log_a)) * (i * x).astype(jnp.float32)

    def combine(left, right):
        a1, b1 = left
        a2, b2 = right
        return a1 * a2, a2 * b1 + b2

    _, h = lax.associative_scan(combine, (a, u), axis=1)
    return h.astype(x.dtype)

def forgetting_attention(q, k, v, f_logit):
    B, S, H, d = q.shape
    f32 = jnp.float32
    qh = q.astype(f32).transpose(0, 2, 1, 3) * (d ** -0.5)
    kh = k.astype(f32).transpose(0, 2, 1, 3)
    vh = v.astype(f32).transpose(0, 2, 1, 3)
    c = jnp.cumsum(jax.nn.log_sigmoid(f_logit.astype(f32)), axis=1).transpose(0, 2, 1)
    kpos = jnp.arange(S)

    def block(j):
        start = j * FOX_BLOCK
        qb = lax.dynamic_slice_in_dim(qh, start, FOX_BLOCK, axis=2)
        cb = lax.dynamic_slice_in_dim(c, start, FOX_BLOCK, axis=2)
        qpos = start + jnp.arange(FOX_BLOCK)
        s = jnp.einsum('bhqd,bhkd->bhqk', qb, kh) + cb[..., :, None] - c[:, :, None, :]
        s = jnp.where(kpos[None, :] <= qpos[:, None], s, -jnp.inf)
        return jnp.einsum('bhqk,bhkd->bhqd', jax.nn.softmax(s, axis=-1), vh)

    o = lax.map(block, jnp.arange(S // FOX_BLOCK))
    return o.transpose(1, 0, 3, 2, 4).reshape(B, S, H * d).astype(q.dtype)

def mlstm_mixer(q, k, v, ig, fg, o_pre, norm_w):
    B, S, H, d = q.shape
    L = MLSTM_CHUNK
    nc = S // L
    f32 = jnp.float32

    def chunk4(t):
        return t.astype(f32).reshape(B, nc, L, H, d).transpose(1, 0, 3, 2, 4)

    def chunk3(t):
        return t.astype(f32).reshape(B, nc, L, H).transpose(1, 0, 3, 2)

    qc = chunk4(q)
    kc = chunk4(k) * (d ** -0.5)
    vc = chunk4(v)
    igc = chunk3(ig)
    lfc = chunk3(jax.nn.log_sigmoid(fg.astype(f32)))
    tril = jnp.arange(L)[:, None] >= jnp.arange(L)[None, :]

    def step(carry, inp):
        C, n, m = carry
        qb, kb, vb, ib, lb = inp
        b = jnp.cumsum(lb, axis=-1)
        dmat = jnp.where(tril, b[..., :, None] - b[..., None, :] + ib[..., None, :], -jnp.inf)
        inter = b + m[..., None]
        m_t = jnp.maximum(inter, jnp.max(dmat, axis=-1))
        w_ts = jnp.exp(dmat - m_t[..., None]) * jnp.einsum('bhtd,bhsd->bhts', qb, kb)
        dq = jnp.exp(inter - m_t)
        num = dq[..., None] * jnp.einsum('bhtd,bhde->bhte', qb, C) + jnp.einsum('bhts,bhse->bhte', w_ts, vb)
        den = dq * jnp.einsum('bhtd,bhd->bht', qb, n) + jnp.sum(w_ts, axis=-1)
        h = num / jnp.maximum(jnp.abs(den), jnp.exp(-m_t))[..., None]
        b_last = b[..., -1]
        g = b_last[..., None] - b + ib
        m_new = jnp.maximum(b_last + m, jnp.max(g, axis=-1))
        decay = jnp.exp(b_last + m - m_new)
        kw = kb * jnp.exp(g - m_new[..., None])[..., None]
        C_new = decay[..., None, None] * C + jnp.einsum('bhsd,bhse->bhde', kw, vb)
        n_new = decay[..., None] * n + jnp.sum(kw, axis=2)
        return (C_new, n_new, m_new), h

    init = (jnp.zeros((B, H, d, d), f32), jnp.zeros((B, H, d), f32), jnp.zeros((B, H), f32))
    _, hs = lax.scan(step, init, (qc, kc, vc, igc, lfc))
    h = hs.transpose(1, 0, 3, 2, 4).reshape(B, S, H, d)
    h = head_layer_norm(h, norm_w.reshape(H, d)).reshape(B, S, H * d)
    return (h * jax.nn.sigmoid(o_pre.astype(f32))).astype(q.dtype)

def token_mixer(xn, w_in, conv_w, conv_b, wa, ba, wx, bx, lam, fox_fb, m_ib, m_fb, m_nw,
                gate_b, w_br_lru, w_br_fox, w_br_mlstm, w_out):
    B, S, _ = xn.shape
    lru_in, fox_qkv, fox_f, ml_qkv, ml_if, ml_o, gate_in = split_columns(xn @ w_in)
    ya = rg_lru(causal_depthwise_conv(lru_in, conv_w, conv_b), wa, ba, wx, bx, lam)
    fqkv = fox_qkv.reshape(B, S, 3, FOX_HEADS, FOX_HEAD_DIM)
    yb = forgetting_attention(fqkv[:, :, 0], fqkv[:, :, 1], fqkv[:, :, 2], fox_f + fox_fb)
    mqkv = ml_qkv.reshape(B, S, 3, MLSTM_HEADS, MLSTM_HEAD_DIM)
    yc = mlstm_mixer(mqkv[:, :, 0], mqkv[:, :, 1], mqkv[:, :, 2],
                     ml_if[..., :MLSTM_HEADS] + m_ib, ml_if[..., MLSTM_HEADS:] + m_fb, ml_o, m_nw)
    g = jax.nn.sigmoid(gate_in + gate_b).reshape(B, S, N_BRANCHES, D_MODEL)
    merged = g[:, :, 0] * (ya @ w_br_lru) + g[:, :, 1] * (yb @ w_br_fox) + g[:, :, 2] * (yc @ w_br_mlstm)
    return merged @ w_out

def peer_ffn(x, wq, sub1, sub2, u_tab, v_tab):
    B, S, D = x.shape
    f32 = jnp.float32
    q = (x @ wq).reshape(B, S, PEER_HEADS, PEER_QDIM).astype(f32)
    s1 = jnp.einsum('bshd,nd->bshn', q[..., :PEER_HALF], sub1.astype(f32))
    s2 = jnp.einsum('bshd,nd->bshn', q[..., PEER_HALF:], sub2.astype(f32))
    v1, i1 = lax.top_k(s1, PEER_TOPK)
    v2, i2 = lax.top_k(s2, PEER_TOPK)
    cand = (v1[..., :, None] + v2[..., None, :]).reshape(B, S, PEER_HEADS, PEER_TOPK * PEER_TOPK)
    cidx = (i1[..., :, None] * N_KEYS + i2[..., None, :]).reshape(B, S, PEER_HEADS, PEER_TOPK * PEER_TOPK)
    top_s, pos = lax.top_k(cand, PEER_TOPK)
    idx = jnp.take_along_axis(cidx, pos, axis=-1)
    wgt = jax.nn.softmax(top_s, axis=-1)
    nb = S // PEER_BLOCK
    xb = x.reshape(B, nb, PEER_BLOCK, D).swapaxes(0, 1)
    ib = idx.reshape(B, nb, PEER_BLOCK, PEER_HEADS, PEER_TOPK).swapaxes(0, 1)
    wb = wgt.reshape(B, nb, PEER_BLOCK, PEER_HEADS, PEER_TOPK).swapaxes(0, 1)

    def block(args):
        xc, ic, wc = args
        act = jax.nn.gelu(jnp.einsum('bphkd,bpd->bphk', u_tab[ic], xc).astype(f32))
        coef = (wc * act).astype(x.dtype)
        return jnp.einsum('bphk,bphkd->bpd', coef, v_tab[ic])

    out = lax.map(block, (xb, ib, wb))
    return out.swapaxes(0, 1).reshape(B, S, D)

def setup_inputs(seed: int = 0) -> dict:
    key = jax.random.key(seed)
    ks = jax.random.split(key, 26)
    f32 = jnp.float32

    def nrm(k, shape, scale):
        return jax.random.normal(k, shape, f32) * scale

    a_pow = jax.random.uniform(ks[9], (DEPTH, LRU_WIDTH), f32, 0.9, 0.999)
    a0 = a_pow ** (1.0 / LRU_C)
    return {
        'x': nrm(ks[0], (BATCH, SEQ, D_MODEL), 1.0),
        'norm1_w': 1.0 + nrm(ks[1], (DEPTH, D_MODEL), 0.05),
        'w_in': nrm(ks[2], (DEPTH, D_MODEL, IN_COLS), D_MODEL ** -0.5),
        'lru_conv_w': nrm(ks[3], (DEPTH, CONV_WIDTH, LRU_WIDTH), CONV_WIDTH ** -0.5),
        'lru_conv_b': nrm(ks[4], (DEPTH, LRU_WIDTH), 0.02),
        'lru_wa': nrm(ks[5], (DEPTH, LRU_BLOCKS, LRU_BLOCK, LRU_BLOCK), LRU_BLOCK ** -0.5),
        'lru_ba': nrm(ks[6], (DEPTH, LRU_WIDTH), 0.02),
        'lru_wx': nrm(ks[7], (DEPTH, LRU_BLOCKS, LRU_BLOCK, LRU_BLOCK), LRU_BLOCK ** -0.5),
        'lru_bx': nrm(ks[8], (DEPTH, LRU_WIDTH), 0.02),
        'lru_lambda': jnp.log(a0) - jnp.log1p(-a0),
        'fox_fgate_b': jax.random.uniform(ks[10], (DEPTH, FOX_HEADS), f32, 1.0, 5.0),
        'mlstm_igate_b': nrm(ks[11], (DEPTH, MLSTM_HEADS), 0.1),
        'mlstm_fgate_b': jnp.linspace(3.0, 6.0, MLSTM_HEADS, dtype=f32)[None, :] + nrm(ks[12], (DEPTH, MLSTM_HEADS), 0.05),
        'mlstm_norm_w': 1.0 + nrm(ks[13], (DEPTH, MLSTM_WIDTH), 0.05),
        'merge_gate_b': nrm(ks[14], (DEPTH, N_BRANCHES * D_MODEL), 0.02),
        'w_br_lru': nrm(ks[15], (DEPTH, LRU_WIDTH, D_MODEL), LRU_WIDTH ** -0.5),
        'w_br_fox': nrm(ks[16], (DEPTH, FOX_WIDTH, D_MODEL), FOX_WIDTH ** -0.5),
        'w_br_mlstm': nrm(ks[17], (DEPTH, MLSTM_WIDTH, D_MODEL), MLSTM_WIDTH ** -0.5),
        'w_out': nrm(ks[18], (DEPTH, D_MODEL, D_MODEL), D_MODEL ** -0.5),
        'norm2_w': 1.0 + nrm(ks[19], (DEPTH, D_MODEL), 0.05),
        'peer_wq': nrm(ks[20], (DEPTH, D_MODEL, PEER_HEADS * PEER_QDIM), D_MODEL ** -0.5),
        'peer_subkeys1': nrm(ks[21], (DEPTH, N_KEYS, PEER_HALF), PEER_HALF ** -0.5),
        'peer_subkeys2': nrm(ks[22], (DEPTH, N_KEYS, PEER_HALF), PEER_HALF ** -0.5),
        'peer_u': nrm(ks[23], (DEPTH, N_EXPERTS, D_MODEL), D_MODEL ** -0.5),
        'peer_v': nrm(ks[24], (DEPTH, N_EXPERTS, D_MODEL), PEER_HEADS ** -0.5),
        'final_norm_w': 1.0 + nrm(ks[25], (D_MODEL,), 0.05),
    }

def reference(x, norm1_w, w_in, lru_conv_w, lru_conv_b, lru_wa, lru_ba, lru_wx, lru_bx, lru_lambda,
              fox_fgate_b, mlstm_igate_b, mlstm_fgate_b, mlstm_norm_w, merge_gate_b,
              w_br_lru, w_br_fox, w_br_mlstm, w_out, norm2_w,
              peer_wq, peer_subkeys1, peer_subkeys2, peer_u, peer_v, final_norm_w):
    for l in range(DEPTH):
        xn = rms_norm(x, norm1_w[l])
        x = x + token_mixer(xn, w_in[l], lru_conv_w[l], lru_conv_b[l], lru_wa[l], lru_ba[l],
                            lru_wx[l], lru_bx[l], lru_lambda[l], fox_fgate_b[l], mlstm_igate_b[l],
                            mlstm_fgate_b[l], mlstm_norm_w[l], merge_gate_b[l],
                            w_br_lru[l], w_br_fox[l], w_br_mlstm[l], w_out[l])
        hn = rms_norm(x, norm2_w[l])
        x = x + peer_ffn(hn, peer_wq[l], peer_subkeys1[l], peer_subkeys2[l], peer_u[l], peer_v[l])
    return rms_norm(x, final_norm_w)


_drawn_inputs = setup_inputs


def setup_inputs(seed=0):
    import zlib

    import numpy as np

    out = dict(_drawn_inputs(seed))
    spreads = {}
    factors = {'lru_ba': 4.087, 'lru_bx': 3.281, 'mlstm_igate_b': 64.0, 'merge_gate_b': 2.767}
    for name, (base, spread) in spreads.items():
        noise = np.random.default_rng([zlib.crc32(name.encode()), seed]).standard_normal(out[name].shape)
        drawn = base * np.exp(spread * noise) if base else spread * noise
        out[name] = jnp.asarray(drawn.astype(out[name].dtype))
    for name, factor in factors.items():
        out[name] = (out[name] * factor).astype(out[name].dtype)
    return out
```

```python
from contextlib import ExitStack

import concourse.bass as bass
from concourse import mybir
import numpy as np

F32 = mybir.dt.float32
I32 = mybir.dt.int32
U32 = mybir.dt.uint32
ALU = mybir.AluOpType
ACT = mybir.ActivationFunctionType
AX = mybir.AxisListType
ds = bass.ds

P = 128
SEQ = 512
D = 1024
DEPTH = 2
TT = SEQ // P
KC = D // P
EPS = 1e-6
FOX_H, FOX_D = 16, 64
ML_H, ML_D = 8, 128
CONV = 4
TOPK = 16
N_KEYS = 128
PEER_H = 8
SLOTS = PEER_H * TOPK
GR = 8
NEG = -1e30

C_LRU, C_FOX, C_FOXF = 0, D, D + 3 * D
C_ML = C_FOXF + FOX_H
C_MLI = C_ML + 3 * D
C_MLF = C_MLI + ML_H
C_O = C_MLF + ML_H
C_GATE = C_O + D
NROW = ML_H + FOX_H

ROUNDS = dict(LRU=2, FV=2, MA=4, FQ=4, MO=2, MB=4, MV=2, MQ=4, MC=4, OUT=2, WQ=4)
NROUND = sum(ROUNDS.values())
ROUND0 = {p: sum(list(ROUNDS.values())[:n]) for n, p in enumerate(ROUNDS)}

PV_COLS = {}
_at = 0
for _n, _w in (("conv_w", CONV * KC), ("conv_b", KC), ("ba", KC), ("bx", KC), ("gate_b", 3 * KC),
               ("lam", KC), ("nw", KC), ("fbias", 1), ("ibias", 1), ("wgate", KC * 32), ("sub", 2 * P)):
    PV_COLS[_n] = (_at, _at + _w)
    _at += _w
PV = _at


class Count:

    def __init__(self, sem, plan, credit=0):
        self.sem, self.plan, self.credit, self.start = sem, plan, credit, {}
        n = 0
        for phase, (iters, per) in plan.items():
            self.start[phase] = n
            n += iters * per
        self.total = n

    def at(self, L, phase, i, n):
        return L * self.total + i * self.plan[phase][1] + (self.start[phase] + n + self.credit)


class Chain:

    def __init__(self, eng, count, L, phase, i):
        self.eng, self.count, self.where, self.n = eng, count, (L, phase, i), 0

    def step(self, ins):
        ins.then_inc(self.count.sem, 1)
        self.n += 1

    def wait(self):
        self.eng.wait_ge(self.count.sem, self.count.at(*self.where, self.n))

    def close(self):
        want = self.count.plan[self.where[1]][1]
        assert self.n == want, f"{self.where[1]}: {self.n} steps, {want} planned"


def fox_steps():
    seq = [("C", 0)]
    for k in range(16 + 3):
        if k < 16:
            seq.append(("S", k))
        if k % 4 == 2 and k < 13:
            seq.append(("C", k // 4 + 1))
        if 2 <= k < 18:
            seq.append(("T", k - 2))
        if k >= 3:
            seq.append(("V", k - 3))
            if (k - 3) % 8 == 7:
                seq.append(("Y", (k - 3) // 8))
    return seq


def build(nc, x_in, w_stream, w_lru, pvec, nrows, fnorm, u_tab, v_tab, out):
    with ExitStack() as ctx:
        def sb(name, shape, dt=F32):
            return ctx.enter_context(nc.sbuf_tensor(name, shape, dt))

        def sem(name):
            return ctx.enter_context(nc.semaphore(name))

        bank = [ctx.enter_context(nc.psum_tensor(f"bank{b}", [P, SEQ], F32)) for b in range(8)]

        x = sb("x", [P, TT, D])
        hn = sb("hn", [P, TT, D])
        xT = sb("xT", [P, KC, SEQ])
        ring = [sb(f"ring{s}", [P, D]) for s in range(4)]
        lruw = sb("lruw", [P, 4, 2, P])
        pv = sb("pv", [P, PV])
        nwb = sb("nwb", [P, 2, D])
        big = sb("big", [P, 2 * KC, SEQ])
        yT = big[:, 0:KC, :]
        merged = big[:, KC:2 * KC, :]
        bflat = big[:, :, :].rearrange("p a n -> p (a n)")
        vg = sb("vg", [P, 2 * KC, SEQ])
        v_sb = vg[:, 0:KC, :].rearrange("p (t a) c -> p t (a c)", t=TT)
        og = vg[:, KC:2 * KC, :]
        gring = vg[:, :, :].rearrange("p (r a) c -> p r (a c)", r=GR)
        qk = sb("qk", [P, 4, SEQ])
        att = sb("att", [P, 8192])
        ident = sb("ident", [P, P])
        ones = sb("ones", [P, SEQ])
        inv = sb("inv", [P, P])
        mask_q = sb("mask_q", [P, P])
        mask_k = sb("mask_k", [P, P])
        iota_i = sb("iota_i", [P, TOPK], I32)
        iota_f = sb("iota_f", [P, TOPK])
        eps_t = sb("eps_t", [P, 1])
        stat = sb("stat", [P, 4, TT])
        hb = sb("hb", [P, 5 * KC])
        nsp = sb("nsp", [P, KC])
        hnw = sb("hnw", [P, KC])
        lp = sb("lp", [P, 3, KC])
        first_expert = sb("first_expert", [P, 1])
        rows = att[0:NROW, 0:6 * SEQ].rearrange("p (a n) -> p a n", a=6)
        cum = sb("cum", [NROW, SEQ])
        g_row = sb("g_row", [ML_H, SEQ])
        G_row = sb("G_row", [ML_H, SEQ])
        m_row = sb("m_row", [ML_H, SEQ])
        cumc = sb("cumc", [P, TT, NROW])
        gcol = sb("gcol", [P, TT, ML_H])
        sel = sb("sel", [NROW, 4, P])
        vst = sb("vst", [P, TT, 2, P])
        hflat = hn[:, :, :].rearrange("p t d -> p (t d)")
        NPAD = SEQ + CONV - 1
        xpad = hflat[:, 0:4 * NPAD].rearrange("p (s n) -> p s n", s=4)
        gt = [hflat[:, (5 + j) * SEQ:(6 + j) * SEQ] for j in range(2)]
        mtmp = hflat[:, 7 * SEQ:8 * SEQ]

        xc = merged[:, 0:4, :]
        R = merged[:, 4:8, :]
        TI = og[:, 0:4, :]
        A = og[:, 4:8, :]
        TH = qk
        sc = att[:, 0:1024].rearrange("p (a n) -> p a n", a=2)
        pr = att[:, 1024:2048].rearrange("p (a n) -> p a n", a=2)
        pT = att[:, 2048:3072].rearrange("p (a n) -> p a n", a=2)
        cb = att[:, 3072:4096].rearrange("p (a n) -> p a n", a=2)
        ytok = att[:, 4096:4608].rearrange("p (t n) -> p t n", t=TT)
        nmax = att[:, 4608:4624]
        rsum = att[:, 4624:4640]
        rinv = att[:, 4640:4656]
        E = att[:, 0:4096].rearrange("p (a s n) -> p a s n", a=2, s=4)
        gb = att[:, 4096:4608]
        gdm = att[:, 4608:5120].rearrange("p (s n) -> p s n", s=4)
        em = att[:, 5120:6144].rearrange("p (a n) -> p a n", a=2)
        hh = att[:, 6144:7168].rearrange("p (a n) -> p a n", a=2)
        sq = att[:, 7168:8192].rearrange("p (a n) -> p a n", a=2)
        keys = bflat[:, 0:2048].rearrange("p (g n) -> p g n", g=16)
        kval = bflat[:, 2048:2304].rearrange("p (g n) -> p g n", g=16)
        vals = bflat[:, 2304:3328].rearrange("p (t a n) -> p t a n", t=TT, n=TOPK)
        idxf = bflat[:, 3328:4352].rearrange("p (t a n) -> p t a n", t=TT, n=TOPK)
        kidx = sb("kidx", [P, 16, TOPK], U32)
        cand = att[:, 0:2048].rearrange("p (h n) -> p h n", h=PEER_H)
        eqb = att[:, 2048:4096]
        tv = att[:, 4608:4736].rearrange("p (h n) -> p h n", h=PEER_H)
        posa = att[:, 4736:4864]
        posb = att[:, 4864:4992]
        e1 = att[:, 4992:5120]
        e2 = att[:, 5120:5248]
        wts = att[:, 5248:5376]
        actv = att[:, 5376:5504]
        th = att[:, 5504:5632]
        gin = att[:, 5632:5760]
        coef = att[:, 5760:5888]
        ssum = att[:, 5888:5896]
        posu = sb("posu", [P, SLOTS], U32)
        posu2 = sb("posu2", [P, 2, SLOTS], U32)
        eidx = sb("eidx", [P, TT, SLOTS], U32)
        estage = [sb(f"estage{h}", [P, GR], U32) for h in range(2)]

        def pcol(name, a, b=None):
            c0 = PV_COLS[name][0]
            return pv[:, c0 + a:c0 + (a + 1 if b is None else b)]

        def dcol(buf, at):
            return buf[:, ds(at, 1)]

        wgate = pcol("wgate", 0, KC * 32).rearrange("p (k n) -> p k n", k=KC)
        subk = pcol("sub", 0, 2 * P).rearrange("p (a n) -> p a n", a=2)

        x_loaded = sem("x_loaded")
        fnw_loaded = sem("fnw_loaded")
        consts_ready = sem("consts_ready")
        pool_step = sem("pool_step")
        params_ready = sem("params_ready")
        lruw_ready = sem("lruw_ready")
        w_ready = [sem(f"w_ready{s}") for s in range(4)]
        proj_done = sem("proj_done")
        g_ready = [sem(f"g_ready{q}") for q in range(GR)]
        out_done = sem("out_done")
        out_ready = sem("out_ready")
        pool_stage = sem("pool_stage")
        waits_taken = sem("waits_taken")
        pad_ready = sem("pad_ready")
        ms_final = sem("ms_final")
        sd_final = sem("sd_final")
        final_step = sem("final_step")
        drained_sem = [sem(f"drained{b}") for b in range(8)]
        drained = [Count(drained_sem[s], {p: (n, 1) for p, n in ROUNDS.items()}, 1) for s in range(4)]
        work = [dict(N1=(1, 2), G=(1, int(b < 2)), LRU=(2, 2), COLS=(1, int(b >= 2)),
                     FQ=(4, (8, 8, 16, 22)[b]), MQ=(4, (4, 4, 6, 6)[b]), N2=(1, 2), WQ=(4, 1))
                for b in range(4)]
        drained += [Count(drained_sem[4 + b], work[b], 1) for b in range(4)]
        filled = {4 + b: Count(sem(f"filled{4 + b}"), work[b]) for b in range(4)}
        one = lambda *names: {n: (1, 1) for n in names}
        layer_done = Count(sem("layer_done"), one("L"), 1)
        ms_ready = Count(sem("ms_ready"), one("N1", "N2"))
        sd_ready = Count(sem("sd_ready"), one("N1", "N2"))
        hn_ready = Count(sem("hn_ready"), dict(N1=(1, TT), N2=(1, TT)))
        zexp_in = Count(sem("zexp_in"), one("P", "G"))
        zexp_out = Count(sem("zexp_out"), one("P", "G"))
        rows_ready = Count(sem("rows_ready"), one("G"))
        conv_done = Count(sem("conv_done"), dict(LRU=(2, 4)))
        la_ready = Count(sem("la_ready"), dict(LRU=(2, 1)))
        ea_ready = Count(sem("ea_ready"), dict(LRU=(2, 2)))
        q_ready = Count(sem("q_ready"), dict(LRU=(2, 1)))
        sq_ready = Count(sem("sq_ready"), dict(LRU=(2, 1)))
        lru_done = Count(sem("lru_done"), dict(LRU=(2, 1)), 1)
        merged_ready = Count(sem("merged_ready"), dict(MB=(4, 2), MC=(4, 2)), 1)
        sel_ready = Count(sem("sel_ready"), dict(FQ=(4, 1), MQ=(4, 1)))
        vst_ready = Count(sem("vst_ready"), dict(MQ=(4, 1)))
        srow_ready = Count(sem("srow_ready"), dict(FQ=(4, 16)))
        prob_ready = Count(sem("prob_ready"), dict(FQ=(4, 16)), 2)
        rinv_ready = Count(sem("rinv_ready"), dict(FQ=(4, 16)))
        gdm_ready = Count(sem("gdm_ready"), dict(MQ=(4, 2)))
        dec_ready = Count(sem("dec_ready"), dict(MQ=(4, 8)))
        wts_ready = Count(sem("wts_ready"), dict(MQ=(4, 8)))
        h_ready = Count(sem("h_ready"), dict(MQ=(4, 2)))
        hc_ready = Count(sem("hc_ready"), dict(MQ=(4, 2)))
        hsq_ready = Count(sem("hsq_ready"), dict(MQ=(4, 2)))
        ml_y = Count(sem("ml_y"), dict(MQ=(4, 2)), 2)
        og_done = Count(sem("og_done"), dict(MO=(2, 4)))
        best_done = Count(sem("best_done"), dict(WQ=(4, 1)), 1)
        wsm_in = Count(sem("wsm_in"), dict(T=(TT, 1)))
        wsm_out = Count(sem("wsm_out"), dict(T=(TT, 1)))
        tanh_in = Count(sem("tanh_in"), dict(T=(TT, 1)))
        tanh_out = Count(sem("tanh_out"), dict(T=(TT, 1)))
        eidx_ready = Count(sem("eidx_ready"), dict(T=(TT, 1)))
        g_used = Count(sem("g_used"), dict(T=(TT, 2 * SLOTS)), GR)
        dve_step = Count(sem("dve_step"), dict(
            N1=(1, 5), P=(1, 17), G=(1, 18), LRU=(2, 21), FQ=(4, 16), MQ=(4, 8),
            N2=(1, 5), WQ=(4, 81)))
        choose_step = Count(sem("choose_step"), dict(T=(TT, 55)))
        gelu_step = Count(sem("gelu_step"), dict(T=(TT, 4)))
        dve_total = dve_step.total

        def stand(eng):
            eng.sem_inc(waits_taken, 1)

        def rnd(L, phase, i):
            return L * NROUND + i + ROUND0[phase]

        block = ctx.enter_context(nc.Block())

        @block.sync
        def _(sp):
            sp.dma_start(x[:, :, :], x_in.rearrange("(t p) d -> p t d", p=P)).then_inc(x_loaded, 16)
            for s in range(4):
                sp.dma_start(ring[s][:, :], w_stream[s]).then_inc(w_ready[s], 16)
            with sp.Fori(1, DEPTH * NROUND) as r:
                for s in range(4):
                    sp.wait_ge(proj_done, 4 * r + (s - 3))
                    sp.dma_start(ring[s][:, :], w_stream[4 * r + s]).then_inc(w_ready[s], 16)
            sp.wait_ge(layer_done.sem, DEPTH + 1)
            sp.dma_start(nwb[:, 0, :], fnorm.partition_broadcast(P)).then_inc(fnw_loaded, 16)
            sp.wait_ge(out_ready, 4)
            sp.dma_start(out.rearrange("(t p) d -> p t d", p=P), hn[:, :, :]).then_inc(out_done, 16)
            sp.wait_ge(out_done, 16)

        @block.gpsimd
        def _(pool):
            nc.gpsimd.memset(ident[:, :], 0.0).then_inc(pool_step, 1)
            nc.gpsimd.memset(mask_q[:, :], 0.0).then_inc(pool_step, 1)
            nc.gpsimd.memset(mask_k[:, :], 0.0).then_inc(pool_step, 1)
            nc.gpsimd.memset(ones[:, :], 1.0).then_inc(pool_step, 1)
            nc.gpsimd.memset(inv[:, :], 1.0 / P).then_inc(pool_step, 1)
            nc.gpsimd.memset(eps_t[:, :], EPS).then_inc(pool_step, 1)
            nc.gpsimd.iota(iota_i[:, :], pattern=[[1, TOPK]], base=0, channel_multiplier=0).then_inc(pool_step, 1)
            pool.wait_ge(pool_step, 7)
            nc.gpsimd.affine_select(out=ident[:, :], in_=ident[:, :], compare_op=ALU.not_equal, fill=1.0,
                                    base=0, pattern=[[-1, P]], channel_multiplier=1).then_inc(consts_ready, 1)
            nc.gpsimd.affine_select(out=mask_q[:, :], in_=mask_q[:, :], compare_op=ALU.is_ge, fill=NEG,
                                    base=0, pattern=[[-1, P]], channel_multiplier=1).then_inc(consts_ready, 1)
            nc.gpsimd.affine_select(out=mask_k[:, :], in_=mask_k[:, :], compare_op=ALU.is_ge, fill=-NEG,
                                    base=0, pattern=[[1, P]], channel_multiplier=-1).then_inc(consts_ready, 1)
            nc.gpsimd.tensor_copy(iota_f[:, :], iota_i[:, :]).then_inc(consts_ready, 1)
            pool.wait_ge(consts_ready, 4)

            def gathers(table, L, t, base):
                stand(pool)
                with pool.Fori(0, SLOTS // (2 * GR)) as j:
                    for half in range(2):
                        nc.gpsimd.tensor_copy(estage[half][:, :], eidx[:, t, ds(2 * GR * j + GR * half, GR)])\
                            .then_inc(pool_stage, 1)
                        pool.wait_ge(pool_stage, stage_at(L, t, base, j, half))
                        for q in range(GR):
                            n = base + GR * half + q
                            pool.wait_ge(g_used.sem, g_used.at(L, "T", t, n) + 2 * GR * j + (1 - GR))
                            stand(pool)
                            nc.gpsimd.indirect_dma_start(
                                out=gring[:, q, :], out_offset=None, in_=table,
                                in_offset=bass.IndirectOffsetOnAxis(ap=estage[half][:, q:q + 1], axis=0))\
                                .then_inc(g_ready[q], 16)

            def stage_at(L, t, base, j, half):
                per = 2 * SLOTS // GR
                return (L * TT + t) * per + base // GR + 2 * j + (half + 1)

            with pool.Fori(0, DEPTH) as L:
                with pool.Fori(0, 4) as i:
                    pool.wait_ge(filled[7].sem, filled[7].at(L, "FQ", i, 0))
                    nc.gpsimd.tensor_copy(sel[:, :, :], ident[0:NROW, ds(4 * i + ML_H, 4)]
                                          .unsqueeze(2).to_broadcast([NROW, 4, P])).then_inc(sel_ready.sem, 1)
                with pool.Fori(0, 4) as i:
                    pool.wait_ge(filled[7].sem, filled[7].at(L, "MQ", i, 0))
                    pool.wait_ge(filled[6].sem, filled[6].at(L, "MQ", i, 0))
                    nc.gpsimd.tensor_copy(sel[:, 0:2, :], ident[0:NROW, ds(2 * i, 2)]
                                          .unsqueeze(2).to_broadcast([NROW, 2, P])).then_inc(sel_ready.sem, 1)
                    for s in range(4):
                        pool.wait_ge(drained[s].sem, drained[s].at(L, "MV", 1, 1))
                    nc.gpsimd.tensor_copy(vst[:, :, :, :].rearrange("p t a n -> p t (a n)"),
                                          v_sb[:, :, ds(2 * P * i, 2 * P)]).then_inc(vst_ready.sem, 1)
                with pool.Fori(0, TT) as t:
                    pool.wait_ge(eidx_ready.sem, eidx_ready.at(L, "T", t, 1))
                    gathers(u_tab, L, t, 0)
                    gathers(v_tab, L, t, SLOTS)

        @block.tensor
        def _(pe):
            for b in range(8):
                pe.sem_inc(drained_sem[b], 1)
            pe.wait_ge(consts_ready, 4)

            def fill_wait(b, L, ph, i, n):
                pe.wait_ge(drained[b].sem, drained[b].at(L, ph, i, n))

            def transpose_norm(L, ph):
                for c in range(KC):
                    b = 4 + c % 4
                    fill_wait(b, L, ph, 0, c // 4)
                    for t in range(TT):
                        if c == 0:
                            pe.wait_ge(hn_ready.sem, hn_ready.at(L, ph, 0, t + 1))
                        mm = nc.tensor.transpose(bank[b][:, t * P:(t + 1) * P], hn[:, t, c * P:(c + 1) * P], ident[:, :])
                    mm.then_inc(filled[b].sem, 1)
                for b in range(4, 8):
                    pe.wait_ge(drained[b].sem, drained[b].at(L, ph, 0, 2))
                stand(pe)

            def project(L, ph, i, s, src):
                r = rnd(L, ph, i)
                pe.wait_ge(w_ready[s], 16 * r + 16)
                pe.wait_ge(drained_sem[s], r + 1)
                for k in range(KC):
                    mm = nc.tensor.matmul(bank[s][:, :], ring[s][:, k * P:(k + 1) * P], src[:, k, :],
                                          start=(k == 0), stop=(k == KC - 1))
                mm.then_inc(proj_done, 1)

            def project_tokens(L, ph, i, src):
                r = rnd(L, ph, i)
                for s in range(4):
                    pe.wait_ge(w_ready[s], 16 * r + 16)
                    for t in range(TT):
                        if s == 0:
                            pe.wait_ge(drained_sem[t], r + 1)
                        for kk in range(2):
                            k = 2 * s + kk
                            mm = nc.tensor.matmul(bank[t][:, :], src[:, k, t * P:(t + 1) * P],
                                                  ring[s][:, kk * SEQ:(kk + 1) * SEQ],
                                                  start=(k == 0), stop=(k == KC - 1))
                    mm.then_inc(proj_done, 1)

            def merge(L, ph):
                stand(pe)
                with pe.Fori(0, 4) as i:
                    for s in range(4):
                        project(L, ph, i, s, yT if s % 2 == 0 else xT)

            with pe.Fori(0, DEPTH) as L:
                transpose_norm(L, "N1")
                pe.wait_ge(params_ready, 48 * L + 48)
                for b, c0, c1 in ((4, 0, NROW), (5, NROW, 32)):
                    fill_wait(b, L, "G", 0, 0)
                    for k in range(KC):
                        mm = nc.tensor.matmul(bank[b][0:c1 - c0, :], wgate[:, k, c0:c1], xT[:, k, :],
                                              start=(k == 0), stop=(k == KC - 1))
                    mm.then_inc(filled[b].sem, 1)
                with pe.Fori(0, 2) as i:
                    for s in range(4):
                        project(L, "LRU", i, s, xT)
                    pe.wait_ge(lruw_ready, 32 * L + 16 * i + 16)
                    for s in range(4):
                        pe.wait_ge(conv_done.sem, conv_done.at(L, "LRU", i, s + 1))
                        for g in range(2):
                            b = 4 + 2 * (s % 2) + g
                            fill_wait(b, L, "LRU", i, s // 2)
                            nc.tensor.matmul(bank[b][:, :], lruw[:, s, g, :], xc[:, s, :], start=True, stop=True)\
                                .then_inc(filled[b].sem, 1)
                pe.wait_ge(rows_ready.sem, rows_ready.at(L, "G", 0, 1))
                fill_wait(6, L, "COLS", 0, 0)
                stand(pe)
                for t in range(TT):
                    mm = nc.tensor.transpose(bank[6][:, t * NROW:(t + 1) * NROW], cum[:, t * P:(t + 1) * P],
                                             ident[0:NROW, 0:NROW])
                mm.then_inc(filled[6].sem, 1)
                fill_wait(7, L, "COLS", 0, 0)
                stand(pe)
                for t in range(TT):
                    mm = nc.tensor.transpose(bank[7][:, t * ML_H:(t + 1) * ML_H], g_row[:, t * P:(t + 1) * P],
                                             ident[0:ML_H, 0:ML_H])
                mm.then_inc(filled[7].sem, 1)
                with pe.Fori(0, 2) as i:
                    project_tokens(L, "FV", i, xT)
                pe.wait_ge(lru_done.sem, lru_done.at(L, "LRU", 1, 1))
                merge(L, "MA")
                with pe.Fori(0, 4) as i:
                    for s in range(4):
                        project(L, "FQ", i, s, xT)
                    pe.wait_ge(sel_ready.sem, sel_ready.at(L, "FQ", i, 1))
                    n6 = n7 = 0
                    for kind, u in fox_steps():
                        t, h = u % 4, u // 4
                        b = 4 + u % 2
                        if kind == "C":
                            fill_wait(7, L, "FQ", i, n7)
                            nc.tensor.matmul(bank[7][:, :], sel[:, u, :], cum[:, :], start=True, stop=True)\
                                .then_inc(filled[7].sem, 1)
                            n7 += 1
                        elif kind == "S":
                            pp, hp = h // 2, h % 2
                            if u == 0:
                                for s in range(4):
                                    pe.wait_ge(drained_sem[s], rnd(L, "FQ", i) + 2)
                            fill_wait(b, L, "FQ", i, u // 2)
                            rowsel = slice(FOX_D * hp, FOX_D * hp + FOX_D)
                            nc.tensor.matmul(bank[b][:, 0:(t + 1) * P], qk[rowsel, 2 * pp, t * P:(t + 1) * P],
                                             qk[rowsel, 2 * pp + 1, 0:(t + 1) * P], start=True, stop=True)\
                                .then_inc(filled[b].sem, 1)
                        elif kind == "T":
                            pe.wait_ge(prob_ready.sem, prob_ready.at(L, "FQ", i, u + 1))
                            fill_wait(6, L, "FQ", i, n6)
                            for kb in range(t + 1):
                                mm = nc.tensor.transpose(bank[6][:, kb * P:(kb + 1) * P],
                                                         pr[:, u % 2, kb * P:(kb + 1) * P], ident[:, :])
                            mm.then_inc(filled[6].sem, 1)
                            n6 += 1
                        elif kind == "V":
                            pe.wait_ge(drained_sem[6], drained[6].at(L, "FQ", i, u + 1))
                            fill_wait(7, L, "FQ", i, n7)
                            for kb in range(t + 1):
                                mm = nc.tensor.matmul(bank[7][:, 0:FOX_D], pT[:, u % 2, kb * P:(kb + 1) * P],
                                                      v_sb[:, kb, ds(4 * FOX_D * i + FOX_D * h, FOX_D)],
                                                      start=(kb == 0), stop=(kb == t))
                            mm.then_inc(filled[7].sem, 1)
                            n7 += 1
                        else:
                            fill_wait(7, L, "FQ", i, n7)
                            for tt in range(TT):
                                mm = nc.tensor.transpose(bank[7][:, tt * P:(tt + 1) * P], ytok[:, tt, :], ident[:, :])
                            mm.then_inc(filled[7].sem, 1)
                            n7 += 1
                with pe.Fori(0, 2) as i:
                    for s in range(4):
                        project(L, "MO", i, s, xT)
                pe.wait_ge(drained_sem[7], drained[7].at(L, "FQ", 3, 22))
                merge(L, "MB")
                with pe.Fori(0, 2) as i:
                    project_tokens(L, "MV", i, xT)
                with pe.Fori(0, 4) as i:
                    for s in range(4):
                        project(L, "MQ", i, s, xT)
                    pe.wait_ge(sel_ready.sem, sel_ready.at(L, "MQ", i, 1))
                    n = {6: 0, 7: 0}

                    def spread(b, p, row):
                        fill_wait(b, L, "MQ", i, n[b])
                        nc.tensor.matmul(bank[b][:, :], sel[0:ML_H, p, :], row[:, :], start=True, stop=True)\
                            .then_inc(filled[b].sem, 1)
                        n[b] += 1

                    def scores_of(p):
                        for s in range(TT):
                            b = 4 + s % 2
                            fill_wait(b, L, "MQ", i, 2 * p + s // 2)
                            nc.tensor.matmul(bank[b][:, 0:SEQ - s * P], qk[:, 2 * p + 1, s * P:(s + 1) * P],
                                             qk[:, 2 * p, s * P:SEQ], start=True, stop=True)\
                                .then_inc(filled[b].sem, 1)

                    def num_den(p):
                        for b in (6, 7):
                            fill_wait(b, L, "MQ", i, n[b])
                            for s in range(TT):
                                if b == 6:
                                    pe.wait_ge(wts_ready.sem, wts_ready.at(L, "MQ", i, 4 * p + s + 1))
                                lhsT = vst[:, s, p, :] if b == 6 else ones[:, 0:P]
                                mm = nc.tensor.matmul(bank[b][:, s * P:SEQ], lhsT, E[:, p, s, 0:SEQ - s * P],
                                                      start=(s == 0), stop=(s == TT - 1))
                            mm.then_inc(filled[b].sem, 1)
                            n[b] += 1

                    def mean(p, b, src, ready):
                        pe.wait_ge(ready.sem, ready.at(L, "MQ", i, p + 1))
                        fill_wait(b, L, "MQ", i, n[b])
                        nc.tensor.matmul(bank[b][:, :], inv[:, :], src[:, p, :], start=True, stop=True)\
                            .then_inc(filled[b].sem, 1)
                        n[b] += 1

                    for s in range(4):
                        pe.wait_ge(drained_sem[s], rnd(L, "MQ", i) + 2)
                    pe.wait_ge(vst_ready.sem, vst_ready.at(L, "MQ", i, 1))
                    spread(6, 0, G_row)
                    spread(7, 0, m_row)
                    scores_of(0)
                    num_den(0)
                    spread(6, 1, G_row)
                    spread(7, 1, m_row)
                    scores_of(1)
                    mean(0, 6, hh, h_ready)
                    num_den(1)
                    mean(0, 7, sq, hsq_ready)
                    mean(1, 6, hh, h_ready)
                    mean(1, 7, sq, hsq_ready)
                pe.wait_ge(ml_y.sem, ml_y.at(L, "MQ", 3, 2))
                merge(L, "MC")
                pe.wait_ge(merged_ready.sem, merged_ready.at(L, "MC", 3, 2))
                stand(pe)
                with pe.Fori(0, 2) as i:
                    project_tokens(L, "OUT", i, merged)
                transpose_norm(L, "N2")
                with pe.Fori(0, 4) as i:
                    for s in range(4):
                        project(L, "WQ", i, s, xT)
                    for s in range(4):
                        pe.wait_ge(drained_sem[s], rnd(L, "WQ", i) + 2)
                        fill_wait(4 + s, L, "WQ", i, 0)
                        for t in range(TT):
                            mm = nc.tensor.matmul(bank[4 + s][:, t * P:(t + 1) * P], qk[:, s, t * P:(t + 1) * P],
                                                  subk[:, s % 2, :], start=True, stop=True)
                        mm.then_inc(filled[4 + s].sem, 1)

        @block.scalar
        def _(act):
            act.sem_inc(prob_ready.sem, 2)

            def evac_norm(L, ph):
                act.wait_ge(ms_ready.sem, ms_ready.at(L, ph, 0, 1))
                nc.scalar.activation(stat[:, 2, :], stat[:, 1, :], ACT.Sqrt).then_inc(sd_ready.sem, 1)
                for c in range(KC):
                    b = 4 + c % 4
                    act.wait_ge(filled[b].sem, filled[b].at(L, ph, 0, c // 4 + 1))
                    nc.scalar.copy(xT[:, c, :], bank[b][:, :]).then_inc(drained_sem[b], 1)

            def proj_wait(L, ph, i, s):
                act.wait_ge(proj_done, 4 * rnd(L, ph, i) + (s + 1))

            def values(L, ph):
                with act.Fori(0, 2) as i:
                    proj_wait(L, ph, i, 3)
                    for t in range(TT):
                        nc.scalar.copy(v_sb[:, t, ds(SEQ * i, SEQ)], bank[t][:, :]).then_inc(drained_sem[t], 1)

            def merge_gates(L, ph, branch):
                with act.Fori(0, 4) as i:
                    for j in range(2):
                        proj_wait(L, ph, i, 2 * j + 1)
                        nc.scalar.activation(gt[j], bank[2 * j + 1][:, :], ACT.Tanh, scale=0.5,
                                             bias=dcol(hb, 2 * i + (2 * KC + branch * KC + j)))\
                            .then_inc(drained_sem[2 * j + 1], 1)

            with act.Fori(0, DEPTH) as L:
                act.wait_ge(layer_done.sem, layer_done.at(L, "L", 0, 0))
                act.dma_start(pv[:, :], pvec[L]).then_inc(params_ready, 16)
                for a in range(2):
                    act.dma_start(nwb[:, a, :], nrows[2 * L + a].partition_broadcast(P)).then_inc(params_ready, 16)
                act.dma_start(lruw[:, :, :, :], w_lru[2 * L].rearrange("p (s g n) -> p s g n", s=4, g=2))\
                    .then_inc(lruw_ready, 16)
                evac_norm(L, "N1")
                for ph in ("P", "G"):
                    act.wait_ge(zexp_in.sem, zexp_in.at(L, ph, 0, 1))
                    tile = lp[:, 0, :] if ph == "P" else rows[:, 1, :]
                    nc.scalar.activation(tile, tile, ACT.Exp).then_inc(zexp_out.sem, 1)
                for i in range(2):
                    for s in range(4):
                        proj_wait(L, "LRU", i, s)
                        if s == 0:
                            act.wait_ge(lru_done.sem, lru_done.at(L, "LRU", i, 0))
                        nc.scalar.copy(xpad[:, s, CONV - 1:], bank[s][:, :]).then_inc(drained_sem[s], 1)
                    for s in range(4):
                        for g in range(2):
                            b = 4 + 2 * (s % 2) + g
                            act.wait_ge(filled[b].sem, filled[b].at(L, "LRU", i, s // 2 + 1))
                            nc.scalar.activation((TI if g else R)[:, s, :], bank[b][:, :], ACT.Tanh, scale=0.5,
                                                 bias=hb[:, g * KC + 4 * i + s:g * KC + 4 * i + s + 1])\
                                .then_inc(drained_sem[b], 1)
                    if i == 0:
                        act.dma_start(lruw[:, :, :, :], w_lru[2 * L + 1].rearrange("p (s g n) -> p s g n", s=4, g=2))\
                            .then_inc(lruw_ready, 16)
                    act.wait_ge(la_ready.sem, la_ready.at(L, "LRU", i, 1))
                    nc.scalar.activation(TH[:, :, :], R, ACT.Tanh).then_inc(ea_ready.sem, 1)
                    nc.scalar.activation(A, R, ACT.Exp).then_inc(ea_ready.sem, 1)
                    act.wait_ge(q_ready.sem, q_ready.at(L, "LRU", i, 1))
                    nc.scalar.activation(TH[:, :, :], TH[:, :, :], ACT.Sqrt, scale=-0.25).then_inc(sq_ready.sem, 1)
                act.wait_ge(filled[6].sem, filled[6].at(L, "COLS", 0, 1))
                nc.scalar.copy(cumc[:, :, :], bank[6][:, 0:TT * NROW].rearrange("p (t n) -> p t n", t=TT))\
                    .then_inc(drained_sem[6], 1)
                act.wait_ge(filled[7].sem, filled[7].at(L, "COLS", 0, 1))
                nc.scalar.copy(gcol[:, :, :], bank[7][:, 0:TT * ML_H].rearrange("p (t n) -> p t n", t=TT))\
                    .then_inc(drained_sem[7], 1)
                values(L, "FV")
                merge_gates(L, "MA", 0)
                with act.Fori(0, 4) as i:
                    for s in range(4):
                        proj_wait(L, "FQ", i, s)
                        nc.scalar.activation(qk[:, s, :], bank[s][:, :], ACT.Copy,
                                             scale=FOX_D ** -0.5 if s % 2 == 0 else 1.0)\
                            .then_inc(drained_sem[s], 1)
                    n7 = 0
                    todo = []
                    for kind, u in fox_steps():
                        t, h = u % 4, u // 4
                        n = (t + 1) * P
                        if kind == "S":
                            todo.append(u)
                        if kind == "C":
                            act.wait_ge(filled[7].sem, filled[7].at(L, "FQ", i, n7 + 1))
                            nc.scalar.copy(cb[:, u % 2, :], bank[7][:, :]).then_inc(drained_sem[7], 1)
                            n7 += 1
                        if kind == "T":
                            act.wait_ge(filled[6].sem, filled[6].at(L, "FQ", i, u + 1))
                            nc.scalar.copy(pT[:, u % 2, 0:n], bank[6][:, 0:n]).then_inc(drained_sem[6], 1)
                        if kind == "V":
                            act.wait_ge(filled[7].sem, filled[7].at(L, "FQ", i, n7 + 1))
                            act.wait_ge(rinv_ready.sem, rinv_ready.at(L, "FQ", i, u + 1))
                            nc.scalar.activation(ytok[:, t, FOX_D * (h % 2):FOX_D * (h % 2) + FOX_D],
                                                 bank[7][:, 0:FOX_D], ACT.Copy, scale=rinv[:, u:u + 1])\
                                .then_inc(drained_sem[7], 1)
                            n7 += 1
                        if kind == "Y":
                            act.wait_ge(filled[7].sem, filled[7].at(L, "FQ", i, n7 + 1))
                            nc.scalar.copy(yT[:, 2 * i + u, :], bank[7][:, :]).then_inc(drained_sem[7], 1)
                            n7 += 1
                        if todo and (kind == "V" or (kind == "T" and u == 0) or (kind == "S" and u < 2)):
                            e = todo.pop(0)
                            ne = (e % 4 + 1) * P
                            act.wait_ge(srow_ready.sem, srow_ready.at(L, "FQ", i, e + 1))
                            nc.scalar.activation(pr[:, e % 2, 0:ne], sc[:, e % 2, 0:ne], ACT.Exp,
                                                 bias=nmax[:, e:e + 1], accum_out=rsum[:, e:e + 1])\
                                .then_inc(prob_ready.sem, 1)
                    assert not todo
                with act.Fori(0, 2) as i:
                    for s in range(4):
                        proj_wait(L, "MO", i, s)
                        nc.scalar.activation(og[:, 4 * i + s, :], bank[s][:, :], ACT.Tanh, scale=0.5)\
                            .then_inc(drained_sem[s], 1)
                merge_gates(L, "MB", 1)
                values(L, "MV")
                with act.Fori(0, 4) as i:
                    for s in range(4):
                        proj_wait(L, "MQ", i, s)
                        nc.scalar.activation(qk[:, s, :], bank[s][:, :], ACT.Copy,
                                             scale=ML_D ** -0.5 if s % 2 == 1 else 1.0)\
                            .then_inc(drained_sem[s], 1)
                    for p in range(2):
                        n = 2 * p
                        act.wait_ge(filled[6].sem, filled[6].at(L, "MQ", i, n + 1))
                        nc.scalar.copy(gb, bank[6][:, :]).then_inc(drained_sem[6], 1)
                        act.wait_ge(filled[7].sem, filled[7].at(L, "MQ", i, n + 1))
                        act.wait_ge(ml_y.sem, ml_y.at(L, "MQ", i, p) - 1)
                        nc.scalar.activation(em[:, p, :], bank[7][:, :], ACT.Exp, scale=-1.0)\
                            .then_inc(drained_sem[7], 1)
                        act.wait_ge(drained_sem[6], drained[6].at(L, "MQ", i, n + 1))
                        act.wait_ge(gdm_ready.sem, gdm_ready.at(L, "MQ", i, p + 1))
                        for s in range(TT):
                            gs = gcol[:, s, ds(2 * i + p, 1)]
                            if s < TT - 1:
                                nc.scalar.activation(E[:, p, s, P:SEQ - s * P], gb[:, (s + 1) * P:], ACT.Exp,
                                                     scale=-1.0, bias=gs)
                            nc.scalar.activation(E[:, p, s, 0:P], gdm[:, s, :], ACT.Exp, scale=-1.0, bias=gs)\
                                .then_inc(dec_ready.sem, 1)
                    for p in range(2):
                        act.wait_ge(hc_ready.sem, hc_ready.at(L, "MQ", i, p + 1))
                        nc.scalar.activation(sq[:, p, :], hh[:, p, :], ACT.Square).then_inc(hsq_ready.sem, 1)
                        act.wait_ge(filled[7].sem, filled[7].at(L, "MQ", i, 5 + p))
                        nc.scalar.activation(em[:, p, :], bank[7][:, :], ACT.Sqrt, bias=eps_t[:, :])\
                            .then_inc(drained_sem[7], 1)
                merge_gates(L, "MC", 2)
                evac_norm(L, "N2")
                with act.Fori(0, 4) as i:
                    for s in range(4):
                        proj_wait(L, "WQ", i, s)
                        nc.scalar.copy(qk[:, s, :], bank[s][:, :]).then_inc(drained_sem[s], 1)
                    for s in range(4):
                        act.wait_ge(filled[4 + s].sem, filled[4 + s].at(L, "WQ", i, 1))
                        if s == 0:
                            act.wait_ge(best_done.sem, best_done.at(L, "WQ", i, 0))
                        nc.scalar.copy(keys[:, 4 * s:4 * s + 4, :], bank[4 + s][:, :].rearrange("p (t n) -> p t n", t=TT))\
                            .then_inc(drained_sem[4 + s], 1)

                def soft(L, t):
                    act.wait_ge(wsm_in.sem, wsm_in.at(L, "T", t, 1))
                    nc.scalar.activation(wts, wts, ACT.Exp).then_inc(wsm_out.sem, 1)

                def gelu_tanh(L, t):
                    act.wait_ge(tanh_in.sem, tanh_in.at(L, "T", t, 1))
                    nc.scalar.activation(th, gin, ACT.Tanh).then_inc(tanh_out.sem, 1)

                soft(L, 0)
                with act.Fori(0, TT - 1) as t:
                    gelu_tanh(L, t)
                    soft(L, t + 1)
                gelu_tanh(L, TT - 1)
            act.wait_ge(ms_final, 1)
            nc.scalar.activation(stat[:, 2, :], stat[:, 1, :], ACT.Sqrt).then_inc(sd_final, 1)

        @block.vector
        def _(dve):
            V = nc.vector
            for c in (layer_done, lru_done, ml_y, g_used, merged_ready, best_done):
                dve.sem_inc(c.sem, c.credit)
            V.memset(first_expert[:, :], 0.0).then_inc(final_step, 1)
            dve.wait_ge(final_step, 1)
            dve.wait_ge(x_loaded, 16)

            def stats(c):
                for t in range(TT):
                    c.step(V.scalar_tensor_tensor(out=hn[:, t, :], in0=x[:, t, :], scalar=1.0, in1=x[:, t, :],
                                                  op0=ALU.mult, op1=ALU.mult, accum_out=stat[:, 0, t:t + 1]))
                c.wait()
                return V.tensor_scalar(stat[:, 1, :], stat[:, 0, :], 1.0 / D, EPS, ALU.mult, ALU.add)

            def scale_rows(t, w):
                return V.scalar_tensor_tensor(out=hn[:, t, :], in0=x[:, t, :], scalar=stat[:, 3, t:t + 1], in1=w,
                                              op0=ALU.mult, op1=ALU.mult)

            def norm(L, ph, a):
                c = Chain(dve, dve_step, L, ph, 0)
                stats(c).then_inc(ms_ready.sem, 1)
                dve.wait_ge(sd_ready.sem, sd_ready.at(L, ph, 0, 1))
                c.step(V.reciprocal(stat[:, 3, :], stat[:, 2, :]))
                c.wait()
                if a == 0:
                    dve.wait_ge(params_ready, 48 * L + 48)
                for t in range(TT):
                    scale_rows(t, nwb[:, a, :]).then_inc(hn_ready.sem, 1)
                c.close()

            def log1p(c, z, s, q, r):
                c.step(V.tensor_scalar(s, z, 2.0, None, ALU.add))
                c.wait()
                c.step(V.reciprocal(q, s))
                c.wait()
                c.step(V.tensor_tensor(s, z, q, ALU.mult))
                c.wait()
                c.step(V.tensor_tensor(q, s, s, ALU.mult))
                c.wait()
                c.step(V.tensor_scalar(r, q, 1.0 / 15, None, ALU.mult))
                c.wait()
                for k in (13, 11, 9, 7, 5, 3):
                    c.step(V.scalar_tensor_tensor(out=r, in0=r, scalar=1.0 / k, in1=q, op0=ALU.add, op1=ALU.mult))
                    c.wait()
                c.step(V.scalar_tensor_tensor(out=r, in0=r, scalar=1.0, in1=s, op0=ALU.add, op1=ALU.mult))
                c.wait()

            def merge(L, ph):
                with dve.Fori(0, 4) as i:
                    for j in range(2):
                        dve.wait_ge(proj_done, 4 * rnd(L, ph, i) + (2 * j + 1))
                        dve.wait_ge(drained_sem[2 * j + 1], rnd(L, ph, i) + 2)
                        dst = merged[:, 2 * i + j, :]
                        to = dst if ph == "MA" else mtmp
                        if ph != "MA":
                            dve.wait_ge(merged_ready.sem, merged_ready.at(L, ph, i, j))
                        V.scalar_tensor_tensor(out=to, in0=gt[j], scalar=1.0, in1=bank[2 * j][:, :],
                                               op0=ALU.add, op1=ALU.mult).then_inc(drained_sem[2 * j], 1)
                        if ph != "MA":
                            dve.wait_ge(drained_sem[2 * j], rnd(L, ph, i) + 2)
                            V.tensor_tensor(dst, dst, mtmp, ALU.add).then_inc(merged_ready.sem, 1)

            with dve.Fori(0, DEPTH) as L:
                norm(L, "N1", 0)
                c = Chain(dve, dve_step, L, "P", 0)
                lam = pcol("lam", 0, KC)
                c.step(V.tensor_scalar(hb[:, :], pcol("ba", 0, 5 * KC), 0.5, None, ALU.mult))
                c.step(V.tensor_scalar(hnw[:, :], pcol("nw", 0, KC), 0.5, None, ALU.mult))
                c.step(V.tensor_scalar(nsp[:, :], lam, -1.0, None, ALU.mult))
                c.wait()
                V.tensor_tensor(lp[:, 0, :], lam, nsp[:, :], ALU.min).then_inc(zexp_in.sem, 1)
                dve.wait_ge(zexp_out.sem, zexp_out.at(L, "P", 0, 1))
                log1p(c, lp[:, 0, :], lp[:, 1, :], lp[:, 2, :], lp[:, 0, :])
                c.step(V.tensor_scalar(nsp[:, :], nsp[:, :], 0.0, -4.0, ALU.max, ALU.mult))
                c.wait()
                c.step(V.scalar_tensor_tensor(out=nsp[:, :], in0=lp[:, 0, :], scalar=-8.0, in1=nsp[:, :],
                                              op0=ALU.mult, op1=ALU.add))
                c.close()
                c = Chain(dve, dve_step, L, "G", 0)
                dve.wait_ge(filled[4].sem, filled[4].at(L, "G", 0, 1))
                V.tensor_scalar(rows[:, 0, :], bank[4][0:NROW, :], pcol("fbias", 0)[0:NROW, :], None, ALU.add)\
                    .then_inc(drained_sem[4], 1)
                dve.wait_ge(filled[5].sem, filled[5].at(L, "G", 0, 1))
                V.tensor_scalar(rows[0:ML_H, 5, :], bank[5][0:ML_H, :], pcol("ibias", 0)[0:ML_H, :], None, ALU.add)\
                    .then_inc(drained_sem[5], 1)
                dve.wait_ge(drained_sem[4], drained[4].at(L, "G", 0, 1))
                c.step(V.tensor_scalar(rows[:, 1, :], rows[:, 0, :], -1.0, None, ALU.mult))
                c.wait()
                V.tensor_tensor(rows[:, 1, :], rows[:, 1, :], rows[:, 0, :], ALU.min).then_inc(zexp_in.sem, 1)
                dve.wait_ge(zexp_out.sem, zexp_out.at(L, "G", 0, 1))
                log1p(c, rows[:, 1, :], rows[:, 2, :], rows[:, 3, :], rows[:, 4, :])
                c.step(V.tensor_scalar(rows[:, 0, :], rows[:, 0, :], 0.0, None, ALU.min))
                c.wait()
                c.step(V.scalar_tensor_tensor(out=rows[:, 0, :], in0=rows[:, 4, :], scalar=-2.0, in1=rows[:, 0, :],
                                              op0=ALU.mult, op1=ALU.add))
                c.wait()
                c.step(V.tensor_tensor_scan(cum[:, :], ones[0:NROW, :], rows[:, 0, :], 0.0, ALU.mult, ALU.add))
                c.wait()
                dve.wait_ge(drained_sem[5], drained[5].at(L, "G", 0, 1))
                c.step(V.tensor_tensor(g_row[:, :], rows[0:ML_H, 5, :], cum[0:ML_H, :], ALU.subtract))
                c.wait()
                c.step(V.tensor_tensor_scan(G_row[:, :], g_row[:, :], g_row[:, :], 0.0, ALU.max, ALU.max))
                c.wait()
                V.tensor_tensor(m_row[:, :], G_row[:, :], cum[0:ML_H, :], ALU.add).then_inc(rows_ready.sem, 1)
                c.close()
                for b in range(4, 8):
                    dve.wait_ge(drained_sem[b], drained[b].at(L, "N1", 0, 2))
                V.memset(xpad[:, :, 0:CONV - 1], 0.0).then_inc(pad_ready, 1)
                dve.wait_ge(pad_ready, L + 1)
                stand(dve)
                with dve.Fori(0, 2) as i:
                    c = Chain(dve, dve_step, L, "LRU", i)
                    for k in range(CONV):
                        for s in range(4):
                            if k == 0:
                                dve.wait_ge(drained_sem[s], rnd(L, "LRU", i) + 2)
                            w = dcol(pv, 4 * i + (PV_COLS["conv_w"][0] + k * KC + s))
                            src = xpad[:, s, k:k + SEQ]
                            if k == 0:
                                c.step(V.tensor_scalar(xc[:, s, :], src, w, dcol(pv, 4 * i + (PV_COLS["conv_b"][0] + s)),
                                                       ALU.mult, ALU.add))
                            else:
                                ins = V.scalar_tensor_tensor(out=xc[:, s, :], in0=src, scalar=w, in1=xc[:, s, :],
                                                             op0=ALU.mult, op1=ALU.add)
                                if k == CONV - 1:
                                    ins.then_inc(conv_done.sem, 1)
                                else:
                                    c.step(ins)
                        if k < CONV - 1:
                            c.wait()
                    for s in range(4):
                        b = 4 + 2 * (s % 2)
                        dve.wait_ge(drained_sem[b], drained[b].at(L, "LRU", i, s // 2 + 1))
                        ins = V.tensor_scalar(R[:, s, :], R[:, s, :], 1.0, dcol(nsp, 4 * i + s), ALU.add, ALU.mult)
                        if s < 3:
                            c.step(ins)
                        else:
                            ins.then_inc(la_ready.sem, 1)
                    dve.wait_ge(drained_sem[5], drained[5].at(L, "LRU", i, 2))
                    dve.wait_ge(drained_sem[7], drained[7].at(L, "LRU", i, 2))
                    dve.wait_ge(conv_done.sem, conv_done.at(L, "LRU", i, 4))
                    c.step(V.scalar_tensor_tensor(out=TI, in0=TI, scalar=1.0, in1=xc, op0=ALU.add, op1=ALU.mult))
                    dve.wait_ge(ea_ready.sem, ea_ready.at(L, "LRU", i, 2))
                    c.step(V.tensor_tensor(R, A, A, ALU.mult))
                    c.wait()
                    V.scalar_tensor_tensor(out=TH[:, :, :], in0=R, scalar=1.0, in1=TH[:, :, :], op0=ALU.add, op1=ALU.mult)\
                        .then_inc(q_ready.sem, 1)
                    dve.wait_ge(sq_ready.sem, sq_ready.at(L, "LRU", i, 1))
                    c.step(V.tensor_tensor(TI, TI, TH[:, :, :], ALU.mult))
                    c.wait()
                    for s in range(4):
                        ins = V.tensor_tensor_scan(yT[:, 4 * i + s, :], A[:, s, :], TI[:, s, :], 0.0, ALU.mult, ALU.add)
                        if s < 3:
                            c.step(ins)
                        else:
                            ins.then_inc(lru_done.sem, 1)
                    c.close()
                merge(L, "MA")
                with dve.Fori(0, 4) as i:
                    c = Chain(dve, dve_step, L, "FQ", i)
                    cn = 0
                    n7 = {}
                    count = 0
                    for kind, u in fox_steps():
                        if kind in "CVY":
                            count += 1
                            n7[kind, u] = count
                    for u in range(17):
                        if u < 16:
                            t, h = u % 4, u // 4
                            b, n = 4 + u % 2, (u % 4 + 1) * P
                            if t == 0:
                                dve.wait_ge(drained_sem[7], drained[7].at(L, "FQ", i, n7["C", h]))
                                if u == 0:
                                    dve.wait_ge(drained_sem[6], drained[6].at(L, "COLS", 0, 1))
                            dve.wait_ge(filled[b].sem, filled[b].at(L, "FQ", i, u // 2 + 1))
                            dve.wait_ge(prob_ready.sem, prob_ready.at(L, "FQ", i, u) - 1)
                            V.scalar_tensor_tensor(out=sc[:, u % 2, 0:n], in0=bank[b][:, 0:n],
                                                   scalar=cumc[:, t, ds(4 * i + (ML_H + h), 1)],
                                                   in1=cb[:, h % 2, 0:n], op0=ALU.add, op1=ALU.subtract)\
                                .then_inc(drained_sem[b], 1)
                            dve.wait_ge(drained_sem[b], drained[b].at(L, "FQ", i, u // 2 + 1))
                            diag = sc[:, u % 2, n - P:n]
                            c.step(V.tensor_tensor(diag, diag, mask_q[:, :], ALU.add))
                            c.wait()
                            V.tensor_reduce(nmax[:, u:u + 1], sc[:, u % 2, 0:n], AX.X, ALU.max, negate=True)\
                                .then_inc(srow_ready.sem, 1)
                        if u >= 1:
                            dve.wait_ge(prob_ready.sem, prob_ready.at(L, "FQ", i, u))
                            V.reciprocal(rinv[:, u - 1:u], rsum[:, u - 1:u]).then_inc(rinv_ready.sem, 1)
                    c.close()
                stand(dve)
                with dve.Fori(0, 2) as i:
                    for s in range(4):
                        dve.wait_ge(drained_sem[s], rnd(L, "MO", i) + 2)
                        V.tensor_scalar(og[:, 4 * i + s, :], og[:, 4 * i + s, :], 1.0, dcol(hnw, 4 * i + s),
                                        ALU.add, ALU.mult).then_inc(og_done.sem, 1)
                merge(L, "MB")
                with dve.Fori(0, 4) as i:
                    c = Chain(dve, dve_step, L, "MQ", i)

                    def decay_mask(p):
                        dve.wait_ge(drained_sem[6], drained[6].at(L, "MQ", i, 2 * p + 1))
                        V.tensor_tensor(gdm, gb.rearrange("p (s n) -> p s n", s=4),
                                        mask_k[:, :].unsqueeze(1).to_broadcast([P, 4, P]), ALU.add)\
                            .then_inc(gdm_ready.sem, 1)

                    def weigh(p):
                        for s in range(TT):
                            b = 4 + s % 2
                            n = SEQ - s * P
                            dve.wait_ge(filled[b].sem, filled[b].at(L, "MQ", i, 2 * p + s // 2 + 1))
                            dve.wait_ge(dec_ready.sem, dec_ready.at(L, "MQ", i, 4 * p + s + 1))
                            V.tensor_tensor(E[:, p, s, 0:n], bank[b][:, 0:n], E[:, p, s, 0:n], ALU.mult)\
                                .then_inc(drained_sem[b], 1)
                            dve.wait_ge(drained_sem[b], drained[b].at(L, "MQ", i, 2 * p + s // 2 + 1))
                            dve.sem_inc(wts_ready.sem, 1)

                    def hidden(p):
                        n = 4 if p else 2
                        n6 = 5 if p else 2
                        n7 = 4 if p else 2
                        dve.wait_ge(drained_sem[7], drained[7].at(L, "MQ", i, 2 * p + 1))
                        dve.wait_ge(filled[7].sem, filled[7].at(L, "MQ", i, n7))
                        c.step(V.tensor_tensor(em[:, p, :], bank[7][:, :], em[:, p, :], ALU.max))
                        c.wait()
                        V.scalar_tensor_tensor(out=em[:, p, :], in0=bank[7][:, :], scalar=-1.0, in1=em[:, p, :],
                                               op0=ALU.mult, op1=ALU.max).then_inc(drained_sem[7], 1)
                        dve.wait_ge(drained_sem[7], drained[7].at(L, "MQ", i, n7))
                        c.step(V.reciprocal(em[:, p, :], em[:, p, :]))
                        c.wait()
                        dve.wait_ge(filled[6].sem, filled[6].at(L, "MQ", i, n6))
                        V.tensor_tensor(hh[:, p, :], bank[6][:, :], em[:, p, :], ALU.mult).then_inc(drained_sem[6], 1)
                        dve.wait_ge(drained_sem[6], drained[6].at(L, "MQ", i, n6))
                        dve.sem_inc(h_ready.sem, 1)

                    def centre(p):
                        n6 = 6 if p else 4
                        dve.wait_ge(filled[6].sem, filled[6].at(L, "MQ", i, n6))
                        V.tensor_tensor(hh[:, p, :], hh[:, p, :], bank[6][:, :], ALU.subtract)\
                            .then_inc(drained_sem[6], 1)
                        dve.wait_ge(drained_sem[6], drained[6].at(L, "MQ", i, n6))
                        dve.sem_inc(hc_ready.sem, 1)

                    decay_mask(0)
                    weigh(0)
                    hidden(0)
                    decay_mask(1)
                    weigh(1)
                    centre(0)
                    hidden(1)
                    centre(1)
                    for p in range(2):
                        dve.wait_ge(drained_sem[7], drained[7].at(L, "MQ", i, 5 + p))
                        c.step(V.reciprocal(em[:, p, :], em[:, p, :]))
                        c.wait()
                        c.step(V.tensor_tensor(hh[:, p, :], hh[:, p, :], em[:, p, :], ALU.mult))
                        c.wait()
                        V.tensor_tensor(yT[:, 2 * i + p, :], hh[:, p, :], og[:, 2 * i + p, :], ALU.mult)\
                            .then_inc(ml_y.sem, 1)
                    c.close()
                merge(L, "MC")
                with dve.Fori(0, 2) as i:
                    dve.wait_ge(proj_done, 4 * rnd(L, "OUT", i) + 4)
                    for t in range(TT):
                        xs = x[:, t, ds(SEQ * i, SEQ)]
                        V.scalar_tensor_tensor(out=xs, in0=bank[t][:, :], scalar=0.5, in1=xs, op0=ALU.mult, op1=ALU.add)\
                            .then_inc(drained_sem[t], 1)
                for t in range(TT):
                    dve.wait_ge(drained_sem[t], drained[t].at(L, "OUT", 1, 1))
                norm(L, "N2", 1)

                def top16(c, src, val, idx, groups):
                    def step(what):
                        for g in range(groups):
                            c.step(what(g))
                        c.wait()
                        stand(dve)
                    yield step(lambda g: V.max(val[:, g, 0:8], src[:, g, :]))
                    yield step(lambda g: V.max_index(idx[:, g, 0:8], val[:, g, 0:8], src[:, g, :]))
                    yield step(lambda g: V.match_replace(src[:, g, :], val[:, g, 0:8], src[:, g, :], NEG * 1e8))
                    yield step(lambda g: V.max(val[:, g, 8:16], src[:, g, :]))
                    yield step(lambda g: V.max_index(idx[:, g, 8:16], val[:, g, 8:16], src[:, g, :]))

                with dve.Fori(0, 4) as i:
                    c = Chain(dve, dve_step, L, "WQ", i)
                    for s in range(4):
                        dve.wait_ge(drained_sem[4 + s], drained[4 + s].at(L, "WQ", i, 1))
                    stand(dve)
                    for _ in top16(c, keys, kval, kidx, 16):
                        pass
                    c.step(V.tensor_copy(vals[:, :, ds(4 * i, 4), :], kval.rearrange("p (s t) n -> p t s n", t=TT)))
                    V.tensor_copy(idxf[:, :, ds(4 * i, 4), :], kidx[:, :, :].rearrange("p (s t) n -> p t s n", t=TT))\
                        .then_inc(best_done.sem, 1)
                    dve.wait_ge(best_done.sem, best_done.at(L, "WQ", i, 1))
                    c.close()
                    stand(dve)

                w3 = wts.rearrange("p (h n) -> p h n", h=PEER_H)
                full = [P, PEER_H, TOPK, TOPK]
                small = [P, PEER_H, TOPK]

                def choose(t):
                    c = Chain(dve, choose_step, L, "T", t)
                    v4 = vals[:, t, :, :].rearrange("p (h a) n -> p h a n", a=2)
                    i4 = idxf[:, t, :, :].rearrange("p (h a) n -> p h a n", a=2)
                    c.step(V.tensor_tensor(cand.rearrange("p h (a b) -> p h a b", a=TOPK),
                                           v4[:, :, 0, :].unsqueeze(3).to_broadcast(full),
                                           v4[:, :, 1, :].unsqueeze(2).to_broadcast(full), ALU.add))
                    c.wait()
                    stand(dve)
                    yield
                    yield from top16(c, cand, tv, posu[:, :].rearrange("p (h n) -> p h n", h=PEER_H), PEER_H)
                    c.step(V.tensor_scalar(posu2[:, 0, :], posu[:, :], 4, None, ALU.logical_shift_right))
                    c.step(V.tensor_scalar(posu2[:, 1, :], posu[:, :], 15, None, ALU.bitwise_and))
                    c.wait()
                    c.step(V.tensor_copy(posa, posu2[:, 0, :]))
                    c.step(V.tensor_copy(posb, posu2[:, 1, :]))
                    c.wait()
                    yield
                    for half, (pos, e) in enumerate(((posa, e1), (posb, e2))):
                        eq3 = eqb.rearrange("p (k n) -> p k n", n=TOPK)
                        c.step(V.tensor_tensor(eq3, pos.unsqueeze(2).to_broadcast([P, SLOTS, TOPK]),
                                               iota_f[:, :].unsqueeze(1).to_broadcast([P, SLOTS, TOPK]), ALU.is_equal))
                        c.wait()
                        yield
                        eq4 = eqb.rearrange("p (h k n) -> p h k n", h=PEER_H, n=TOPK)
                        c.step(V.tensor_tensor(eq4, eq4, i4[:, :, half, :].unsqueeze(2).to_broadcast(full), ALU.mult))
                        c.wait()
                        yield
                        c.step(V.tensor_reduce(e, eq3, AX.X, ALU.add))
                        c.wait()
                        yield
                    c.step(V.tensor_scalar(e2, e2, first_expert[:, :], None, ALU.add))
                    V.tensor_tensor(w3, tv, tv[:, :, 0:1].to_broadcast(small), ALU.subtract).then_inc(wsm_in.sem, 1)
                    c.wait()
                    V.scalar_tensor_tensor(out=eidx[:, t, :], in0=e1, scalar=float(N_KEYS), in1=e2,
                                           op0=ALU.mult, op1=ALU.add).then_inc(eidx_ready.sem, 1)
                    yield
                    dve.wait_ge(wsm_out.sem, wsm_out.at(L, "T", t, 1))
                    c.step(V.tensor_reduce(ssum, w3, AX.X, ALU.add))
                    c.wait()
                    c.step(V.reciprocal(ssum, ssum))
                    c.wait()
                    c.step(V.tensor_tensor(w3, w3, ssum.unsqueeze(2).to_broadcast(small), ALU.mult))
                    c.wait()
                    c.close()

                def tile(t, last):
                    pieces = iter(()) if last else choose(t + 1)
                    STRETCH = 2
                    turns = 2 * SLOTS // GR
                    for j0 in range(0, turns, STRETCH):
                        values = j0 >= turns // 2
                        if j0 == turns // 2:
                            dve.wait_ge(g_used.sem, g_used.at(L, "T", t, SLOTS))
                            c = Chain(dve, gelu_step, L, "T", t)
                            c.step(V.tensor_tensor(gin, actv, actv, ALU.mult))
                            c.wait()
                            c.step(V.tensor_scalar(gin, gin, 0.044715, 1.0, ALU.mult, ALU.add))
                            c.wait()
                            V.scalar_tensor_tensor(out=gin, in0=gin, scalar=0.7978845608028654, in1=actv,
                                                   op0=ALU.mult, op1=ALU.mult).then_inc(tanh_in.sem, 1)
                            c.step(V.scalar_tensor_tensor(out=coef, in0=actv, scalar=0.5, in1=wts, op0=ALU.mult, op1=ALU.mult))
                            c.wait()
                            dve.wait_ge(tanh_out.sem, tanh_out.at(L, "T", t, 1))
                            c.step(V.scalar_tensor_tensor(out=coef, in0=th, scalar=1.0, in1=coef, op0=ALU.add, op1=ALU.mult))
                            c.wait()
                            c.close()
                        stand(dve)
                        with dve.Fori(j0, j0 + STRETCH) as j:
                            for q in range(GR):
                                dve.wait_ge(g_ready[q], 16 * ((L * TT + t) * turns + j + 1))
                                if values:
                                    dve.wait_ge(g_used.sem, g_used.at(L, "T", t, q) + GR * j)
                                    V.scalar_tensor_tensor(out=x[:, t, :], in0=gring[:, q, :],
                                                           scalar=coef[:, ds(GR * j + (q - SLOTS), 1)],
                                                           in1=x[:, t, :], op0=ALU.mult, op1=ALU.add)\
                                        .then_inc(g_used.sem, 1)
                                else:
                                    V.scalar_tensor_tensor(out=gring[:, q, :], in0=gring[:, q, :], scalar=1.0,
                                                           in1=hn[:, t, :], op0=ALU.mult, op1=ALU.mult,
                                                           accum_out=actv[:, ds(GR * j + q, 1)]).then_inc(g_used.sem, 1)
                        next(pieces, None)
                    assert next(pieces, "end") == "end"

                for _ in choose(0):
                    pass
                stand(dve)
                with dve.Fori(0, TT - 1) as t:
                    tile(t, False)
                tile(TT - 1, True)
                dve.wait_ge(g_used.sem, g_used.at(L, "T", TT - 1, 2 * SLOTS))
                V.tensor_scalar(first_expert[:, :], first_expert[:, :], float(N_KEYS * N_KEYS), None, ALU.add)\
                    .then_inc(layer_done.sem, 1)

            for t in range(TT):
                V.scalar_tensor_tensor(out=hn[:, t, :], in0=x[:, t, :], scalar=1.0, in1=x[:, t, :],
                                       op0=ALU.mult, op1=ALU.mult, accum_out=stat[:, 0, t:t + 1]).then_inc(final_step, 1)
            dve.wait_ge(final_step, TT + 1)
            V.tensor_scalar(stat[:, 1, :], stat[:, 0, :], 1.0 / D, EPS, ALU.mult, ALU.add).then_inc(ms_final, 1)
            dve.wait_ge(sd_final, 1)
            V.reciprocal(stat[:, 3, :], stat[:, 2, :]).then_inc(final_step, 1)
            dve.wait_ge(final_step, TT + 2)
            dve.wait_ge(fnw_loaded, 16)
            for t in range(TT):
                scale_rows(t, nwb[:, 0, :]).then_inc(out_ready, 1)


def _rows_of(w, c0, n=P):
    return w[:, c0:c0 + n].reshape(KC, P, n).transpose(1, 0, 2).reshape(P, KC * n)


def _token_chunks(w, c0):
    return [w[2 * P * s:2 * P * (s + 1), c0:c0 + SEQ].reshape(2, P, SEQ).transpose(1, 0, 2).reshape(P, 2 * SEQ)
            for s in range(4)]


def _stream(w_in, w_lru, w_fox, w_ml, w_out, wq):
    chunks = []
    for i in range(2):
        chunks += [_rows_of(w_in, C_LRU + (4 * i + s) * P) for s in range(4)]
    for i in range(2):
        chunks += _token_chunks(w_in, C_FOX + 2 * D + i * SEQ)

    def merge(w, b):
        for j in range(KC):
            chunks.append(_rows_of(w, j * P))
            chunks.append(_rows_of(w_in, C_GATE + b * D + j * P))

    def pairs(c0):
        for j in range(KC):
            chunks.append(_rows_of(w_in, c0 + j * P))
            chunks.append(_rows_of(w_in, c0 + D + j * P))

    merge(w_lru, 0)
    pairs(C_FOX)
    for j in range(KC):
        chunks.append(_rows_of(w_in, C_O + j * P))
    merge(w_fox, 1)
    for i in range(2):
        chunks += _token_chunks(w_in, C_ML + 2 * D + i * SEQ)
    pairs(C_ML)
    merge(w_ml, 2)
    for i in range(2):
        chunks += _token_chunks(w_out, i * SEQ)
    for j in range(2 * KC):
        chunks.append(_rows_of(wq, j * P))
    return chunks


def kernel(x, norm1_w, w_in, lru_conv_w, lru_conv_b, lru_wa, lru_ba, lru_wx, lru_bx, lru_lambda,
           fox_fgate_b, mlstm_igate_b, mlstm_fgate_b, mlstm_norm_w, merge_gate_b,
           w_br_lru, w_br_fox, w_br_mlstm, w_out, norm2_w,
           peer_wq, peer_subkeys1, peer_subkeys2, peer_u, peer_v, final_norm_w):
    import concourse.bacc as bacc
    from concourse.bass_utils import run_bass_kernel_spmd as run

    def column(v):
        return np.asarray(v).reshape(-1, P).T

    def column_of(v, n):
        c = np.zeros((P, 1), np.float32)
        c[0:n, 0] = v
        return c

    stream, pvs, lru = [], [], []
    for L in range(DEPTH):
        w = np.asarray(w_in[L])
        stream += _stream(w, np.asarray(w_br_lru[L]), np.asarray(w_br_fox[L]), np.asarray(w_br_mlstm[L]),
                          np.asarray(w_out[L]), np.asarray(peer_wq[L]))
        wgate = np.concatenate([w[:, C_MLF:C_MLF + ML_H], w[:, C_FOXF:C_FOXF + FOX_H], w[:, C_MLI:C_MLI + ML_H]], axis=1)
        fb = np.concatenate([np.asarray(mlstm_fgate_b[L]), np.asarray(fox_fgate_b[L])])
        pvs.append(np.concatenate([
            column(lru_conv_w[L]), column(lru_conv_b[L]), column(lru_ba[L]), column(lru_bx[L]),
            column(merge_gate_b[L]), column(lru_lambda[L]), column(mlstm_norm_w[L]),
            column_of(fb, NROW), column_of(np.asarray(mlstm_igate_b[L]), ML_H),
            _rows_of(wgate, 0, 32), np.asarray(peer_subkeys1[L]).T, np.asarray(peer_subkeys2[L]).T], axis=1))
        both = np.stack([np.asarray(lru_wa[L]), np.asarray(lru_wx[L])], axis=1)
        lru.append(both.reshape(2, 4, 2, P, P).transpose(0, 3, 1, 2, 4).reshape(2, P, D))
    arrays = {
        "x_in": np.ascontiguousarray(np.asarray(x)[0]),
        "w_stream": np.stack(stream),
        "w_lru": np.concatenate(lru),
        "pvec": np.stack(pvs),
        "nrows": np.stack([np.asarray(a) for L in range(DEPTH) for a in (norm1_w[L], norm2_w[L])]),
        "fnorm": np.asarray(final_norm_w),
        "u_tab": np.asarray(peer_u).reshape(-1, D),
        "v_tab": np.asarray(peer_v).reshape(-1, D),
    }
    nc = bacc.Bacc("TRN2", target_bir_lowering=False, num_devices=1)
    args = [nc.dram_tensor(n, a.shape, mybir.dt.from_np(a.dtype), kind="ExternalInput").ap() for n, a in arrays.items()]
    out = nc.dram_tensor("out", (SEQ, D), F32, kind="ExternalOutput").ap()
    build(nc, *args, out)
    r = run(nc, [arrays], core_ids=[0])
    return r.results[0]["out"].reshape(1, SEQ, D)
```

```python
from contextlib import ExitStack

import concourse.bass as bass
from concourse import mybir
import numpy as np

F32 = mybir.dt.float32
F32R = mybir.dt.float32r
I32 = mybir.dt.int32
U32 = mybir.dt.uint32
ALU = mybir.AluOpType
ACT = mybir.ActivationFunctionType
AX = mybir.AxisListType
ds = bass.ds

P = 128
SEQ = 512
D = 1024
DEPTH = 2
TT = SEQ // P
KC = D // P
EPS = 1e-6
FOX_H, FOX_D = 16, 64
ML_H, ML_D = 8, 128
CONV = 4
TOPK = 16
N_KEYS = 128
PEER_H = 8
SLOTS = PEER_H * TOPK
GR = 8
NEG = -1e30

C_LRU, C_FOX, C_FOXF = 0, D, D + 3 * D
C_ML = C_FOXF + FOX_H
C_MLI = C_ML + 3 * D
C_MLF = C_MLI + ML_H
C_O = C_MLF + ML_H
C_GATE = C_O + D
NROW = ML_H + FOX_H
I_ROW = 32
GATES = I_ROW + ML_H

ROUNDS = dict(LRU=2, FV=2, MA=4, FQ=4, MV=2, MB=4, MO=2, MQ=4, MC=4, OUT=2, WQ=4)
NROUND = sum(ROUNDS.values())
ROUND0 = {p: sum(list(ROUNDS.values())[:n]) for n, p in enumerate(ROUNDS)}

PV_COLS = {}
_at = 0
for _n, _w in (("conv_w", CONV * KC), ("conv_b", KC), ("ba", KC), ("bx", KC), ("gate_b", 3 * KC),
               ("lam", KC), ("nw", KC), ("fbias", 1), ("ibias", 1), ("sub", 2 * P), ("wgate", KC * GATES)):
    PV_COLS[_n] = (_at, _at + _w)
    _at += _w
PV = _at
PV_KEPT = PV_COLS["wgate"][0]


class Count:

    def __init__(self, sem, plan, credit=0):
        self.sem, self.plan, self.credit, self.start = sem, plan, credit, {}
        n = 0
        for phase, (iters, per) in plan.items():
            self.start[phase] = n
            n += iters * per
        self.total = n

    def at(self, L, phase, i, n):
        return L * self.total + i * self.plan[phase][1] + (self.start[phase] + n + self.credit)


class Chain:

    def __init__(self, eng, count, L, phase, i):
        self.eng, self.count, self.where, self.n = eng, count, (L, phase, i), 0

    def step(self, ins):
        ins.then_inc(self.count.sem, 1)
        self.n += 1

    def wait(self):
        self.eng.wait_ge(self.count.sem, self.count.at(*self.where, self.n))

    def close(self):
        want = self.count.plan[self.where[1]][1]
        assert self.n == want, f"{self.where[1]}: {self.n} steps, {want} planned"


def fox_steps():
    seq = [("C", 0)]
    for k in range(16 + 3):
        if k < 16:
            seq.append(("S", k))
        if k % 4 == 2 and k < 13:
            seq.append(("C", k // 4 + 1))
        if 2 <= k < 18:
            seq.append(("T", k - 2))
        if k >= 3:
            seq.append(("V", k - 3))
            if (k - 3) % 8 == 7:
                seq.append(("Y", (k - 3) // 8))
    return seq


def build(nc, x_in, w_stream, w_lru, pvec, nrows, fnorm, u_tab, v_tab, out):
    with ExitStack() as ctx:
        def sb(name, shape, dt=F32):
            return ctx.enter_context(nc.sbuf_tensor(name, shape, dt))

        def sem(name):
            return ctx.enter_context(nc.semaphore(name))

        bank = [ctx.enter_context(nc.psum_tensor(f"bank{b}", [P, SEQ], F32)) for b in range(8)]

        vg_at = -(-nc.sbuf_base // 32) * 32
        vg = sb("vg", [P, 2 * KC, SEQ])
        hn_at = nc.sbuf_base
        hn = sb("hn", [P, TT, D])
        big_at = nc.sbuf_base
        big = sb("big", [P, 2 * KC, SEQ])
        att_at = nc.sbuf_base
        att = sb("att", [P, 8192])
        xl_mix = nc.alloc_sbuf_tensor_at("xl_mix", [P, TT, D], F32R, offset=hn_at)
        xl_peer = nc.alloc_sbuf_tensor_at("xl_peer", [P, TT, D], F32R, offset=vg_at)
        x = sb("x", [P, TT, D])
        y_hi_lru = nc.alloc_sbuf_tensor_at("y_hi_lru", [P, KC, SEQ], F32R, offset=att_at)
        y_hi = nc.alloc_sbuf_tensor_at("y_hi", [P, KC, SEQ], F32R, offset=vg_at + 4 * KC * SEQ)
        y_lo = nc.alloc_sbuf_tensor_at("y_lo", [P, KC, SEQ], F32R, offset=big_at)
        m_hi = nc.alloc_sbuf_tensor_at("m_hi", [P, KC, SEQ], F32R, offset=vg_at)
        m_lo = nc.alloc_sbuf_tensor_at("m_lo", [P, KC, SEQ], F32R, offset=big_at + 4 * KC * SEQ)
        xT = sb("xT", [P, KC, SEQ], F32R)
        w_hi = [sb(f"w_hi{b}", [P, D], F32R) for b in range(2)]
        w_lo = [sb(f"w_lo{b}", [P, D], F32R) for b in range(2)]
        ring = [sb(f"ring{s}", [P, D]) for s in range(4)]
        pv = sb("pv", [P, PV_KEPT])
        nwb = sb("nwb", [P, D])
        yT = big[:, 0:KC, :]
        merged = big[:, KC:2 * KC, :]
        bflat = big[:, :, :].rearrange("p a n -> p (a n)")
        v_sb = vg[:, 0:KC, :].rearrange("p (t a) c -> p t (a c)", t=TT)
        og = vg[:, KC:2 * KC, :]
        gring = vg[:, :, :].rearrange("p (r a) c -> p r (a c)", r=GR)
        qk = sb("qk", [P, 4, SEQ])
        ident = sb("ident", [P, P])
        ones = sb("ones", [P, P])
        inv = sb("inv", [P, P])
        mask_q = sb("mask_q", [P, P])
        mask_k = sb("mask_k", [P, P])
        iota_i = sb("iota_i", [P, TOPK], I32)
        iota_f = sb("iota_f", [P, TOPK])
        eps_t = sb("eps_t", [P, 1])
        stat = sb("stat", [P, 4, TT])
        hb = sb("hb", [P, 5 * KC])
        nsp = sb("nsp", [P, KC])
        hnw = sb("hnw", [P, KC])
        lp = sb("lp", [P, 3, KC])
        first_expert = sb("first_expert", [P, 1])
        rows = att[0:NROW, 0:6 * SEQ].rearrange("p (a n) -> p a n", a=6)
        cum = sb("cum", [NROW, SEQ])
        g_row = sb("g_row", [ML_H, SEQ])
        G_row = sb("G_row", [ML_H, SEQ])
        m_row = sb("m_row", [ML_H, SEQ])
        cumc = sb("cumc", [P, TT, NROW])
        gcol = sb("gcol", [P, TT, ML_H])
        sel = sb("sel", [NROW, 4, P])
        vst = sb("vst", [P, TT, 2, P])
        lruw = att[:, 6656:6656 + 8 * P].rearrange("p (s g n) -> p s g n", s=4, g=2)
        wgate = att[:, 7680:7680 + KC * GATES]
        NPAD = SEQ + CONV - 1
        xpad = att[:, 4096:4096 + 4 * NPAD].rearrange("p (s n) -> p s n", s=4)
        gt = [att[:, 4096 + j * SEQ:4096 + (j + 1) * SEQ] for j in range(2)]
        mtmp = att[:, 7168:7168 + SEQ]

        xc = merged[:, 0:4, :]
        R = merged[:, 4:8, :]
        TI = og[:, 0:4, :]
        A = og[:, 4:8, :]
        TH = qk
        sc = att[:, 0:1024].rearrange("p (a n) -> p a n", a=2)
        pr = att[:, 1024:2048].rearrange("p (a n) -> p a n", a=2)
        pT = att[:, 2048:3072].rearrange("p (a n) -> p a n", a=2)
        cb = att[:, 3072:4096].rearrange("p (a n) -> p a n", a=2)
        ytok = att[:, 4096:4608].rearrange("p (t n) -> p t n", t=TT)
        nmax = att[:, 4608:4624]
        rsum = att[:, 4624:4640]
        rinv = att[:, 4640:4656]
        E = att[:, 0:4096].rearrange("p (a s n) -> p a s n", a=2, s=4)
        gb = att[:, 4096:4608]
        gdm = att[:, 4608:5120].rearrange("p (s n) -> p s n", s=4)
        em = att[:, 5120:6144].rearrange("p (a n) -> p a n", a=2)
        hh = att[:, 6144:7168].rearrange("p (a n) -> p a n", a=2)
        sq = att[:, 7168:8192].rearrange("p (a n) -> p a n", a=2)
        keys = bflat[:, 0:2048].rearrange("p (g n) -> p g n", g=16)
        kval = bflat[:, 2048:2304].rearrange("p (g n) -> p g n", g=16)
        vals = bflat[:, 2304:3328].rearrange("p (t a n) -> p t a n", t=TT, n=TOPK)
        idxf = bflat[:, 3328:4352].rearrange("p (t a n) -> p t a n", t=TT, n=TOPK)
        kidx = bflat[:, 4352:4608].bitcast(U32).rearrange("p (g n) -> p g n", g=16)
        cand = att[:, 0:2048].rearrange("p (h n) -> p h n", h=PEER_H)
        eqb = att[:, 2048:4096]
        tv = att[:, 4608:4736].rearrange("p (h n) -> p h n", h=PEER_H)
        posa = att[:, 4736:4864]
        posb = att[:, 4864:4992]
        e1 = att[:, 4992:5120]
        e2 = att[:, 5120:5248]
        wts = att[:, 5248:5376]
        actv = att[:, 5376:5504]
        th = att[:, 5504:5632]
        gin = att[:, 5632:5760]
        coef = att[:, 5760:5888]
        ssum = att[:, 5888:5896]
        posu = att[:, 6144:6272].bitcast(U32)
        posu2 = att[:, 6272:6528].bitcast(U32).rearrange("p (a n) -> p a n", a=2)
        eidx = bflat[:, 4608:5120].bitcast(U32).rearrange("p (t n) -> p t n", t=TT)
        estage = [sb(f"estage{h}", [P, GR], U32) for h in range(2)]

        def pcol(name, a, b=None):
            c0 = PV_COLS[name][0]
            return pv[:, c0 + a:c0 + (a + 1 if b is None else b)]

        def dcol(buf, at):
            return buf[:, ds(at, 1)]

        subk = pcol("sub", 0, 2 * P).rearrange("p (a n) -> p a n", a=2)

        x_loaded = sem("x_loaded")
        fnw_loaded = sem("fnw_loaded")
        consts_ready = sem("consts_ready")
        pool_step = sem("pool_step")
        params_ready = sem("params_ready")
        wgate_ready = sem("wgate_ready")
        nw_loaded = sem("nw_loaded")
        lruw_ready = sem("lruw_ready")
        w_ready = [sem(f"w_ready{s}") for s in range(4)]
        proj_done = sem("proj_done")
        g_ready = [sem(f"g_ready{q}") for q in range(GR)]
        out_done = sem("out_done")
        out_ready = sem("out_ready")
        pool_stage = sem("pool_stage")
        waits_taken = sem("waits_taken")
        pad_ready = sem("pad_ready")
        ms_final = sem("ms_final")
        sd_final = sem("sd_final")
        final_step = sem("final_step")
        drained_sem = [sem(f"drained{b}") for b in range(8)]
        drained = [Count(drained_sem[s], {p: (n, 1) for p, n in ROUNDS.items()}, 1) for s in range(4)]
        work = [dict(N1=(1, 2), G=(1, int(b == 0)), LRU=(2, 2), COLS=(1, int(b >= 2)),
                     FQ=(4, (8, 8, 16, 22)[b]), MQ=(4, (4, 4, 6, 6)[b]), N2=(1, 2), WQ=(4, 1))
                for b in range(4)]
        drained += [Count(drained_sem[4 + b], work[b], 1) for b in range(4)]
        filled = {4 + b: Count(sem(f"filled{4 + b}"), work[b]) for b in range(4)}
        one = lambda *names: {n: (1, 1) for n in names}
        layer_done = Count(sem("layer_done"), one("L"), 1)
        ms_ready = Count(sem("ms_ready"), one("N1", "N2"))
        sd_ready = Count(sem("sd_ready"), one("N1", "N2"))
        xh_ready = Count(sem("xh_ready"), dict(N1=(1, KC), N2=(1, KC)))
        split = dict(G=(1, 1), **{p: (n, 4) for p, n in ROUNDS.items()})
        hi_done = Count(sem("hi_done"), split)
        split_ready = Count(sem("split_ready"), split)
        y_hi_ready = Count(sem("y_hi_ready"), dict(LRU=(2, 1), FQ=(4, 2), MQ=(4, 1), MC=(4, 1)))
        y_lo_ready = Count(sem("y_lo_ready"), dict(LRU=(1, 1), FQ=(4, 1), MQ=(4, 1), MC=(4, 1)))
        hn_ready = Count(sem("hn_ready"), dict(N1=(1, TT), N2=(1, TT)))
        zexp_in = Count(sem("zexp_in"), one("P", "G"))
        zexp_out = Count(sem("zexp_out"), one("P", "G"))
        rows_ready = Count(sem("rows_ready"), one("G"))
        conv_done = Count(sem("conv_done"), dict(LRU=(2, 4)))
        la_ready = Count(sem("la_ready"), dict(LRU=(2, 1)))
        ea_ready = Count(sem("ea_ready"), dict(LRU=(2, 2)))
        q_ready = Count(sem("q_ready"), dict(LRU=(2, 1)))
        sq_ready = Count(sem("sq_ready"), dict(LRU=(2, 1)))
        lru_done = Count(sem("lru_done"), dict(LRU=(2, 1)), 1)
        merged_ready = Count(sem("merged_ready"), dict(MB=(4, 2), MC=(4, 2)), 1)
        sel_ready = Count(sem("sel_ready"), dict(FQ=(4, 1), MQ=(4, 1)))
        vst_ready = Count(sem("vst_ready"), dict(MQ=(4, 1)))
        srow_ready = Count(sem("srow_ready"), dict(FQ=(4, 16)))
        prob_ready = Count(sem("prob_ready"), dict(FQ=(4, 16)), 2)
        rinv_ready = Count(sem("rinv_ready"), dict(FQ=(4, 16)))
        gdm_ready = Count(sem("gdm_ready"), dict(MQ=(4, 2)))
        dec_ready = Count(sem("dec_ready"), dict(MQ=(4, 8)))
        wts_ready = Count(sem("wts_ready"), dict(MQ=(4, 8)))
        h_ready = Count(sem("h_ready"), dict(MQ=(4, 2)))
        hc_ready = Count(sem("hc_ready"), dict(MQ=(4, 2)))
        hsq_ready = Count(sem("hsq_ready"), dict(MQ=(4, 2)))
        ml_y = Count(sem("ml_y"), dict(MQ=(4, 2)), 2)
        og_done = Count(sem("og_done"), dict(MO=(2, 4)))
        best_done = Count(sem("best_done"), dict(WQ=(4, 1)), 1)
        wsm_in = Count(sem("wsm_in"), dict(T=(TT, 1)))
        wsm_out = Count(sem("wsm_out"), dict(T=(TT, 1)))
        tanh_in = Count(sem("tanh_in"), dict(T=(TT, 1)))
        tanh_out = Count(sem("tanh_out"), dict(T=(TT, 1)))
        eidx_ready = Count(sem("eidx_ready"), dict(T=(TT, 1)))
        g_used = Count(sem("g_used"), dict(T=(TT, 2 * SLOTS)), GR)
        dve_step = Count(sem("dve_step"), dict(
            N1=(1, 5), P=(1, 17), G=(1, 19), LRU=(2, 21), FQ=(4, 16), MQ=(4, 8),
            N2=(1, 5), WQ=(4, 81)))
        choose_step = Count(sem("choose_step"), dict(T=(TT, 55)))
        gelu_step = Count(sem("gelu_step"), dict(T=(TT, 4)))
        dve_total = dve_step.total

        def stand(eng):
            eng.sem_inc(waits_taken, 1)

        def rnd(L, phase, i):
            return L * NROUND + i + ROUND0[phase]

        def slots_done(L, phase, i, n):
            return 4 * rnd(L, phase, i) + (n + 4)

        block = ctx.enter_context(nc.Block())

        @block.sync
        def _(sp):
            sp.dma_start(x[:, :, :], x_in.rearrange("(t p) d -> p t d", p=P)).then_inc(x_loaded, 16)
            for s in range(4):
                sp.dma_start(ring[s][:, :], w_stream[s]).then_inc(w_ready[s], 16)
            with sp.Fori(1, DEPTH * NROUND) as r:
                for s in range(4):
                    sp.wait_ge(proj_done, 4 * r + (s + 1))
                    sp.dma_start(ring[s][:, :], w_stream[4 * r + s]).then_inc(w_ready[s], 16)
            sp.wait_ge(layer_done.sem, DEPTH + 1)
            sp.dma_start(nwb[:, :], fnorm.partition_broadcast(P)).then_inc(fnw_loaded, 16)
            sp.wait_ge(out_ready, 4)
            sp.dma_start(out.rearrange("(t p) d -> p t d", p=P), hn[:, :, :]).then_inc(out_done, 16)
            sp.wait_ge(out_done, 16)

        @block.gpsimd
        def _(pool):
            nc.gpsimd.memset(ident[:, :], 0.0).then_inc(pool_step, 1)
            nc.gpsimd.memset(mask_q[:, :], 0.0).then_inc(pool_step, 1)
            nc.gpsimd.memset(mask_k[:, :], 0.0).then_inc(pool_step, 1)
            nc.gpsimd.memset(ones[:, :], 1.0).then_inc(pool_step, 1)
            nc.gpsimd.memset(inv[:, :], 1.0 / P).then_inc(pool_step, 1)
            nc.gpsimd.memset(eps_t[:, :], EPS).then_inc(pool_step, 1)
            nc.gpsimd.iota(iota_i[:, :], pattern=[[1, TOPK]], base=0, channel_multiplier=0).then_inc(pool_step, 1)
            pool.wait_ge(pool_step, 7)
            nc.gpsimd.affine_select(out=ident[:, :], in_=ident[:, :], compare_op=ALU.not_equal, fill=1.0,
                                    base=0, pattern=[[-1, P]], channel_multiplier=1).then_inc(consts_ready, 1)
            nc.gpsimd.affine_select(out=mask_q[:, :], in_=mask_q[:, :], compare_op=ALU.is_ge, fill=NEG,
                                    base=0, pattern=[[-1, P]], channel_multiplier=1).then_inc(consts_ready, 1)
            nc.gpsimd.affine_select(out=mask_k[:, :], in_=mask_k[:, :], compare_op=ALU.is_ge, fill=-NEG,
                                    base=0, pattern=[[1, P]], channel_multiplier=-1).then_inc(consts_ready, 1)
            nc.gpsimd.tensor_copy(iota_f[:, :], iota_i[:, :]).then_inc(consts_ready, 1)
            pool.wait_ge(consts_ready, 4)

            def gathers(table, L, t, base):
                stand(pool)
                with pool.Fori(0, SLOTS // (2 * GR)) as j:
                    for half in range(2):
                        nc.gpsimd.tensor_copy(estage[half][:, :], eidx[:, t, ds(2 * GR * j + GR * half, GR)])\
                            .then_inc(pool_stage, 1)
                        pool.wait_ge(pool_stage, stage_at(L, t, base, j, half))
                        for q in range(GR):
                            n = base + GR * half + q
                            pool.wait_ge(g_used.sem, g_used.at(L, "T", t, n) + 2 * GR * j + (1 - GR))
                            stand(pool)
                            nc.gpsimd.indirect_dma_start(
                                out=gring[:, q, :], out_offset=None, in_=table,
                                in_offset=bass.IndirectOffsetOnAxis(ap=estage[half][:, q:q + 1], axis=0))\
                                .then_inc(g_ready[q], 16)

            def stage_at(L, t, base, j, half):
                per = 2 * SLOTS // GR
                return (L * TT + t) * per + base // GR + 2 * j + (half + 1)

            def split_parts(b, src, n, L, ph, i, k):
                stand(pool)
                nc.gpsimd.tensor_tensor(w_hi[b][:, 0:n], src, ones[:, 0:1].to_broadcast([P, n]), ALU.mult)\
                    .then_inc(hi_done.sem, 1)
                pool.wait_ge(hi_done.sem, hi_done.at(L, ph, i, k + 1))
                nc.gpsimd.tensor_tensor(w_lo[b][:, 0:n], src, w_hi[b][:, 0:n].bitcast(F32), ALU.subtract)\
                    .then_inc(split_ready.sem, 1)

            def split_round(L, ph, i, slots=range(4)):
                for s in slots:
                    pool.wait_ge(w_ready[s], 16 * rnd(L, ph, i) + 16)
                    pool.wait_ge(proj_done, slots_done(L, ph, i, s - 1))
                    split_parts(s % 2, ring[s][:, :], D, L, ph, i, s)

            def split_rounds(L, ph):
                with pool.Fori(0, ROUNDS[ph]) as i:
                    split_round(L, ph, i)

            with pool.Fori(0, DEPTH) as L:
                pool.wait_ge(wgate_ready, 16 * L + 16)
                split_parts(0, wgate, KC * GATES, L, "G", 0, 0)
                pool.wait_ge(filled[4].sem, filled[4].at(L, "G", 0, 1))
                stand(pool)
                split_rounds(L, "LRU")
                split_rounds(L, "FV")
                split_rounds(L, "MA")
                with pool.Fori(0, 4) as i:
                    split_round(L, "FQ", i, (0, 1))
                    pool.wait_ge(filled[7].sem, filled[7].at(L, "FQ", i, 0))
                    stand(pool)
                    nc.gpsimd.tensor_copy(sel[:, :, :], ident[0:NROW, ds(4 * i + ML_H, 4)]
                                          .unsqueeze(2).to_broadcast([NROW, 4, P])).then_inc(sel_ready.sem, 1)
                    split_round(L, "FQ", i, (2, 3))
                split_rounds(L, "MV")
                split_rounds(L, "MB")
                split_rounds(L, "MO")
                with pool.Fori(0, 4) as i:
                    split_round(L, "MQ", i, (0, 1))
                    pool.wait_ge(filled[7].sem, filled[7].at(L, "MQ", i, 0))
                    pool.wait_ge(filled[6].sem, filled[6].at(L, "MQ", i, 0))
                    stand(pool)
                    nc.gpsimd.tensor_copy(sel[:, 0:2, :], ident[0:NROW, ds(2 * i, 2)]
                                          .unsqueeze(2).to_broadcast([NROW, 2, P])).then_inc(sel_ready.sem, 1)
                    for s in range(4):
                        pool.wait_ge(drained[s].sem, drained[s].at(L, "MV", 1, 1))
                    stand(pool)
                    nc.gpsimd.tensor_copy(vst[:, :, :, :].rearrange("p t a n -> p t (a n)"),
                                          v_sb[:, :, ds(2 * P * i, 2 * P)]).then_inc(vst_ready.sem, 1)
                    split_round(L, "MQ", i, (2, 3))
                split_rounds(L, "MC")
                split_rounds(L, "OUT")
                split_rounds(L, "WQ")
                with pool.Fori(0, TT) as t:
                    pool.wait_ge(eidx_ready.sem, eidx_ready.at(L, "T", t, 1))
                    gathers(u_tab, L, t, 0)
                    gathers(v_tab, L, t, SLOTS)

        @block.tensor
        def _(pe):
            for b in range(8):
                pe.sem_inc(drained_sem[b], 1)
            pe.wait_ge(consts_ready, 4)

            def fill_wait(b, L, ph, i, n):
                pe.wait_ge(drained[b].sem, drained[b].at(L, ph, i, n))

            def transpose_norm(L, ph):
                for c in range(KC):
                    b = 4 + c % 4
                    fill_wait(b, L, ph, 0, c // 4)
                    for t in range(TT):
                        if c == 0:
                            pe.wait_ge(hn_ready.sem, hn_ready.at(L, ph, 0, t + 1))
                        mm = nc.tensor.transpose(bank[b][:, t * P:(t + 1) * P], hn[:, t, c * P:(c + 1) * P], ident[:, :])
                    mm.then_inc(filled[b].sem, 1)
                pe.wait_ge(xh_ready.sem, xh_ready.at(L, ph, 0, KC))
                stand(pe)

            def low_wait(L, ph):
                for b in range(4, 8):
                    pe.wait_ge(drained[b].sem, drained[b].at(L, ph, 0, 2))

            def high_low(out, w, x, low_wait):
                for c in range(KC):
                    for part in range(2):
                        nc.tensor.matmul(out, w(c)[part], x(c)[0], start=(c == 0 and part == 0), stop=False)
                low_wait()
                for c in range(KC):
                    mm = nc.tensor.matmul(out, w(c)[0], x(c)[1], start=False, stop=(c == KC - 1))
                return mm

            def x_parts(low):
                return lambda c: (xT[:, c, :], low[:, :, c * P:(c + 1) * P])

            def y_parts(hi):
                return lambda c: (hi[:, c, :], y_lo[:, c, :])

            def project(L, ph, i, s, x, low_wait=lambda: None):
                pe.wait_ge(split_ready.sem, split_ready.at(L, ph, i, s + 1))
                pe.wait_ge(drained_sem[s], rnd(L, ph, i) + 1)
                high_low(bank[s][:, :], lambda c: [w[s % 2][:, c * P:(c + 1) * P] for w in (w_hi, w_lo)], x, low_wait)\
                    .then_inc(proj_done, 1)

            def project_tokens(L, ph, i, hi, lo):
                for s in range(4):
                    pe.wait_ge(split_ready.sem, split_ready.at(L, ph, i, s + 1))
                    for t in range(TT):
                        if s == 0:
                            pe.wait_ge(drained_sem[t], rnd(L, ph, i) + 1)
                        for kk in range(2):
                            c = 2 * s + kk
                            wh, wl = (w[s % 2][:, kk * SEQ:(kk + 1) * SEQ] for w in (w_hi, w_lo))
                            for n, (lhsT, rhs) in enumerate(((hi(c, t), wh), (hi(c, t), wl), (lo(c, t), wh))):
                                mm = nc.tensor.matmul(bank[t][:, :], lhsT, rhs, start=(c == 0 and n == 0),
                                                      stop=(c == KC - 1 and n == 2))
                    mm.then_inc(proj_done, 1)

            def of_tile(buf):
                return lambda c, t: buf[:, c, t * P:(t + 1) * P]

            def xl_of_tile(c, t):
                return xl_mix[:, t, c * P:(c + 1) * P]

            def merge(L, ph, hi):
                stand(pe)
                with pe.Fori(0, 4) as i:
                    for s in range(4):
                        project(L, ph, i, s, x_parts(xl_mix) if s % 2 else y_parts(hi))

            with pe.Fori(0, DEPTH) as L:
                transpose_norm(L, "N1")
                pe.wait_ge(split_ready.sem, split_ready.at(L, "G", 0, 1))
                fill_wait(4, L, "G", 0, 0)
                high_low(bank[4][0:GATES, :], lambda c: [w[0][:, c * GATES:(c + 1) * GATES] for w in (w_hi, w_lo)],
                         x_parts(xl_mix), lambda: low_wait(L, "N1")).then_inc(filled[4].sem, 1)
                with pe.Fori(0, 2) as i:
                    for s in range(4):
                        project(L, "LRU", i, s, x_parts(xl_mix))
                    pe.wait_ge(lruw_ready, 32 * L + 16 * i + 16)
                    for s in range(4):
                        pe.wait_ge(conv_done.sem, conv_done.at(L, "LRU", i, s + 1))
                        for g in range(2):
                            b = 4 + 2 * (s % 2) + g
                            fill_wait(b, L, "LRU", i, s // 2)
                            nc.tensor.matmul(bank[b][:, :], lruw[:, s, g, :], xc[:, s, :], start=True, stop=True)\
                                .then_inc(filled[b].sem, 1)
                pe.wait_ge(rows_ready.sem, rows_ready.at(L, "G", 0, 1))
                fill_wait(6, L, "COLS", 0, 0)
                stand(pe)
                for t in range(TT):
                    mm = nc.tensor.transpose(bank[6][:, t * NROW:(t + 1) * NROW], cum[:, t * P:(t + 1) * P],
                                             ident[0:NROW, 0:NROW])
                mm.then_inc(filled[6].sem, 1)
                fill_wait(7, L, "COLS", 0, 0)
                stand(pe)
                for t in range(TT):
                    mm = nc.tensor.transpose(bank[7][:, t * ML_H:(t + 1) * ML_H], g_row[:, t * P:(t + 1) * P],
                                             ident[0:ML_H, 0:ML_H])
                mm.then_inc(filled[7].sem, 1)
                with pe.Fori(0, 2) as i:
                    project_tokens(L, "FV", i, of_tile(xT), xl_of_tile)
                pe.wait_ge(y_lo_ready.sem, y_lo_ready.at(L, "LRU", 0, 1))
                merge(L, "MA", y_hi_lru)
                with pe.Fori(0, 4) as i:
                    for s in range(4):
                        project(L, "FQ", i, s, x_parts(xl_mix))
                    pe.wait_ge(sel_ready.sem, sel_ready.at(L, "FQ", i, 1))
                    n6 = n7 = 0
                    for kind, u in fox_steps():
                        t, h = u % 4, u // 4
                        b = 4 + u % 2
                        if kind == "C":
                            fill_wait(7, L, "FQ", i, n7)
                            nc.tensor.matmul(bank[7][:, :], sel[:, u, :], cum[:, :], start=True, stop=True)\
                                .then_inc(filled[7].sem, 1)
                            n7 += 1
                        elif kind == "S":
                            pp, hp = h // 2, h % 2
                            if u == 0:
                                for s in range(4):
                                    pe.wait_ge(drained_sem[s], rnd(L, "FQ", i) + 2)
                            fill_wait(b, L, "FQ", i, u // 2)
                            rowsel = slice(FOX_D * hp, FOX_D * hp + FOX_D)
                            nc.tensor.matmul(bank[b][:, 0:(t + 1) * P], qk[rowsel, 2 * pp, t * P:(t + 1) * P],
                                             qk[rowsel, 2 * pp + 1, 0:(t + 1) * P], start=True, stop=True)\
                                .then_inc(filled[b].sem, 1)
                        elif kind == "T":
                            pe.wait_ge(prob_ready.sem, prob_ready.at(L, "FQ", i, u + 1))
                            fill_wait(6, L, "FQ", i, n6)
                            for kb in range(t + 1):
                                mm = nc.tensor.transpose(bank[6][:, kb * P:(kb + 1) * P],
                                                         pr[:, u % 2, kb * P:(kb + 1) * P], ident[:, :])
                            mm.then_inc(filled[6].sem, 1)
                            n6 += 1
                        elif kind == "V":
                            pe.wait_ge(drained_sem[6], drained[6].at(L, "FQ", i, u + 1))
                            fill_wait(7, L, "FQ", i, n7)
                            for kb in range(t + 1):
                                mm = nc.tensor.matmul(bank[7][:, 0:FOX_D], pT[:, u % 2, kb * P:(kb + 1) * P],
                                                      v_sb[:, kb, ds(4 * FOX_D * i + FOX_D * h, FOX_D)],
                                                      start=(kb == 0), stop=(kb == t))
                            mm.then_inc(filled[7].sem, 1)
                            n7 += 1
                        else:
                            fill_wait(7, L, "FQ", i, n7)
                            for tt in range(TT):
                                mm = nc.tensor.transpose(bank[7][:, tt * P:(tt + 1) * P], ytok[:, tt, :], ident[:, :])
                            mm.then_inc(filled[7].sem, 1)
                            n7 += 1
                with pe.Fori(0, 2) as i:
                    project_tokens(L, "MV", i, of_tile(xT), xl_of_tile)
                pe.wait_ge(y_lo_ready.sem, y_lo_ready.at(L, "FQ", 3, 1))
                merge(L, "MB", y_hi)
                with pe.Fori(0, 2) as i:
                    for s in range(4):
                        project(L, "MO", i, s, x_parts(xl_mix))
                with pe.Fori(0, 4) as i:
                    for s in range(4):
                        project(L, "MQ", i, s, x_parts(xl_mix))
                    pe.wait_ge(sel_ready.sem, sel_ready.at(L, "MQ", i, 1))
                    n = {6: 0, 7: 0}

                    def spread(b, p, row):
                        fill_wait(b, L, "MQ", i, n[b])
                        nc.tensor.matmul(bank[b][:, :], sel[0:ML_H, p, :], row[:, :], start=True, stop=True)\
                            .then_inc(filled[b].sem, 1)
                        n[b] += 1

                    def scores_of(p):
                        for s in range(TT):
                            b = 4 + s % 2
                            fill_wait(b, L, "MQ", i, 2 * p + s // 2)
                            nc.tensor.matmul(bank[b][:, 0:SEQ - s * P], qk[:, 2 * p + 1, s * P:(s + 1) * P],
                                             qk[:, 2 * p, s * P:SEQ], start=True, stop=True)\
                                .then_inc(filled[b].sem, 1)

                    def num_den(p):
                        for b in (6, 7):
                            fill_wait(b, L, "MQ", i, n[b])
                            for s in range(TT):
                                if b == 6:
                                    pe.wait_ge(wts_ready.sem, wts_ready.at(L, "MQ", i, 4 * p + s + 1))
                                lhsT = vst[:, s, p, :] if b == 6 else ones[:, 0:P]
                                mm = nc.tensor.matmul(bank[b][:, s * P:SEQ], lhsT, E[:, p, s, 0:SEQ - s * P],
                                                      start=(s == 0), stop=(s == TT - 1))
                            mm.then_inc(filled[b].sem, 1)
                            n[b] += 1

                    def mean(p, b, src, ready):
                        pe.wait_ge(ready.sem, ready.at(L, "MQ", i, p + 1))
                        fill_wait(b, L, "MQ", i, n[b])
                        nc.tensor.matmul(bank[b][:, :], inv[:, :], src[:, p, :], start=True, stop=True)\
                            .then_inc(filled[b].sem, 1)
                        n[b] += 1

                    for s in range(4):
                        pe.wait_ge(drained_sem[s], rnd(L, "MQ", i) + 2)
                    pe.wait_ge(vst_ready.sem, vst_ready.at(L, "MQ", i, 1))
                    spread(6, 0, G_row)
                    spread(7, 0, m_row)
                    scores_of(0)
                    num_den(0)
                    spread(6, 1, G_row)
                    spread(7, 1, m_row)
                    scores_of(1)
                    mean(0, 6, hh, h_ready)
                    num_den(1)
                    mean(0, 7, sq, hsq_ready)
                    mean(1, 6, hh, h_ready)
                    mean(1, 7, sq, hsq_ready)
                pe.wait_ge(y_lo_ready.sem, y_lo_ready.at(L, "MQ", 3, 1))
                merge(L, "MC", y_hi)
                pe.wait_ge(y_lo_ready.sem, y_lo_ready.at(L, "MC", 3, 1))
                stand(pe)
                with pe.Fori(0, 2) as i:
                    project_tokens(L, "OUT", i, of_tile(m_hi), of_tile(m_lo))
                transpose_norm(L, "N2")
                with pe.Fori(0, 4) as i:
                    for s in range(4):
                        project(L, "WQ", i, s, x_parts(xl_peer), lambda: low_wait(L, "N2"))
                    for s in range(4):
                        pe.wait_ge(drained_sem[s], rnd(L, "WQ", i) + 2)
                        fill_wait(4 + s, L, "WQ", i, 0)
                        for t in range(TT):
                            mm = nc.tensor.matmul(bank[4 + s][:, t * P:(t + 1) * P], qk[:, s, t * P:(t + 1) * P],
                                                  subk[:, s % 2, :], start=True, stop=True)
                        mm.then_inc(filled[4 + s].sem, 1)

        @block.scalar
        def _(act):
            act.sem_inc(prob_ready.sem, 2)

            def evac_norm(L, ph):
                act.wait_ge(ms_ready.sem, ms_ready.at(L, ph, 0, 1))
                nc.scalar.activation(stat[:, 2, :], stat[:, 1, :], ACT.Sqrt).then_inc(sd_ready.sem, 1)
                for c in range(KC):
                    b = 4 + c % 4
                    act.wait_ge(filled[b].sem, filled[b].at(L, ph, 0, c // 4 + 1))
                    nc.scalar.copy(xT[:, c, :], bank[b][:, :]).then_inc(xh_ready.sem, 1)

            def proj_wait(L, ph, i, s):
                act.wait_ge(proj_done, slots_done(L, ph, i, s + 1))

            def values(L, ph, i):
                proj_wait(L, ph, i, 3)
                for t in range(TT):
                    nc.scalar.copy(v_sb[:, t, i * SEQ:(i + 1) * SEQ], bank[t][:, :]).then_inc(drained_sem[t], 1)

            def lru_high(L, i):
                act.wait_ge(lru_done.sem, lru_done.at(L, "LRU", i, 1))
                nc.scalar.copy(y_hi_lru[:, 4 * i:4 * i + 4, :], yT[:, 4 * i:4 * i + 4, :]).then_inc(y_hi_ready.sem, 1)

            def merge_gates(L, ph, branch):
                with act.Fori(0, 4) as i:
                    for j in range(2):
                        proj_wait(L, ph, i, 2 * j + 1)
                        nc.scalar.activation(gt[j], bank[2 * j + 1][:, :], ACT.Tanh, scale=0.5,
                                             bias=dcol(hb, 2 * i + (2 * KC + branch * KC + j)))\
                            .then_inc(drained_sem[2 * j + 1], 1)
                    if ph == "MC":
                        act.wait_ge(merged_ready.sem, merged_ready.at(L, "MC", i, 2))
                        nc.scalar.copy(m_hi[:, ds(2 * i, 2), :], merged[:, ds(2 * i, 2), :]).then_inc(y_hi_ready.sem, 1)

            with act.Fori(0, DEPTH) as L:
                act.wait_ge(layer_done.sem, layer_done.at(L, "L", 0, 0))
                act.dma_start(pv[:, :], pvec[L][:, 0:PV_KEPT]).then_inc(params_ready, 16)
                act.dma_start(wgate, pvec[L][:, PV_KEPT:PV]).then_inc(wgate_ready, 16)
                act.dma_start(nwb[:, :], nrows[2 * L].partition_broadcast(P)).then_inc(nw_loaded, 16)
                act.dma_start(lruw, w_lru[2 * L].rearrange("p (s g n) -> p s g n", s=4, g=2))\
                    .then_inc(lruw_ready, 16)
                evac_norm(L, "N1")
                act.wait_ge(hn_ready.sem, hn_ready.at(L, "N1", 0, TT))
                act.dma_start(nwb[:, :], nrows[2 * L + 1].partition_broadcast(P)).then_inc(nw_loaded, 16)
                for ph in ("P", "G"):
                    act.wait_ge(zexp_in.sem, zexp_in.at(L, ph, 0, 1))
                    tile = lp[:, 0, :] if ph == "P" else rows[:, 1, :]
                    nc.scalar.activation(tile, tile, ACT.Exp).then_inc(zexp_out.sem, 1)
                for i in range(2):
                    for s in range(4):
                        proj_wait(L, "LRU", i, s)
                        if s == 0:
                            act.wait_ge(lru_done.sem, lru_done.at(L, "LRU", i, 0))
                        nc.scalar.copy(xpad[:, s, CONV - 1:], bank[s][:, :]).then_inc(drained_sem[s], 1)
                    for s in range(4):
                        for g in range(2):
                            b = 4 + 2 * (s % 2) + g
                            act.wait_ge(filled[b].sem, filled[b].at(L, "LRU", i, s // 2 + 1))
                            nc.scalar.activation((TI if g else R)[:, s, :], bank[b][:, :], ACT.Tanh, scale=0.5,
                                                 bias=hb[:, g * KC + 4 * i + s:g * KC + 4 * i + s + 1])\
                                .then_inc(drained_sem[b], 1)
                    if i == 0:
                        act.dma_start(lruw, w_lru[2 * L + 1].rearrange("p (s g n) -> p s g n", s=4, g=2))\
                            .then_inc(lruw_ready, 16)
                    if i == 1:
                        lru_high(L, 0)
                    act.wait_ge(la_ready.sem, la_ready.at(L, "LRU", i, 1))
                    nc.scalar.activation(TH[:, :, :], R, ACT.Tanh).then_inc(ea_ready.sem, 1)
                    nc.scalar.activation(A, R, ACT.Exp).then_inc(ea_ready.sem, 1)
                    act.wait_ge(q_ready.sem, q_ready.at(L, "LRU", i, 1))
                    nc.scalar.activation(TH[:, :, :], TH[:, :, :], ACT.Sqrt, scale=-0.25).then_inc(sq_ready.sem, 1)
                act.wait_ge(filled[6].sem, filled[6].at(L, "COLS", 0, 1))
                nc.scalar.copy(cumc[:, :, :], bank[6][:, 0:TT * NROW].rearrange("p (t n) -> p t n", t=TT))\
                    .then_inc(drained_sem[6], 1)
                act.wait_ge(filled[7].sem, filled[7].at(L, "COLS", 0, 1))
                nc.scalar.copy(gcol[:, :, :], bank[7][:, 0:TT * ML_H].rearrange("p (t n) -> p t n", t=TT))\
                    .then_inc(drained_sem[7], 1)
                values(L, "FV", 0)
                lru_high(L, 1)
                values(L, "FV", 1)
                merge_gates(L, "MA", 0)
                with act.Fori(0, 4) as i:
                    for s in range(4):
                        proj_wait(L, "FQ", i, s)
                        nc.scalar.activation(qk[:, s, :], bank[s][:, :], ACT.Copy,
                                             scale=FOX_D ** -0.5 if s % 2 == 0 else 1.0)\
                            .then_inc(drained_sem[s], 1)
                    n7 = 0
                    todo = []
                    for kind, u in fox_steps():
                        t, h = u % 4, u // 4
                        n = (t + 1) * P
                        if kind == "S":
                            todo.append(u)
                        if kind == "C":
                            act.wait_ge(filled[7].sem, filled[7].at(L, "FQ", i, n7 + 1))
                            nc.scalar.copy(cb[:, u % 2, :], bank[7][:, :]).then_inc(drained_sem[7], 1)
                            n7 += 1
                        if kind == "T":
                            act.wait_ge(filled[6].sem, filled[6].at(L, "FQ", i, u + 1))
                            nc.scalar.copy(pT[:, u % 2, 0:n], bank[6][:, 0:n]).then_inc(drained_sem[6], 1)
                        if kind == "V":
                            act.wait_ge(filled[7].sem, filled[7].at(L, "FQ", i, n7 + 1))
                            act.wait_ge(rinv_ready.sem, rinv_ready.at(L, "FQ", i, u + 1))
                            nc.scalar.activation(ytok[:, t, FOX_D * (h % 2):FOX_D * (h % 2) + FOX_D],
                                                 bank[7][:, 0:FOX_D], ACT.Copy, scale=rinv[:, u:u + 1])\
                                .then_inc(drained_sem[7], 1)
                            n7 += 1
                        if kind == "Y":
                            act.wait_ge(filled[7].sem, filled[7].at(L, "FQ", i, n7 + 1))
                            nc.scalar.copy(yT[:, 2 * i + u, :], bank[7][:, :]).then_inc(drained_sem[7], 1)
                            n7 += 1
                            act.wait_ge(drained_sem[7], drained[7].at(L, "FQ", i, n7))
                            nc.scalar.copy(y_hi[:, ds(2 * i + u, 1), :], yT[:, ds(2 * i + u, 1), :])\
                                .then_inc(y_hi_ready.sem, 1)
                        if todo and (kind == "V" or (kind == "T" and u == 0) or (kind == "S" and u < 2)):
                            e = todo.pop(0)
                            ne = (e % 4 + 1) * P
                            act.wait_ge(srow_ready.sem, srow_ready.at(L, "FQ", i, e + 1))
                            nc.scalar.activation(pr[:, e % 2, 0:ne], sc[:, e % 2, 0:ne], ACT.Exp,
                                                 bias=nmax[:, e:e + 1], accum_out=rsum[:, e:e + 1])\
                                .then_inc(prob_ready.sem, 1)
                    assert not todo
                values(L, "MV", 0)
                values(L, "MV", 1)
                merge_gates(L, "MB", 1)
                with act.Fori(0, 2) as i:
                    for s in range(4):
                        proj_wait(L, "MO", i, s)
                        nc.scalar.activation(og[:, 4 * i + s, :], bank[s][:, :], ACT.Tanh, scale=0.5)\
                            .then_inc(drained_sem[s], 1)
                with act.Fori(0, 4) as i:
                    for s in range(4):
                        proj_wait(L, "MQ", i, s)
                        nc.scalar.activation(qk[:, s, :], bank[s][:, :], ACT.Copy,
                                             scale=ML_D ** -0.5 if s % 2 == 1 else 1.0)\
                            .then_inc(drained_sem[s], 1)
                    for p in range(2):
                        n = 2 * p
                        act.wait_ge(filled[6].sem, filled[6].at(L, "MQ", i, n + 1))
                        nc.scalar.copy(gb, bank[6][:, :]).then_inc(drained_sem[6], 1)
                        act.wait_ge(filled[7].sem, filled[7].at(L, "MQ", i, n + 1))
                        act.wait_ge(ml_y.sem, ml_y.at(L, "MQ", i, p) - 1)
                        nc.scalar.activation(em[:, p, :], bank[7][:, :], ACT.Exp, scale=-1.0)\
                            .then_inc(drained_sem[7], 1)
                        act.wait_ge(drained_sem[6], drained[6].at(L, "MQ", i, n + 1))
                        act.wait_ge(gdm_ready.sem, gdm_ready.at(L, "MQ", i, p + 1))
                        for s in range(TT):
                            gs = gcol[:, s, ds(2 * i + p, 1)]
                            if s < TT - 1:
                                nc.scalar.activation(E[:, p, s, P:SEQ - s * P], gb[:, (s + 1) * P:], ACT.Exp,
                                                     scale=-1.0, bias=gs)
                            nc.scalar.activation(E[:, p, s, 0:P], gdm[:, s, :], ACT.Exp, scale=-1.0, bias=gs)\
                                .then_inc(dec_ready.sem, 1)
                    for p in range(2):
                        act.wait_ge(hc_ready.sem, hc_ready.at(L, "MQ", i, p + 1))
                        nc.scalar.activation(sq[:, p, :], hh[:, p, :], ACT.Square).then_inc(hsq_ready.sem, 1)
                        act.wait_ge(filled[7].sem, filled[7].at(L, "MQ", i, 5 + p))
                        nc.scalar.activation(em[:, p, :], bank[7][:, :], ACT.Sqrt, bias=eps_t[:, :])\
                            .then_inc(drained_sem[7], 1)
                    act.wait_ge(ml_y.sem, ml_y.at(L, "MQ", i, 2))
                    nc.scalar.copy(y_hi[:, ds(2 * i, 2), :], yT[:, ds(2 * i, 2), :]).then_inc(y_hi_ready.sem, 1)
                merge_gates(L, "MC", 2)
                evac_norm(L, "N2")
                with act.Fori(0, 4) as i:
                    for s in range(4):
                        proj_wait(L, "WQ", i, s)
                        nc.scalar.copy(qk[:, s, :], bank[s][:, :]).then_inc(drained_sem[s], 1)
                    for s in range(4):
                        act.wait_ge(filled[4 + s].sem, filled[4 + s].at(L, "WQ", i, 1))
                        if s == 0:
                            act.wait_ge(best_done.sem, best_done.at(L, "WQ", i, 0))
                        nc.scalar.copy(keys[:, 4 * s:4 * s + 4, :], bank[4 + s][:, :].rearrange("p (t n) -> p t n", t=TT))\
                            .then_inc(drained_sem[4 + s], 1)

                def soft(L, t):
                    act.wait_ge(wsm_in.sem, wsm_in.at(L, "T", t, 1))
                    nc.scalar.activation(wts, wts, ACT.Exp).then_inc(wsm_out.sem, 1)

                def gelu_tanh(L, t):
                    act.wait_ge(tanh_in.sem, tanh_in.at(L, "T", t, 1))
                    nc.scalar.activation(th, gin, ACT.Tanh).then_inc(tanh_out.sem, 1)

                soft(L, 0)
                with act.Fori(0, TT - 1) as t:
                    gelu_tanh(L, t)
                    soft(L, t + 1)
                gelu_tanh(L, TT - 1)
            act.wait_ge(ms_final, 1)
            nc.scalar.activation(stat[:, 2, :], stat[:, 1, :], ACT.Sqrt).then_inc(sd_final, 1)

        @block.vector
        def _(dve):
            V = nc.vector
            dve.sem_inc(proj_done, 4)
            for c in (layer_done, lru_done, ml_y, g_used, merged_ready, best_done):
                dve.sem_inc(c.sem, c.credit)
            V.memset(first_expert[:, :], 0.0).then_inc(final_step, 1)
            dve.wait_ge(final_step, 1)
            dve.wait_ge(x_loaded, 16)

            def stats(c):
                for t in range(TT):
                    c.step(V.scalar_tensor_tensor(out=hn[:, t, :], in0=x[:, t, :], scalar=1.0, in1=x[:, t, :],
                                                  op0=ALU.mult, op1=ALU.mult, accum_out=stat[:, 0, t:t + 1]))
                c.wait()
                return V.tensor_scalar(stat[:, 1, :], stat[:, 0, :], 1.0 / D, EPS, ALU.mult, ALU.add)

            def scale_rows(t, w):
                return V.scalar_tensor_tensor(out=hn[:, t, :], in0=x[:, t, :], scalar=stat[:, 3, t:t + 1], in1=w,
                                              op0=ALU.mult, op1=ALU.mult)

            def norm(L, ph, a):
                c = Chain(dve, dve_step, L, ph, 0)
                stats(c).then_inc(ms_ready.sem, 1)
                dve.wait_ge(sd_ready.sem, sd_ready.at(L, ph, 0, 1))
                c.step(V.reciprocal(stat[:, 3, :], stat[:, 2, :]))
                c.wait()
                dve.wait_ge(nw_loaded, 32 * L + 16 * (a + 1))
                for t in range(TT):
                    scale_rows(t, nwb[:, :]).then_inc(hn_ready.sem, 1)
                c.close()
                low = xl_peer if a else xl_mix
                for k in range(KC):
                    b = 4 + k % 4
                    dve.wait_ge(xh_ready.sem, xh_ready.at(L, ph, 0, k + 1))
                    V.tensor_tensor(low[:, :, k * P:(k + 1) * P], bank[b][:, :].rearrange("p (t n) -> p t n", t=TT),
                                    xT[:, k, :].bitcast(F32).rearrange("p (t n) -> p t n", t=TT), ALU.subtract)\
                        .then_inc(drained_sem[b], 1)

            def log1p(c, z, s, q, r):
                c.step(V.tensor_scalar(s, z, 2.0, None, ALU.add))
                c.wait()
                c.step(V.reciprocal(q, s))
                c.wait()
                c.step(V.tensor_tensor(s, z, q, ALU.mult))
                c.wait()
                c.step(V.tensor_tensor(q, s, s, ALU.mult))
                c.wait()
                c.step(V.tensor_scalar(r, q, 1.0 / 15, None, ALU.mult))
                c.wait()
                for k in (13, 11, 9, 7, 5, 3):
                    c.step(V.scalar_tensor_tensor(out=r, in0=r, scalar=1.0 / k, in1=q, op0=ALU.add, op1=ALU.mult))
                    c.wait()
                c.step(V.scalar_tensor_tensor(out=r, in0=r, scalar=1.0, in1=s, op0=ALU.add, op1=ALU.mult))
                c.wait()

            def merge(L, ph):
                with dve.Fori(0, 4) as i:
                    for j in range(2):
                        dve.wait_ge(proj_done, slots_done(L, ph, i, 2 * j + 1))
                        dve.wait_ge(drained_sem[2 * j + 1], rnd(L, ph, i) + 2)
                        dst = merged[:, 2 * i + j, :]
                        to = dst if ph == "MA" else mtmp
                        if ph != "MA":
                            dve.wait_ge(merged_ready.sem, merged_ready.at(L, ph, i, j))
                        V.scalar_tensor_tensor(out=to, in0=gt[j], scalar=1.0, in1=bank[2 * j][:, :],
                                               op0=ALU.add, op1=ALU.mult).then_inc(drained_sem[2 * j], 1)
                        if ph != "MA":
                            dve.wait_ge(drained_sem[2 * j], rnd(L, ph, i) + 2)
                            V.tensor_tensor(dst, dst, mtmp, ALU.add).then_inc(merged_ready.sem, 1)
                    if ph == "MC":
                        low_part(L, ph, i, m_lo, merged, m_hi, 1)

            def low_part(L, ph, i, lo, src, hi, n):
                dve.wait_ge(y_hi_ready.sem, y_hi_ready.at(L, ph, i, n))
                V.tensor_tensor(lo[:, ds(2 * i, 2), :], src[:, ds(2 * i, 2), :], hi[:, ds(2 * i, 2), :].bitcast(F32),
                                ALU.subtract).then_inc(y_lo_ready.sem, 1)

            with dve.Fori(0, DEPTH) as L:
                norm(L, "N1", 0)
                c = Chain(dve, dve_step, L, "P", 0)
                dve.wait_ge(params_ready, 16 * L + 16)
                lam = pcol("lam", 0, KC)
                c.step(V.tensor_scalar(hb[:, :], pcol("ba", 0, 5 * KC), 0.5, None, ALU.mult))
                c.step(V.tensor_scalar(hnw[:, :], pcol("nw", 0, KC), 0.5, None, ALU.mult))
                c.step(V.tensor_scalar(nsp[:, :], lam, -1.0, None, ALU.mult))
                c.wait()
                V.tensor_tensor(lp[:, 0, :], lam, nsp[:, :], ALU.min).then_inc(zexp_in.sem, 1)
                dve.wait_ge(zexp_out.sem, zexp_out.at(L, "P", 0, 1))
                log1p(c, lp[:, 0, :], lp[:, 1, :], lp[:, 2, :], lp[:, 0, :])
                c.step(V.tensor_scalar(nsp[:, :], nsp[:, :], 0.0, -4.0, ALU.max, ALU.mult))
                c.wait()
                c.step(V.scalar_tensor_tensor(out=nsp[:, :], in0=lp[:, 0, :], scalar=-8.0, in1=nsp[:, :],
                                              op0=ALU.mult, op1=ALU.add))
                c.close()
                c = Chain(dve, dve_step, L, "G", 0)
                dve.wait_ge(filled[4].sem, filled[4].at(L, "G", 0, 1))
                c.step(V.tensor_scalar(rows[:, 0, :], bank[4][0:NROW, :], pcol("fbias", 0)[0:NROW, :], None, ALU.add))
                c.wait()
                V.tensor_scalar(rows[0:ML_H, 5, :], bank[4][I_ROW:GATES, :], pcol("ibias", 0)[0:ML_H, :], None, ALU.add)\
                    .then_inc(drained_sem[4], 1)
                c.step(V.tensor_scalar(rows[:, 1, :], rows[:, 0, :], -1.0, None, ALU.mult))
                c.wait()
                V.tensor_tensor(rows[:, 1, :], rows[:, 1, :], rows[:, 0, :], ALU.min).then_inc(zexp_in.sem, 1)
                dve.wait_ge(zexp_out.sem, zexp_out.at(L, "G", 0, 1))
                log1p(c, rows[:, 1, :], rows[:, 2, :], rows[:, 3, :], rows[:, 4, :])
                c.step(V.tensor_scalar(rows[:, 0, :], rows[:, 0, :], 0.0, None, ALU.min))
                c.wait()
                c.step(V.scalar_tensor_tensor(out=rows[:, 0, :], in0=rows[:, 4, :], scalar=-2.0, in1=rows[:, 0, :],
                                              op0=ALU.mult, op1=ALU.add))
                c.wait()
                c.step(V.tensor_tensor_scan(cum[:, :], ones[0:NROW, 0:1].to_broadcast([NROW, SEQ]), rows[:, 0, :], 0.0, ALU.mult, ALU.add))
                c.wait()
                dve.wait_ge(drained_sem[4], drained[4].at(L, "G", 0, 1))
                c.step(V.tensor_tensor(g_row[:, :], rows[0:ML_H, 5, :], cum[0:ML_H, :], ALU.subtract))
                c.wait()
                c.step(V.tensor_tensor_scan(G_row[:, :], g_row[:, :], g_row[:, :], 0.0, ALU.max, ALU.max))
                c.wait()
                V.tensor_tensor(m_row[:, :], G_row[:, :], cum[0:ML_H, :], ALU.add).then_inc(rows_ready.sem, 1)
                c.close()
                V.memset(xpad[:, :, 0:CONV - 1], 0.0).then_inc(pad_ready, 1)
                dve.wait_ge(pad_ready, L + 1)
                stand(dve)
                with dve.Fori(0, 2) as i:
                    c = Chain(dve, dve_step, L, "LRU", i)
                    for k in range(CONV):
                        for s in range(4):
                            if k == 0:
                                dve.wait_ge(drained_sem[s], rnd(L, "LRU", i) + 2)
                            w = dcol(pv, 4 * i + (PV_COLS["conv_w"][0] + k * KC + s))
                            src = xpad[:, s, k:k + SEQ]
                            if k == 0:
                                c.step(V.tensor_scalar(xc[:, s, :], src, w, dcol(pv, 4 * i + (PV_COLS["conv_b"][0] + s)),
                                                       ALU.mult, ALU.add))
                            else:
                                ins = V.scalar_tensor_tensor(out=xc[:, s, :], in0=src, scalar=w, in1=xc[:, s, :],
                                                             op0=ALU.mult, op1=ALU.add)
                                if k == CONV - 1:
                                    ins.then_inc(conv_done.sem, 1)
                                else:
                                    c.step(ins)
                        if k < CONV - 1:
                            c.wait()
                    for s in range(4):
                        b = 4 + 2 * (s % 2)
                        dve.wait_ge(drained_sem[b], drained[b].at(L, "LRU", i, s // 2 + 1))
                        ins = V.tensor_scalar(R[:, s, :], R[:, s, :], 1.0, dcol(nsp, 4 * i + s), ALU.add, ALU.mult)
                        if s < 3:
                            c.step(ins)
                        else:
                            ins.then_inc(la_ready.sem, 1)
                    dve.wait_ge(drained_sem[5], drained[5].at(L, "LRU", i, 2))
                    dve.wait_ge(drained_sem[7], drained[7].at(L, "LRU", i, 2))
                    dve.wait_ge(conv_done.sem, conv_done.at(L, "LRU", i, 4))
                    c.step(V.scalar_tensor_tensor(out=TI, in0=TI, scalar=1.0, in1=xc, op0=ALU.add, op1=ALU.mult))
                    dve.wait_ge(ea_ready.sem, ea_ready.at(L, "LRU", i, 2))
                    c.step(V.tensor_tensor(R, A, A, ALU.mult))
                    c.wait()
                    V.scalar_tensor_tensor(out=TH[:, :, :], in0=R, scalar=1.0, in1=TH[:, :, :], op0=ALU.add, op1=ALU.mult)\
                        .then_inc(q_ready.sem, 1)
                    dve.wait_ge(sq_ready.sem, sq_ready.at(L, "LRU", i, 1))
                    c.step(V.tensor_tensor(TI, TI, TH[:, :, :], ALU.mult))
                    c.wait()
                    for s in range(4):
                        ins = V.tensor_tensor_scan(yT[:, 4 * i + s, :], A[:, s, :], TI[:, s, :], 0.0, ALU.mult, ALU.add)
                        if s < 3:
                            c.step(ins)
                        else:
                            ins.then_inc(lru_done.sem, 1)
                    c.close()
                dve.wait_ge(y_hi_ready.sem, y_hi_ready.at(L, "LRU", 1, 1))
                V.tensor_tensor(y_lo[:, :, :], yT, y_hi_lru[:, :, :].bitcast(F32), ALU.subtract).then_inc(y_lo_ready.sem, 1)
                merge(L, "MA")
                with dve.Fori(0, 4) as i:
                    c = Chain(dve, dve_step, L, "FQ", i)
                    cn = 0
                    n7 = {}
                    count = 0
                    for kind, u in fox_steps():
                        if kind in "CVY":
                            count += 1
                            n7[kind, u] = count
                    for u in range(17):
                        if u < 16:
                            t, h = u % 4, u // 4
                            b, n = 4 + u % 2, (u % 4 + 1) * P
                            if t == 0:
                                dve.wait_ge(drained_sem[7], drained[7].at(L, "FQ", i, n7["C", h]))
                                if u == 0:
                                    dve.wait_ge(drained_sem[6], drained[6].at(L, "COLS", 0, 1))
                            dve.wait_ge(filled[b].sem, filled[b].at(L, "FQ", i, u // 2 + 1))
                            dve.wait_ge(prob_ready.sem, prob_ready.at(L, "FQ", i, u) - 1)
                            V.scalar_tensor_tensor(out=sc[:, u % 2, 0:n], in0=bank[b][:, 0:n],
                                                   scalar=cumc[:, t, ds(4 * i + (ML_H + h), 1)],
                                                   in1=cb[:, h % 2, 0:n], op0=ALU.add, op1=ALU.subtract)\
                                .then_inc(drained_sem[b], 1)
                            dve.wait_ge(drained_sem[b], drained[b].at(L, "FQ", i, u // 2 + 1))
                            diag = sc[:, u % 2, n - P:n]
                            c.step(V.tensor_tensor(diag, diag, mask_q[:, :], ALU.add))
                            c.wait()
                            V.tensor_reduce(nmax[:, u:u + 1], sc[:, u % 2, 0:n], AX.X, ALU.max, negate=True)\
                                .then_inc(srow_ready.sem, 1)
                        if u >= 1:
                            dve.wait_ge(prob_ready.sem, prob_ready.at(L, "FQ", i, u))
                            V.reciprocal(rinv[:, u - 1:u], rsum[:, u - 1:u]).then_inc(rinv_ready.sem, 1)
                    low_part(L, "FQ", i, y_lo, yT, y_hi, 2)
                    c.close()
                merge(L, "MB")
                stand(dve)
                with dve.Fori(0, 2) as i:
                    for s in range(4):
                        dve.wait_ge(drained_sem[s], rnd(L, "MO", i) + 2)
                        V.tensor_scalar(og[:, 4 * i + s, :], og[:, 4 * i + s, :], 1.0, dcol(hnw, 4 * i + s),
                                        ALU.add, ALU.mult).then_inc(og_done.sem, 1)
                with dve.Fori(0, 4) as i:
                    c = Chain(dve, dve_step, L, "MQ", i)

                    def decay_mask(p):
                        dve.wait_ge(drained_sem[6], drained[6].at(L, "MQ", i, 2 * p + 1))
                        V.tensor_tensor(gdm, gb.rearrange("p (s n) -> p s n", s=4),
                                        mask_k[:, :].unsqueeze(1).to_broadcast([P, 4, P]), ALU.add)\
                            .then_inc(gdm_ready.sem, 1)

                    def weigh(p):
                        for s in range(TT):
                            b = 4 + s % 2
                            n = SEQ - s * P
                            dve.wait_ge(filled[b].sem, filled[b].at(L, "MQ", i, 2 * p + s // 2 + 1))
                            dve.wait_ge(dec_ready.sem, dec_ready.at(L, "MQ", i, 4 * p + s + 1))
                            V.tensor_tensor(E[:, p, s, 0:n], bank[b][:, 0:n], E[:, p, s, 0:n], ALU.mult)\
                                .then_inc(drained_sem[b], 1)
                            dve.wait_ge(drained_sem[b], drained[b].at(L, "MQ", i, 2 * p + s // 2 + 1))
                            dve.sem_inc(wts_ready.sem, 1)

                    def hidden(p):
                        n = 4 if p else 2
                        n6 = 5 if p else 2
                        n7 = 4 if p else 2
                        dve.wait_ge(drained_sem[7], drained[7].at(L, "MQ", i, 2 * p + 1))
                        dve.wait_ge(filled[7].sem, filled[7].at(L, "MQ", i, n7))
                        c.step(V.tensor_tensor(em[:, p, :], bank[7][:, :], em[:, p, :], ALU.max))
                        c.wait()
                        V.scalar_tensor_tensor(out=em[:, p, :], in0=bank[7][:, :], scalar=-1.0, in1=em[:, p, :],
                                               op0=ALU.mult, op1=ALU.max).then_inc(drained_sem[7], 1)
                        dve.wait_ge(drained_sem[7], drained[7].at(L, "MQ", i, n7))
                        c.step(V.reciprocal(em[:, p, :], em[:, p, :]))
                        c.wait()
                        dve.wait_ge(filled[6].sem, filled[6].at(L, "MQ", i, n6))
                        V.tensor_tensor(hh[:, p, :], bank[6][:, :], em[:, p, :], ALU.mult).then_inc(drained_sem[6], 1)
                        dve.wait_ge(drained_sem[6], drained[6].at(L, "MQ", i, n6))
                        dve.sem_inc(h_ready.sem, 1)

                    def centre(p):
                        n6 = 6 if p else 4
                        dve.wait_ge(filled[6].sem, filled[6].at(L, "MQ", i, n6))
                        V.tensor_tensor(hh[:, p, :], hh[:, p, :], bank[6][:, :], ALU.subtract)\
                            .then_inc(drained_sem[6], 1)
                        dve.wait_ge(drained_sem[6], drained[6].at(L, "MQ", i, n6))
                        dve.sem_inc(hc_ready.sem, 1)

                    decay_mask(0)
                    weigh(0)
                    hidden(0)
                    decay_mask(1)
                    weigh(1)
                    centre(0)
                    hidden(1)
                    centre(1)
                    for p in range(2):
                        dve.wait_ge(drained_sem[7], drained[7].at(L, "MQ", i, 5 + p))
                        c.step(V.reciprocal(em[:, p, :], em[:, p, :]))
                        c.wait()
                        c.step(V.tensor_tensor(hh[:, p, :], hh[:, p, :], em[:, p, :], ALU.mult))
                        c.wait()
                        V.tensor_tensor(yT[:, 2 * i + p, :], hh[:, p, :], og[:, 2 * i + p, :], ALU.mult)\
                            .then_inc(ml_y.sem, 1)
                    low_part(L, "MQ", i, y_lo, yT, y_hi, 1)
                    c.close()
                merge(L, "MC")
                with dve.Fori(0, 2) as i:
                    dve.wait_ge(proj_done, slots_done(L, "OUT", i, 4))
                    for t in range(TT):
                        xs = x[:, t, ds(SEQ * i, SEQ)]
                        V.scalar_tensor_tensor(out=xs, in0=bank[t][:, :], scalar=0.5, in1=xs, op0=ALU.mult, op1=ALU.add)\
                            .then_inc(drained_sem[t], 1)
                for t in range(TT):
                    dve.wait_ge(drained_sem[t], drained[t].at(L, "OUT", 1, 1))
                norm(L, "N2", 1)

                def top16(c, src, val, idx, groups):
                    def step(what):
                        for g in range(groups):
                            c.step(what(g))
                        c.wait()
                        stand(dve)
                    yield step(lambda g: V.max(val[:, g, 0:8], src[:, g, :]))
                    yield step(lambda g: V.max_index(idx[:, g, 0:8], val[:, g, 0:8], src[:, g, :]))
                    yield step(lambda g: V.match_replace(src[:, g, :], val[:, g, 0:8], src[:, g, :], NEG * 1e8))
                    yield step(lambda g: V.max(val[:, g, 8:16], src[:, g, :]))
                    yield step(lambda g: V.max_index(idx[:, g, 8:16], val[:, g, 8:16], src[:, g, :]))

                with dve.Fori(0, 4) as i:
                    c = Chain(dve, dve_step, L, "WQ", i)
                    for s in range(4):
                        dve.wait_ge(drained_sem[4 + s], drained[4 + s].at(L, "WQ", i, 1))
                    stand(dve)
                    for _ in top16(c, keys, kval, kidx, 16):
                        pass
                    c.step(V.tensor_copy(vals[:, :, ds(4 * i, 4), :], kval.rearrange("p (s t) n -> p t s n", t=TT)))
                    V.tensor_copy(idxf[:, :, ds(4 * i, 4), :], kidx.rearrange("p (s t) n -> p t s n", t=TT))\
                        .then_inc(best_done.sem, 1)
                    dve.wait_ge(best_done.sem, best_done.at(L, "WQ", i, 1))
                    c.close()
                    stand(dve)

                w3 = wts.rearrange("p (h n) -> p h n", h=PEER_H)
                full = [P, PEER_H, TOPK, TOPK]
                small = [P, PEER_H, TOPK]

                def choose(t):
                    c = Chain(dve, choose_step, L, "T", t)
                    v4 = vals[:, t, :, :].rearrange("p (h a) n -> p h a n", a=2)
                    i4 = idxf[:, t, :, :].rearrange("p (h a) n -> p h a n", a=2)
                    c.step(V.tensor_tensor(cand.rearrange("p h (a b) -> p h a b", a=TOPK),
                                           v4[:, :, 0, :].unsqueeze(3).to_broadcast(full),
                                           v4[:, :, 1, :].unsqueeze(2).to_broadcast(full), ALU.add))
                    c.wait()
                    stand(dve)
                    yield
                    yield from top16(c, cand, tv, posu.rearrange("p (h n) -> p h n", h=PEER_H), PEER_H)
                    c.step(V.tensor_scalar(posu2[:, 0, :], posu, 4, None, ALU.logical_shift_right))
                    c.step(V.tensor_scalar(posu2[:, 1, :], posu, 15, None, ALU.bitwise_and))
                    c.wait()
                    c.step(V.tensor_copy(posa, posu2[:, 0, :]))
                    c.step(V.tensor_copy(posb, posu2[:, 1, :]))
                    c.wait()
                    yield
                    for half, (pos, e) in enumerate(((posa, e1), (posb, e2))):
                        eq3 = eqb.rearrange("p (k n) -> p k n", n=TOPK)
                        c.step(V.tensor_tensor(eq3, pos.unsqueeze(2).to_broadcast([P, SLOTS, TOPK]),
                                               iota_f[:, :].unsqueeze(1).to_broadcast([P, SLOTS, TOPK]), ALU.is_equal))
                        c.wait()
                        yield
                        eq4 = eqb.rearrange("p (h k n) -> p h k n", h=PEER_H, n=TOPK)
                        c.step(V.tensor_tensor(eq4, eq4, i4[:, :, half, :].unsqueeze(2).to_broadcast(full), ALU.mult))
                        c.wait()
                        yield
                        c.step(V.tensor_reduce(e, eq3, AX.X, ALU.add))
                        c.wait()
                        yield
                    c.step(V.tensor_scalar(e2, e2, first_expert[:, :], None, ALU.add))
                    V.tensor_tensor(w3, tv, tv[:, :, 0:1].to_broadcast(small), ALU.subtract).then_inc(wsm_in.sem, 1)
                    c.wait()
                    V.scalar_tensor_tensor(out=eidx[:, t, :], in0=e1, scalar=float(N_KEYS), in1=e2,
                                           op0=ALU.mult, op1=ALU.add).then_inc(eidx_ready.sem, 1)
                    yield
                    dve.wait_ge(wsm_out.sem, wsm_out.at(L, "T", t, 1))
                    c.step(V.tensor_reduce(ssum, w3, AX.X, ALU.add))
                    c.wait()
                    c.step(V.reciprocal(ssum, ssum))
                    c.wait()
                    c.step(V.tensor_tensor(w3, w3, ssum.unsqueeze(2).to_broadcast(small), ALU.mult))
                    c.wait()
                    c.close()

                def tile(t, last):
                    pieces = iter(()) if last else choose(t + 1)
                    STRETCH = 2
                    turns = 2 * SLOTS // GR
                    for j0 in range(0, turns, STRETCH):
                        values = j0 >= turns // 2
                        if j0 == turns // 2:
                            dve.wait_ge(g_used.sem, g_used.at(L, "T", t, SLOTS))
                            c = Chain(dve, gelu_step, L, "T", t)
                            c.step(V.tensor_tensor(gin, actv, actv, ALU.mult))
                            c.wait()
                            c.step(V.tensor_scalar(gin, gin, 0.044715, 1.0, ALU.mult, ALU.add))
                            c.wait()
                            V.scalar_tensor_tensor(out=gin, in0=gin, scalar=0.7978845608028654, in1=actv,
                                                   op0=ALU.mult, op1=ALU.mult).then_inc(tanh_in.sem, 1)
                            c.step(V.scalar_tensor_tensor(out=coef, in0=actv, scalar=0.5, in1=wts, op0=ALU.mult, op1=ALU.mult))
                            c.wait()
                            dve.wait_ge(tanh_out.sem, tanh_out.at(L, "T", t, 1))
                            c.step(V.scalar_tensor_tensor(out=coef, in0=th, scalar=1.0, in1=coef, op0=ALU.add, op1=ALU.mult))
                            c.wait()
                            c.close()
                        stand(dve)
                        with dve.Fori(j0, j0 + STRETCH) as j:
                            for q in range(GR):
                                dve.wait_ge(g_ready[q], 16 * ((L * TT + t) * turns + j + 1))
                                if values:
                                    dve.wait_ge(g_used.sem, g_used.at(L, "T", t, q) + GR * j)
                                    V.scalar_tensor_tensor(out=x[:, t, :], in0=gring[:, q, :],
                                                           scalar=coef[:, ds(GR * j + (q - SLOTS), 1)],
                                                           in1=x[:, t, :], op0=ALU.mult, op1=ALU.add)\
                                        .then_inc(g_used.sem, 1)
                                else:
                                    V.scalar_tensor_tensor(out=gring[:, q, :], in0=gring[:, q, :], scalar=1.0,
                                                           in1=hn[:, t, :], op0=ALU.mult, op1=ALU.mult,
                                                           accum_out=actv[:, ds(GR * j + q, 1)]).then_inc(g_used.sem, 1)
                        next(pieces, None)
                    assert next(pieces, "end") == "end"

                for _ in choose(0):
                    pass
                stand(dve)
                with dve.Fori(0, TT - 1) as t:
                    tile(t, False)
                tile(TT - 1, True)
                dve.wait_ge(g_used.sem, g_used.at(L, "T", TT - 1, 2 * SLOTS))
                V.tensor_scalar(first_expert[:, :], first_expert[:, :], float(N_KEYS * N_KEYS), None, ALU.add)\
                    .then_inc(layer_done.sem, 1)

            for t in range(TT):
                V.scalar_tensor_tensor(out=hn[:, t, :], in0=x[:, t, :], scalar=1.0, in1=x[:, t, :],
                                       op0=ALU.mult, op1=ALU.mult, accum_out=stat[:, 0, t:t + 1]).then_inc(final_step, 1)
            dve.wait_ge(final_step, TT + 1)
            V.tensor_scalar(stat[:, 1, :], stat[:, 0, :], 1.0 / D, EPS, ALU.mult, ALU.add).then_inc(ms_final, 1)
            dve.wait_ge(sd_final, 1)
            V.reciprocal(stat[:, 3, :], stat[:, 2, :]).then_inc(final_step, 1)
            dve.wait_ge(final_step, TT + 2)
            dve.wait_ge(fnw_loaded, 16)
            for t in range(TT):
                scale_rows(t, nwb[:, :]).then_inc(out_ready, 1)


def _rows_of(w, c0, n=P):
    return w[:, c0:c0 + n].reshape(KC, P, n).transpose(1, 0, 2).reshape(P, KC * n)


def _token_chunks(w, c0):
    return [w[2 * P * s:2 * P * (s + 1), c0:c0 + SEQ].reshape(2, P, SEQ).transpose(1, 0, 2).reshape(P, 2 * SEQ)
            for s in range(4)]


def _stream(w_in, w_lru, w_fox, w_ml, w_out, wq):
    chunks = []
    for i in range(2):
        chunks += [_rows_of(w_in, C_LRU + (4 * i + s) * P) for s in range(4)]
    for i in range(2):
        chunks += _token_chunks(w_in, C_FOX + 2 * D + i * SEQ)

    def merge(w, b):
        for j in range(KC):
            chunks.append(_rows_of(w, j * P))
            chunks.append(_rows_of(w_in, C_GATE + b * D + j * P))

    def pairs(c0):
        for j in range(KC):
            chunks.append(_rows_of(w_in, c0 + j * P))
            chunks.append(_rows_of(w_in, c0 + D + j * P))

    merge(w_lru, 0)
    pairs(C_FOX)
    for i in range(2):
        chunks += _token_chunks(w_in, C_ML + 2 * D + i * SEQ)
    merge(w_fox, 1)
    for j in range(KC):
        chunks.append(_rows_of(w_in, C_O + j * P))
    pairs(C_ML)
    merge(w_ml, 2)
    for i in range(2):
        chunks += _token_chunks(w_out, i * SEQ)
    for j in range(2 * KC):
        chunks.append(_rows_of(wq, j * P))
    return chunks


def kernel(x, norm1_w, w_in, lru_conv_w, lru_conv_b, lru_wa, lru_ba, lru_wx, lru_bx, lru_lambda,
           fox_fgate_b, mlstm_igate_b, mlstm_fgate_b, mlstm_norm_w, merge_gate_b,
           w_br_lru, w_br_fox, w_br_mlstm, w_out, norm2_w,
           peer_wq, peer_subkeys1, peer_subkeys2, peer_u, peer_v, final_norm_w):
    import concourse.bacc as bacc
    from concourse.bass_utils import run_bass_kernel_spmd as run

    def column(v):
        return np.asarray(v).reshape(-1, P).T

    def column_of(v, n):
        c = np.zeros((P, 1), np.float32)
        c[0:n, 0] = v
        return c

    stream, pvs, lru = [], [], []
    for L in range(DEPTH):
        w = np.asarray(w_in[L])
        stream += _stream(w, np.asarray(w_br_lru[L]), np.asarray(w_br_fox[L]), np.asarray(w_br_mlstm[L]),
                          np.asarray(w_out[L]), np.asarray(peer_wq[L]))
        wgate = np.concatenate([w[:, C_MLF:C_MLF + ML_H], w[:, C_FOXF:C_FOXF + FOX_H],
                                np.zeros((D, I_ROW - NROW), np.float32), w[:, C_MLI:C_MLI + ML_H]], axis=1)
        fb = np.concatenate([np.asarray(mlstm_fgate_b[L]), np.asarray(fox_fgate_b[L])])
        pvs.append(np.concatenate([
            column(lru_conv_w[L]), column(lru_conv_b[L]), column(lru_ba[L]), column(lru_bx[L]),
            column(merge_gate_b[L]), column(lru_lambda[L]), column(mlstm_norm_w[L]),
            column_of(fb, NROW), column_of(np.asarray(mlstm_igate_b[L]), ML_H),
            np.asarray(peer_subkeys1[L]).T, np.asarray(peer_subkeys2[L]).T, _rows_of(wgate, 0, GATES)], axis=1))
        both = np.stack([np.asarray(lru_wa[L]), np.asarray(lru_wx[L])], axis=1)
        lru.append(both.reshape(2, 4, 2, P, P).transpose(0, 3, 1, 2, 4).reshape(2, P, D))
    arrays = {
        "x_in": np.ascontiguousarray(np.asarray(x)[0]),
        "w_stream": np.stack(stream),
        "w_lru": np.concatenate(lru),
        "pvec": np.stack(pvs),
        "nrows": np.stack([np.asarray(a) for L in range(DEPTH) for a in (norm1_w[L], norm2_w[L])]),
        "fnorm": np.asarray(final_norm_w),
        "u_tab": np.asarray(peer_u).reshape(-1, D),
        "v_tab": np.asarray(peer_v).reshape(-1, D),
    }
    nc = bacc.Bacc("TRN2", target_bir_lowering=False, num_devices=1)
    args = [nc.dram_tensor(n, a.shape, mybir.dt.from_np(a.dtype), kind="ExternalInput").ap() for n, a in arrays.items()]
    out = nc.dram_tensor("out", (SEQ, D), F32, kind="ExternalOutput").ap()
    build(nc, *args, out)
    r = run(nc, [arrays], core_ids=[0])
    return r.results[0]["out"].reshape(1, SEQ, D)
```

```python
from contextlib import ExitStack
from itertools import chain

import concourse.bass as bass
from concourse import mybir
import numpy as np

F32 = mybir.dt.float32
F32R = mybir.dt.float32r
I32 = mybir.dt.int32
U32 = mybir.dt.uint32
ALU = mybir.AluOpType
ACT = mybir.ActivationFunctionType
AX = mybir.AxisListType
ds = bass.ds

P = 128
SEQ = 512
D = 1024
DEPTH = 2
TT = SEQ // P
KC = D // P
EPS = 1e-6
FOX_H, FOX_D = 16, 64
ML_H, ML_D = 8, 128
CONV = 4
TOPK = 16
N_KEYS = 128
PEER_H = 8
SLOTS = PEER_H * TOPK
GR = 8
NEG = -1e30

C_LRU, C_FOX, C_FOXF = 0, D, D + 3 * D
C_ML = C_FOXF + FOX_H
C_MLI = C_ML + 3 * D
C_MLF = C_MLI + ML_H
C_O = C_MLF + ML_H
C_GATE = C_O + D
NROW = ML_H + FOX_H
I_ROW = 32
GATES = I_ROW + ML_H

ROUNDS = dict(LRU=2, FV=2, MA=4, FQ=4, MV=2, MB=4, MO=2, MQ=4, MC=4, OUT=2, WQ=4)
NROUND = sum(ROUNDS.values())
ROUND0 = {p: sum(list(ROUNDS.values())[:n]) for n, p in enumerate(ROUNDS)}

PV_COLS = {}
_at = 0
for _n, _w in (("conv_w", CONV * KC), ("conv_b", KC), ("ba", KC), ("bx", KC), ("gate_b", 3 * KC),
               ("lam", KC), ("nw", KC), ("fbias", 1), ("ibias", 1), ("sub", 2 * P), ("wgate", KC * GATES)):
    PV_COLS[_n] = (_at, _at + _w)
    _at += _w
PV = _at
PV_KEPT = PV_COLS["wgate"][0]


class Count:

    def __init__(self, sem, plan, credit=0):
        self.sem, self.plan, self.credit, self.start = sem, plan, credit, {}
        n = 0
        for phase, (iters, per) in plan.items():
            self.start[phase] = n
            n += iters * per
        self.total = n

    def at(self, L, phase, i, n):
        return L * self.total + i * self.plan[phase][1] + (self.start[phase] + n + self.credit)


class Chain:

    def __init__(self, eng, count, L, phase, i):
        self.eng, self.count, self.where, self.n = eng, count, (L, phase, i), 0

    def step(self, ins):
        ins.then_inc(self.count.sem, 1)
        self.n += 1

    def wait(self):
        self.eng.wait_ge(self.count.sem, self.count.at(*self.where, self.n))

    def close(self):
        want = self.count.plan[self.where[1]][1]
        assert self.n == want, f"{self.where[1]}: {self.n} steps, {want} planned"


def fox_steps():
    seq = [("C", 0)]
    for k in range(16 + 3):
        if k < 16:
            seq.append(("S", k))
        if k % 4 == 2 and k < 13:
            seq.append(("C", k // 4 + 1))
        if 2 <= k < 18:
            seq.append(("T", k - 2))
        if k >= 3:
            seq.append(("V", k - 3))
            if (k - 3) % 8 == 7:
                seq.append(("Y", (k - 3) // 8))
    return seq


def build(nc, x_in, w_stream, w_lru, pvec, nrows, fnorm, u_tab, v_tab, out):
    with ExitStack() as ctx:
        def sb(name, shape, dt=F32):
            return ctx.enter_context(nc.sbuf_tensor(name, shape, dt))

        def sem(name):
            return ctx.enter_context(nc.semaphore(name))

        bank = [ctx.enter_context(nc.psum_tensor(f"bank{b}", [P, SEQ], F32)) for b in range(8)]

        vg_at = -(-nc.sbuf_base // 32) * 32
        vg = sb("vg", [P, 2 * KC, SEQ])
        hn_at = nc.sbuf_base
        hn = sb("hn", [P, TT, D])
        big_at = nc.sbuf_base
        big = sb("big", [P, 2 * KC, SEQ])
        att_at = nc.sbuf_base
        att = sb("att", [P, 8192])
        xl_mix = nc.alloc_sbuf_tensor_at("xl_mix", [P, TT, D], F32R, offset=hn_at)
        xl_peer = nc.alloc_sbuf_tensor_at("xl_peer", [P, TT, D], F32R, offset=vg_at)
        x = sb("x", [P, TT, D])
        y_hi_lru = nc.alloc_sbuf_tensor_at("y_hi_lru", [P, KC, SEQ], F32R, offset=att_at)
        y_hi = nc.alloc_sbuf_tensor_at("y_hi", [P, KC, SEQ], F32R, offset=vg_at + 4 * KC * SEQ)
        y_lo = nc.alloc_sbuf_tensor_at("y_lo", [P, KC, SEQ], F32R, offset=big_at)
        m_hi = nc.alloc_sbuf_tensor_at("m_hi", [P, KC, SEQ], F32R, offset=vg_at)
        m_lo = nc.alloc_sbuf_tensor_at("m_lo", [P, KC, SEQ], F32R, offset=big_at + 4 * KC * SEQ)
        xT = sb("xT", [P, KC, SEQ], F32R)
        w_hi = [sb(f"w_hi{b}", [P, D], F32R) for b in range(2)]
        w_lo = [sb(f"w_lo{b}", [P, D], F32R) for b in range(2)]
        ring = [sb(f"ring{s}", [P, D]) for s in range(4)]
        pv = sb("pv", [P, PV_KEPT])
        nwb = sb("nwb", [P, D])
        yT = big[:, 0:KC, :]
        merged = big[:, KC:2 * KC, :]
        bflat = big[:, :, :].rearrange("p a n -> p (a n)")
        v_sb = vg[:, 0:KC, :].rearrange("p (t a) c -> p t (a c)", t=TT)
        og = vg[:, KC:2 * KC, :]
        gring = vg[:, :, :].rearrange("p (r a) c -> p r (a c)", r=GR)
        qk = sb("qk", [P, 4, SEQ])
        ident = sb("ident", [P, P])
        ones = sb("ones", [P, P])
        head_hot = sb("head_hot", [64 + ML_H, ML_H])
        inv = sb("inv", [P, P])
        mask_q = sb("mask_q", [P, P])
        mask_k = sb("mask_k", [P, P])
        iota_i = sb("iota_i", [P, TOPK], I32)
        iota_f = sb("iota_f", [P, TOPK])
        stat = sb("stat", [P, 4, TT])
        hb = sb("hb", [P, 5 * KC])
        nsp = sb("nsp", [P, KC])
        hnw = sb("hnw", [P, KC])
        lp = sb("lp", [P, 3, KC])
        first_expert = sb("first_expert", [P, 1])
        rows = og[0:NROW, 0:6, :]
        cum = vg[0:NROW, 0, :]
        g_row = vg[0:ML_H, 1, :]
        G_row = vg[0:ML_H, 2, :]
        m_row = vg[0:ML_H, 3, :]
        G_AT, M_AT = 32, 64
        row_parts = sb("row_parts", [M_AT + ML_H, 2, SEQ], F32R)
        cumc = sb("cumc", [P, TT, NROW])
        gcol = sb("gcol", [P, TT, ML_H])
        sel = sb("sel", [M_AT + ML_H, 4, P], F32R)
        vst = sb("vst", [P, TT, 2, P])
        lruw = att[:, 6656:6656 + 8 * P].rearrange("p (s g n) -> p s g n", s=4, g=2)
        wgate = att[:, 7680:7680 + KC * GATES]
        NPAD = SEQ + CONV - 1
        xpad = att[:, 2536:2536 + KC * NPAD].rearrange("p (s n) -> p s n", s=KC)
        gt = [att[:, 4096 + j * SEQ:4096 + (j + 1) * SEQ] for j in range(2)]
        mtmp = att[:, 7168:7168 + SEQ]

        xc = merged[:, 0:4, :]
        R = merged[:, 4:8, :]
        TI = og[:, 0:4, :]
        A = og[:, 4:8, :]
        TH = qk
        sc = att[:, 0:1024].rearrange("p (a n) -> p a n", a=2)
        pr = att[:, 1024:2048].rearrange("p (a n) -> p a n", a=2)
        pT = att[:, 2048:3072].rearrange("p (a n) -> p a n", a=2)
        cb = att[:, 3072:4096].rearrange("p (a n) -> p a n", a=2)
        ytok = att[:, 4096:4608].rearrange("p (t n) -> p t n", t=TT)
        nmax = att[:, 4608:4624]
        rsum = att[:, 4624:4640]
        rinv = att[:, 4640:4656]
        E = att[:, 0:4096].rearrange("p (a s n) -> p a s n", a=2, s=4)
        gb = att[:, 4096:4608]
        gdm = att[:, 4608:5120].rearrange("p (s n) -> p s n", s=4)
        em = att[:, 5120:6144].rearrange("p (a n) -> p a n", a=2)
        hh = att[:, 6144:7168].rearrange("p (a n) -> p a n", a=2)
        sq = att[:, 7168:8192].rearrange("p (a n) -> p a n", a=2)
        keys = bflat[:, 0:2048].rearrange("p (g n) -> p g n", g=16)
        kval = bflat[:, 2048:2304].rearrange("p (g n) -> p g n", g=16)
        vals = bflat[:, 2304:3328].rearrange("p (t a n) -> p t a n", t=TT, n=TOPK)
        idxf = bflat[:, 3328:4352].rearrange("p (t a n) -> p t a n", t=TT, n=TOPK)
        kidx = bflat[:, 4352:4608].bitcast(U32).rearrange("p (g n) -> p g n", g=16)
        cand = att[:, 0:2048].rearrange("p (h n) -> p h n", h=PEER_H)
        eqb = att[:, 2048:4096]
        tv = att[:, 4608:4736].rearrange("p (h n) -> p h n", h=PEER_H)
        posa = att[:, 4736:4864]
        posb = att[:, 4864:4992]
        e1 = att[:, 4992:5120]
        e2 = att[:, 5120:5248]
        wts = att[:, 5248:5376]
        actv = att[:, 5376:5504]
        th = att[:, 5504:5632]
        gin = att[:, 5632:5760]
        coef = att[:, 5760:5888]
        ssum = att[:, 5888:5896]
        posu = att[:, 6144:6272].bitcast(U32)
        posu2 = att[:, 6272:6528].bitcast(U32).rearrange("p (a n) -> p a n", a=2)
        eidx = bflat[:, 4608:5120].bitcast(U32).rearrange("p (t n) -> p t n", t=TT)
        estage = [sb(f"estage{h}", [P, GR], U32) for h in range(2)]

        def pcol(name, a, b=None):
            c0 = PV_COLS[name][0]
            return pv[:, c0 + a:c0 + (a + 1 if b is None else b)]

        def dcol(buf, at):
            return buf[:, ds(at, 1)]

        subk = pcol("sub", 0, 2 * P).rearrange("p (a n) -> p a n", a=2)

        x_loaded = sem("x_loaded")
        fnw_loaded = sem("fnw_loaded")
        consts_ready = sem("consts_ready")
        pool_step = sem("pool_step")
        params_ready = sem("params_ready")
        wgate_ready = sem("wgate_ready")
        nw_loaded = sem("nw_loaded")
        lruw_ready = sem("lruw_ready")
        w_ready = [sem(f"w_ready{s}") for s in range(4)]
        proj_done = sem("proj_done")
        g_ready = [sem(f"g_ready{q}") for q in range(GR)]
        out_done = sem("out_done")
        out_ready = sem("out_ready")
        pool_stage = sem("pool_stage")
        waits_taken = sem("waits_taken")
        pad_ready = sem("pad_ready")
        ms_final = sem("ms_final")
        sd_final = sem("sd_final")
        final_step = sem("final_step")
        drained_sem = [sem(f"drained{b}") for b in range(8)]
        drained = [Count(drained_sem[s], {p: (n, 1) for p, n in ROUNDS.items()}, 1) for s in range(4)]
        work = [dict(N1=(1, 2), G=(1, int(b == 0)), LRU=(2, 2), COLS=(1, int(b >= 2)),
                     FQ=(4, (8, 8, 16, 22)[b]), MQ=(4, (4, 4, 6, 6)[b]), N2=(1, 2), WQ=(4, 1))
                for b in range(4)]
        drained += [Count(drained_sem[4 + b], work[b], 1) for b in range(4)]
        filled = {4 + b: Count(sem(f"filled{4 + b}"), work[b]) for b in range(4)}
        one = lambda *names: {n: (1, 1) for n in names}
        layer_done = Count(sem("layer_done"), one("L"), 1)
        ms_ready = Count(sem("ms_ready"), one("N1", "N2"))
        sd_ready = Count(sem("sd_ready"), one("N1", "N2"))
        xh_ready = Count(sem("xh_ready"), dict(N1=(1, KC), N2=(1, KC)))
        split = dict(G=(1, 1), **{p: (n, 4) for p, n in ROUNDS.items()})
        hi_done = Count(sem("hi_done"), split)
        split_ready = Count(sem("split_ready"), split)
        y_hi_ready = Count(sem("y_hi_ready"), dict(LRU=(2, 1), FQ=(4, 2), MQ=(4, 1), MC=(4, 1)))
        y_lo_ready = Count(sem("y_lo_ready"), dict(LRU=(1, 1), FQ=(4, 1), MQ=(4, 1), MC=(4, 1)))
        hn_ready = Count(sem("hn_ready"), dict(N1=(1, TT), N2=(1, TT)))
        zexp_in = Count(sem("zexp_in"), one("P", "G"))
        zexp_out = Count(sem("zexp_out"), one("P", "G"))
        rows_ready = Count(sem("rows_ready"), dict(G=(1, 3)))
        conv_done = Count(sem("conv_done"), dict(LRU=(2, 4)))
        la_ready = Count(sem("la_ready"), dict(LRU=(2, 1)))
        ea_ready = Count(sem("ea_ready"), dict(LRU=(2, 2)))
        q_ready = Count(sem("q_ready"), dict(LRU=(2, 1)))
        sq_ready = Count(sem("sq_ready"), dict(LRU=(2, 1)))
        lru_done = Count(sem("lru_done"), dict(LRU=(2, 1)), 1)
        merged_ready = Count(sem("merged_ready"), dict(MB=(4, 2), MC=(4, 2)), 1)
        sel_ready = Count(sem("sel_ready"), dict(FQ=(4, 1), MQ=(4, 1)))
        vst_ready = Count(sem("vst_ready"), dict(MQ=(4, 1)))
        srow_ready = Count(sem("srow_ready"), dict(FQ=(4, 16)))
        prob_ready = Count(sem("prob_ready"), dict(FQ=(4, 16)), 2)
        rinv_ready = Count(sem("rinv_ready"), dict(FQ=(4, 16)))
        gdm_ready = Count(sem("gdm_ready"), dict(MQ=(4, 2)))
        dec_ready = Count(sem("dec_ready"), dict(MQ=(4, 8)))
        wts_ready = Count(sem("wts_ready"), dict(MQ=(4, 8)))
        h_ready = Count(sem("h_ready"), dict(MQ=(4, 2)))
        hc_ready = Count(sem("hc_ready"), dict(MQ=(4, 2)))
        hsq_ready = Count(sem("hsq_ready"), dict(MQ=(4, 2)))
        dsq_ready = Count(sem("dsq_ready"), dict(MQ=(4, 2)))
        dev_ready = Count(sem("dev_ready"), dict(MQ=(4, 2)))
        ml_y = Count(sem("ml_y"), dict(MQ=(4, 2)), 2)
        og_done = Count(sem("og_done"), dict(MO=(2, 4)))
        best_done = Count(sem("best_done"), dict(WQ=(4, 1)), 1)
        wsm_in = Count(sem("wsm_in"), dict(T=(TT, 1)))
        wsm_out = Count(sem("wsm_out"), dict(T=(TT, 1)))
        tanh_in = Count(sem("tanh_in"), dict(T=(TT, 1)))
        tanh_out = Count(sem("tanh_out"), dict(T=(TT, 1)))
        eidx_ready = Count(sem("eidx_ready"), dict(T=(TT, 2)))
        g_used = Count(sem("g_used"), dict(T=(TT, 2 * SLOTS)), GR)
        dve_step = Count(sem("dve_step"), dict(
            N1=(1, 1), P=(1, 17), G=(1, 23), LRU=(2, 21), FQ=(4, 16), MQ=(4, 6),
            N2=(1, 5), WQ=(3, 82)))
        last_key_step = Count(sem("last_key_step"), dict(FIRST=(1, 22), REST=(1, 66)))
        square_done = Count(sem("square_done"), dict(T=(TT, 1)), TT)
        choose_step = Count(sem("choose_step"), dict(T=(TT, 67)))
        gelu_step = Count(sem("gelu_step"), dict(T=(TT, 4)))
        dve_total = dve_step.total

        def stand(eng):
            eng.sem_inc(waits_taken, 1)

        def rnd(L, phase, i):
            return L * NROUND + i + ROUND0[phase]

        def slots_done(L, phase, i, n):
            return 4 * rnd(L, phase, i) + (n + 4)

        block = ctx.enter_context(nc.Block())

        @block.sync
        def _(sp):
            sp.dma_start(x[:, :, :], x_in.rearrange("(t p) d -> p t d", p=P)).then_inc(x_loaded, 16)
            for s in range(4):
                sp.dma_start(ring[s][:, :], w_stream[s]).then_inc(w_ready[s], 16)
            with sp.Fori(1, DEPTH * NROUND) as r:
                for s in range(4):
                    sp.wait_ge(proj_done, 4 * r + (s + 1))
                    sp.dma_start(ring[s][:, :], w_stream[4 * r + s]).then_inc(w_ready[s], 16)
            sp.wait_ge(layer_done.sem, DEPTH + 1)
            sp.dma_start(nwb[:, :], fnorm.partition_broadcast(P)).then_inc(fnw_loaded, 16)
            for t in range(TT):
                sp.wait_ge(out_ready, t + 1)
                sp.dma_start(out[t * P:(t + 1) * P, :], hn[:, t, :]).then_inc(out_done, 16)
            sp.wait_ge(out_done, 16 * TT)

        @block.gpsimd
        def _(pool):
            nc.gpsimd.memset(ident[:, :], 0.0).then_inc(pool_step, 1)
            nc.gpsimd.memset(mask_q[:, :], 0.0).then_inc(pool_step, 1)
            nc.gpsimd.memset(mask_k[:, :], 0.0).then_inc(pool_step, 1)
            nc.gpsimd.memset(ones[:, :], 1.0).then_inc(pool_step, 1)
            nc.gpsimd.memset(inv[:, :], 1.0 / P).then_inc(pool_step, 1)
            nc.gpsimd.iota(iota_i[:, :], pattern=[[1, TOPK]], base=0, channel_multiplier=0).then_inc(pool_step, 1)
            pool.wait_ge(pool_step, 6)
            nc.gpsimd.affine_select(out=ident[:, :], in_=ident[:, :], compare_op=ALU.not_equal, fill=1.0,
                                    base=0, pattern=[[-1, P]], channel_multiplier=1).then_inc(consts_ready, 1)
            nc.gpsimd.affine_select(out=mask_q[:, :], in_=mask_q[:, :], compare_op=ALU.is_ge, fill=NEG,
                                    base=0, pattern=[[-1, P]], channel_multiplier=1).then_inc(consts_ready, 1)
            nc.gpsimd.affine_select(out=mask_k[:, :], in_=mask_k[:, :], compare_op=ALU.is_ge, fill=-NEG,
                                    base=0, pattern=[[1, P]], channel_multiplier=-1).then_inc(consts_ready, 1)
            nc.gpsimd.tensor_copy(iota_f[:, :], iota_i[:, :]).then_inc(consts_ready, 1)
            pool.wait_ge(consts_ready, 4)
            nc.gpsimd.tensor_tensor(head_hot[:, :], ident[0:M_AT + ML_H, G_AT:G_AT + ML_H],
                                    ident[0:M_AT + ML_H, M_AT:M_AT + ML_H], ALU.add).then_inc(pool_step, 1)
            pool.wait_ge(pool_step, 7)
            pool.wait_ge(consts_ready, 4)

            def gathers(table, L, t, base, part):
                stand(pool)
                with pool.Fori(part * SLOTS // (4 * GR), (part + 1) * SLOTS // (4 * GR)) as j:
                    for half in range(2):
                        nc.gpsimd.tensor_copy(estage[half][:, :], eidx[:, t, ds(2 * GR * j + GR * half, GR)])\
                            .then_inc(pool_stage, 1)
                        pool.wait_ge(pool_stage, stage_at(L, t, base, j, half))
                        for q in range(GR):
                            n = base + GR * half + q
                            pool.wait_ge(g_used.sem, g_used.at(L, "T", t, n) + 2 * GR * j + (1 - GR))
                            stand(pool)
                            nc.gpsimd.indirect_dma_start(
                                out=gring[:, q, :], out_offset=None, in_=table,
                                in_offset=bass.IndirectOffsetOnAxis(ap=estage[half][:, q:q + 1], axis=0))\
                                .then_inc(g_ready[q], 16)

            def stage_at(L, t, base, j, half):
                per = 2 * SLOTS // GR
                return (L * TT + t) * per + base // GR + 2 * j + (half + 1)

            def split_parts(b, src, n, L, ph, i, k):
                stand(pool)
                nc.gpsimd.tensor_tensor(w_hi[b][:, 0:n], src, ones[:, 0:1].to_broadcast([P, n]), ALU.mult)\
                    .then_inc(hi_done.sem, 1)
                pool.wait_ge(hi_done.sem, hi_done.at(L, ph, i, k + 1))
                nc.gpsimd.tensor_tensor(w_lo[b][:, 0:n], src, w_hi[b][:, 0:n].bitcast(F32), ALU.subtract)\
                    .then_inc(split_ready.sem, 1)

            def split_round(L, ph, i, slots=range(4)):
                for s in slots:
                    pool.wait_ge(w_ready[s], 16 * rnd(L, ph, i) + 16)
                    pool.wait_ge(proj_done, slots_done(L, ph, i, s - 1))
                    split_parts(s % 2, ring[s][:, :], D, L, ph, i, s)

            def split_rounds(L, ph):
                with pool.Fori(0, ROUNDS[ph]) as i:
                    split_round(L, ph, i)

            with pool.Fori(0, DEPTH) as L:
                pool.wait_ge(wgate_ready, 16 * L + 16)
                split_parts(0, wgate, KC * GATES, L, "G", 0, 0)
                pool.wait_ge(filled[4].sem, filled[4].at(L, "G", 0, 1))
                stand(pool)
                split_rounds(L, "LRU")
                split_rounds(L, "FV")
                split_rounds(L, "MA")
                with pool.Fori(0, 4) as i:
                    split_round(L, "FQ", i, (0, 1))
                    pool.wait_ge(filled[7].sem, filled[7].at(L, "FQ", i, 0))
                    stand(pool)
                    nc.gpsimd.tensor_copy(sel[0:NROW, :, :], ident[0:NROW, ds(4 * i + ML_H, 4)]
                                          .unsqueeze(2).to_broadcast([NROW, 4, P])).then_inc(sel_ready.sem, 1)
                    split_round(L, "FQ", i, (2, 3))
                split_rounds(L, "MV")
                split_rounds(L, "MB")
                split_rounds(L, "MO")
                with pool.Fori(0, 4) as i:
                    split_round(L, "MQ", i, (0, 1))
                    pool.wait_ge(filled[7].sem, filled[7].at(L, "MQ", i, 0))
                    pool.wait_ge(filled[6].sem, filled[6].at(L, "MQ", i, 0))
                    stand(pool)
                    nc.gpsimd.tensor_copy(sel[:, 0:2, :], head_hot[:, ds(2 * i, 2)]
                                          .unsqueeze(2).to_broadcast([M_AT + ML_H, 2, P])).then_inc(sel_ready.sem, 1)
                    for s in range(4):
                        pool.wait_ge(drained[s].sem, drained[s].at(L, "MV", 1, 1))
                    stand(pool)
                    nc.gpsimd.tensor_copy(vst[:, :, :, :].rearrange("p t a n -> p t (a n)"),
                                          v_sb[:, :, ds(2 * P * i, 2 * P)]).then_inc(vst_ready.sem, 1)
                    split_round(L, "MQ", i, (2, 3))
                split_rounds(L, "MC")
                split_rounds(L, "OUT")
                split_rounds(L, "WQ")
                with pool.Fori(0, TT) as t:
                    for part in range(2):
                        pool.wait_ge(eidx_ready.sem, eidx_ready.at(L, "T", t, part + 1))
                        gathers(u_tab, L, t, 0, part)
                    for part in range(2):
                        gathers(v_tab, L, t, SLOTS, part)

        @block.tensor
        def _(pe):
            for b in range(8):
                pe.sem_inc(drained_sem[b], 1)
            pe.wait_ge(consts_ready, 4)

            def fill_wait(b, L, ph, i, n):
                pe.wait_ge(drained[b].sem, drained[b].at(L, ph, i, n))

            def transpose_norm(L, ph):
                for c in range(KC):
                    b = 4 + c % 4
                    fill_wait(b, L, ph, 0, c // 4)
                    for t in range(TT):
                        if c == 0:
                            pe.wait_ge(hn_ready.sem, hn_ready.at(L, ph, 0, t + 1))
                        mm = nc.tensor.transpose(bank[b][:, t * P:(t + 1) * P], hn[:, t, c * P:(c + 1) * P], ident[:, :])
                    mm.then_inc(filled[b].sem, 1)
                pe.wait_ge(xh_ready.sem, xh_ready.at(L, ph, 0, KC))
                stand(pe)

            def low_wait(L, ph):
                for b in range(4, 8):
                    pe.wait_ge(drained[b].sem, drained[b].at(L, ph, 0, 2))

            def high_low(out, w, x, low_wait):
                for c in range(KC):
                    for part in range(2):
                        nc.tensor.matmul(out, w(c)[part], x(c)[0], start=(c == 0 and part == 0), stop=False)
                low_wait()
                for c in range(KC):
                    mm = nc.tensor.matmul(out, w(c)[0], x(c)[1], start=False, stop=(c == KC - 1))
                return mm

            def x_parts(low):
                return lambda c: (xT[:, c, :], low[:, :, c * P:(c + 1) * P])

            def y_parts(hi):
                return lambda c: (hi[:, c, :], y_lo[:, c, :])

            def project(L, ph, i, s, x, low_wait=lambda: None):
                pe.wait_ge(split_ready.sem, split_ready.at(L, ph, i, s + 1))
                pe.wait_ge(drained_sem[s], rnd(L, ph, i) + 1)
                high_low(bank[s][:, :], lambda c: [w[s % 2][:, c * P:(c + 1) * P] for w in (w_hi, w_lo)], x, low_wait)\
                    .then_inc(proj_done, 1)

            def project_tokens(L, ph, i, hi, lo):
                for s in range(4):
                    pe.wait_ge(split_ready.sem, split_ready.at(L, ph, i, s + 1))
                    if ph == "OUT":
                        pe.wait_ge(y_lo_ready.sem, y_lo_ready.at(L, "MC", s, 1))
                    for t in range(TT):
                        if s == 0:
                            pe.wait_ge(drained_sem[t], rnd(L, ph, i) + 1)
                        for kk in range(2):
                            c = 2 * s + kk
                            wh, wl = (w[s % 2][:, kk * SEQ:(kk + 1) * SEQ] for w in (w_hi, w_lo))
                            for n, (lhsT, rhs) in enumerate(((hi(c, t), wh), (hi(c, t), wl), (lo(c, t), wh))):
                                mm = nc.tensor.matmul(bank[t][:, :], lhsT, rhs, start=(c == 0 and n == 0),
                                                      stop=(c == KC - 1 and n == 2))
                    mm.then_inc(proj_done, 1)

            def of_tile(buf):
                return lambda c, t: buf[:, c, t * P:(t + 1) * P]

            def xl_of_tile(c, t):
                return xl_mix[:, t, c * P:(c + 1) * P]

            def merge(L, ph, hi, branch_out):
                stand(pe)
                with pe.Fori(0, 4) as i:
                    for s in range(4):
                        if s == 2:
                            pe.wait_ge(y_lo_ready.sem, y_lo_ready.at(L, *branch_out, 1))
                        project(L, ph, i, s, x_parts(xl_mix) if s < 2 else y_parts(hi))

            with pe.Fori(0, DEPTH) as L:
                transpose_norm(L, "N1")
                pe.wait_ge(split_ready.sem, split_ready.at(L, "G", 0, 1))
                fill_wait(4, L, "G", 0, 0)
                high_low(bank[4][0:GATES, :], lambda c: [w[0][:, c * GATES:(c + 1) * GATES] for w in (w_hi, w_lo)],
                         x_parts(xl_mix), lambda: low_wait(L, "N1")).then_inc(filled[4].sem, 1)
                with pe.Fori(0, 2) as i:
                    for s in range(4):
                        project(L, "LRU", i, s, x_parts(xl_mix))

                def gate_products(i):
                    pe.wait_ge(lruw_ready, 32 * L + (16 * i + 16))
                    for s in range(4):
                        pe.wait_ge(conv_done.sem, conv_done.at(L, "LRU", i, s + 1))
                        for g in range(2):
                            b = 4 + 2 * (s % 2) + g
                            fill_wait(b, L, "LRU", i, s // 2)
                            nc.tensor.matmul(bank[b][:, :], lruw[:, s, g, :], xc[:, s, :], start=True, stop=True)\
                                .then_inc(filled[b].sem, 1)

                gate_products(0)
                project_tokens(L, "FV", 0, of_tile(xT), xl_of_tile)
                gate_products(1)
                pe.wait_ge(rows_ready.sem, rows_ready.at(L, "G", 0, 3))
                fill_wait(6, L, "COLS", 0, 0)
                stand(pe)
                for t in range(TT):
                    mm = nc.tensor.transpose(bank[6][:, t * NROW:(t + 1) * NROW], cum[:, t * P:(t + 1) * P],
                                             ident[0:NROW, 0:NROW])
                mm.then_inc(filled[6].sem, 1)
                fill_wait(7, L, "COLS", 0, 0)
                stand(pe)
                for t in range(TT):
                    mm = nc.tensor.transpose(bank[7][:, t * ML_H:(t + 1) * ML_H], g_row[:, t * P:(t + 1) * P],
                                             ident[0:ML_H, 0:ML_H])
                mm.then_inc(filled[7].sem, 1)
                project_tokens(L, "FV", 1, of_tile(xT), xl_of_tile)
                merge(L, "MA", y_hi_lru, ("LRU", 0))
                with pe.Fori(0, 4) as i:
                    for s in range(4):
                        project(L, "FQ", i, s, x_parts(xl_mix))
                    pe.wait_ge(sel_ready.sem, sel_ready.at(L, "FQ", i, 1))
                    n6 = n7 = 0
                    for kind, u in fox_steps():
                        t, h = u % 4, u // 4
                        b = 4 + u % 2
                        if kind == "C":
                            fill_wait(7, L, "FQ", i, n7)
                            for part in range(2):
                                mm = nc.tensor.matmul(bank[7][:, :], sel[0:NROW, u, :], row_parts[0:NROW, part, :],
                                                      start=(part == 0), stop=(part == 1))
                            mm.then_inc(filled[7].sem, 1)
                            n7 += 1
                        elif kind == "S":
                            pp, hp = h // 2, h % 2
                            if u == 0:
                                for s in range(4):
                                    pe.wait_ge(drained_sem[s], rnd(L, "FQ", i) + 2)
                            fill_wait(b, L, "FQ", i, u // 2)
                            rowsel = slice(FOX_D * hp, FOX_D * hp + FOX_D)
                            nc.tensor.matmul(bank[b][:, 0:(t + 1) * P], qk[rowsel, 2 * pp, t * P:(t + 1) * P],
                                             qk[rowsel, 2 * pp + 1, 0:(t + 1) * P], start=True, stop=True)\
                                .then_inc(filled[b].sem, 1)
                        elif kind == "T":
                            pe.wait_ge(prob_ready.sem, prob_ready.at(L, "FQ", i, u + 1))
                            fill_wait(6, L, "FQ", i, n6)
                            for kb in range(t + 1):
                                mm = nc.tensor.transpose(bank[6][:, kb * P:(kb + 1) * P],
                                                         pr[:, u % 2, kb * P:(kb + 1) * P], ident[:, :])
                            mm.then_inc(filled[6].sem, 1)
                            n6 += 1
                        elif kind == "V":
                            pe.wait_ge(drained_sem[6], drained[6].at(L, "FQ", i, u + 1))
                            fill_wait(7, L, "FQ", i, n7)
                            for kb in range(t + 1):
                                mm = nc.tensor.matmul(bank[7][:, 0:FOX_D], pT[:, u % 2, kb * P:(kb + 1) * P],
                                                      v_sb[:, kb, ds(4 * FOX_D * i + FOX_D * h, FOX_D)],
                                                      start=(kb == 0), stop=(kb == t))
                            mm.then_inc(filled[7].sem, 1)
                            n7 += 1
                        else:
                            fill_wait(7, L, "FQ", i, n7)
                            for tt in range(TT):
                                mm = nc.tensor.transpose(bank[7][:, tt * P:(tt + 1) * P], ytok[:, tt, :], ident[:, :])
                            mm.then_inc(filled[7].sem, 1)
                            n7 += 1
                with pe.Fori(0, 2) as i:
                    project_tokens(L, "MV", i, of_tile(xT), xl_of_tile)
                merge(L, "MB", y_hi, ("FQ", 3))
                with pe.Fori(0, 2) as i:
                    for s in range(4):
                        project(L, "MO", i, s, x_parts(xl_mix))
                with pe.Fori(0, 4) as i:
                    n = {6: 0, 7: 0}

                    def spread(b, p, at):
                        fill_wait(b, L, "MQ", i, n[b])
                        for part in range(2):
                            mm = nc.tensor.matmul(bank[b][:, :], sel[at:at + ML_H, p, :], row_parts[at:at + ML_H, part, :],
                                                  start=(part == 0), stop=(part == 1))
                        mm.then_inc(filled[b].sem, 1)
                        n[b] += 1

                    def scores_of(p):
                        for s in range(TT):
                            b = 4 + s % 2
                            fill_wait(b, L, "MQ", i, 2 * p + s // 2)
                            nc.tensor.matmul(bank[b][:, 0:SEQ - s * P], qk[:, 2 * p + 1, s * P:(s + 1) * P],
                                             qk[:, 2 * p, s * P:SEQ], start=True, stop=True)\
                                .then_inc(filled[b].sem, 1)

                    def num_den(p):
                        for b in (6, 7):
                            fill_wait(b, L, "MQ", i, n[b])
                            for s in range(TT):
                                if b == 6:
                                    pe.wait_ge(wts_ready.sem, wts_ready.at(L, "MQ", i, 4 * p + s + 1))
                                lhsT = vst[:, s, p, :] if b == 6 else ones[:, 0:P]
                                mm = nc.tensor.matmul(bank[b][:, s * P:SEQ], lhsT, E[:, p, s, 0:SEQ - s * P],
                                                      start=(s == 0), stop=(s == TT - 1))
                            mm.then_inc(filled[b].sem, 1)
                            n[b] += 1

                    def mean(p, b, src, ready):
                        pe.wait_ge(ready.sem, ready.at(L, "MQ", i, p + 1))
                        fill_wait(b, L, "MQ", i, n[b])
                        nc.tensor.matmul(bank[b][:, :], inv[:, :], src[:, p, :], start=True, stop=True)\
                            .then_inc(filled[b].sem, 1)
                        n[b] += 1

                    for s in range(4):
                        project(L, "MQ", i, s, x_parts(xl_mix))
                        if s == 1:
                            pe.wait_ge(sel_ready.sem, sel_ready.at(L, "MQ", i, 1))
                        if s in (1, 2):
                            spread(6, s - 1, G_AT)
                            spread(7, s - 1, M_AT)
                    for s in range(4):
                        pe.wait_ge(drained_sem[s], rnd(L, "MQ", i) + 2)
                    pe.wait_ge(vst_ready.sem, vst_ready.at(L, "MQ", i, 1))
                    scores_of(0)
                    scores_of(1)
                    num_den(0)
                    mean(0, 6, hh, h_ready)
                    num_den(1)
                    mean(0, 7, sq, hsq_ready)
                    mean(1, 6, hh, h_ready)
                    mean(1, 7, sq, hsq_ready)
                merge(L, "MC", y_hi, ("MQ", 3))
                stand(pe)
                with pe.Fori(0, 2) as i:
                    project_tokens(L, "OUT", i, of_tile(m_hi), of_tile(m_lo))
                transpose_norm(L, "N2")
                with pe.Fori(0, 4) as i:
                    for s in range(4):
                        project(L, "WQ", i, s, x_parts(xl_peer), lambda: low_wait(L, "N2"))
                    for s in range(4):
                        pe.wait_ge(drained_sem[s], rnd(L, "WQ", i) + 2)
                        fill_wait(4 + s, L, "WQ", i, 0)
                        for t in range(TT):
                            mm = nc.tensor.matmul(bank[4 + s][:, t * P:(t + 1) * P], qk[:, s, t * P:(t + 1) * P],
                                                  subk[:, s % 2, :], start=True, stop=True)
                        mm.then_inc(filled[4 + s].sem, 1)

        @block.scalar
        def _(act):
            act.sem_inc(prob_ready.sem, 2)

            def evac_norm(L, ph):
                act.wait_ge(ms_ready.sem, ms_ready.at(L, ph, 0, 1))
                nc.scalar.activation(stat[:, 2, :], stat[:, 1, :], ACT.Sqrt).then_inc(sd_ready.sem, 1)
                for c in range(KC):
                    b = 4 + c % 4
                    act.wait_ge(filled[b].sem, filled[b].at(L, ph, 0, c // 4 + 1))
                    nc.scalar.copy(xT[:, c, :], bank[b][:, :]).then_inc(xh_ready.sem, 1)

            def proj_wait(L, ph, i, s):
                act.wait_ge(proj_done, slots_done(L, ph, i, s + 1))

            def values(L, ph, i):
                proj_wait(L, ph, i, 3)
                for t in range(TT):
                    nc.scalar.copy(v_sb[:, t, i * SEQ:(i + 1) * SEQ], bank[t][:, :]).then_inc(drained_sem[t], 1)

            def lru_high(L, i):
                act.wait_ge(lru_done.sem, lru_done.at(L, "LRU", i, 1))
                nc.scalar.copy(y_hi_lru[:, 4 * i:4 * i + 4, :], yT[:, 4 * i:4 * i + 4, :]).then_inc(y_hi_ready.sem, 1)

            def merge_gates(L, ph, branch):
                with act.Fori(0, 4) as i:
                    for j in range(2):
                        proj_wait(L, ph, i, j)
                        act.wait_ge(drained_sem[2 + j], rnd(L, ph, i) + 1)
                        nc.scalar.activation(gt[j], bank[j][:, :], ACT.Tanh, scale=0.5,
                                             bias=dcol(hb, 2 * i + (2 * KC + branch * KC + j)))\
                            .then_inc(drained_sem[j], 1)
                    if ph == "MC":
                        act.wait_ge(merged_ready.sem, merged_ready.at(L, "MC", i, 2))
                        nc.scalar.copy(m_hi[:, ds(2 * i, 2), :], merged[:, ds(2 * i, 2), :]).then_inc(y_hi_ready.sem, 1)

            with act.Fori(0, DEPTH) as L:
                act.wait_ge(layer_done.sem, layer_done.at(L, "L", 0, 0))
                act.dma_start(pv[:, :], pvec[L][:, 0:PV_KEPT]).then_inc(params_ready, 16)
                act.dma_start(wgate, pvec[L][:, PV_KEPT:PV]).then_inc(wgate_ready, 16)
                act.dma_start(nwb[:, :], nrows[2 * L].partition_broadcast(P)).then_inc(nw_loaded, 16)
                act.dma_start(lruw, w_lru[2 * L].rearrange("p (s g n) -> p s g n", s=4, g=2))\
                    .then_inc(lruw_ready, 16)
                evac_norm(L, "N1")
                act.wait_ge(hn_ready.sem, hn_ready.at(L, "N1", 0, TT))
                act.dma_start(nwb[:, :], nrows[2 * L + 1].partition_broadcast(P)).then_inc(nw_loaded, 16)
                for ph in ("P", "G"):
                    act.wait_ge(zexp_in.sem, zexp_in.at(L, ph, 0, 1))
                    tile = lp[:, 0, :] if ph == "P" else rows[:, 1, :]
                    nc.scalar.activation(tile, tile, ACT.Exp).then_inc(zexp_out.sem, 1)
                for i in range(2):
                    for s in range(4):
                        proj_wait(L, "LRU", i, s)
                        nc.scalar.copy(xpad[:, 4 * i + s, CONV - 1:], bank[s][:, :]).then_inc(drained_sem[s], 1)
                for i in range(2):
                    if i == 1:
                        values(L, "FV", 0)
                    act.wait_ge(lru_done.sem, lru_done.at(L, "LRU", i, 0))
                    for s in range(4):
                        for g in range(2):
                            b = 4 + 2 * (s % 2) + g
                            act.wait_ge(filled[b].sem, filled[b].at(L, "LRU", i, s // 2 + 1))
                            nc.scalar.activation((TI if g else R)[:, s, :], bank[b][:, :], ACT.Tanh, scale=0.5,
                                                 bias=hb[:, g * KC + 4 * i + s:g * KC + 4 * i + s + 1])\
                                .then_inc(drained_sem[b], 1)
                    if i == 0:
                        act.dma_start(lruw, w_lru[2 * L + 1].rearrange("p (s g n) -> p s g n", s=4, g=2))\
                            .then_inc(lruw_ready, 16)
                    if i == 1:
                        lru_high(L, 0)
                    act.wait_ge(la_ready.sem, la_ready.at(L, "LRU", i, 1))
                    nc.scalar.activation(TH[:, :, :], R, ACT.Tanh).then_inc(ea_ready.sem, 1)
                    nc.scalar.activation(A, R, ACT.Exp).then_inc(ea_ready.sem, 1)
                    act.wait_ge(q_ready.sem, q_ready.at(L, "LRU", i, 1))
                    nc.scalar.activation(TH[:, :, :], TH[:, :, :], ACT.Sqrt, scale=-0.25).then_inc(sq_ready.sem, 1)
                act.wait_ge(filled[6].sem, filled[6].at(L, "COLS", 0, 1))
                nc.scalar.copy(cumc[:, :, :], bank[6][:, 0:TT * NROW].rearrange("p (t n) -> p t n", t=TT))\
                    .then_inc(drained_sem[6], 1)
                act.wait_ge(filled[7].sem, filled[7].at(L, "COLS", 0, 1))
                nc.scalar.copy(gcol[:, :, :], bank[7][:, 0:TT * ML_H].rearrange("p (t n) -> p t n", t=TT))\
                    .then_inc(drained_sem[7], 1)
                values(L, "FV", 1)
                lru_high(L, 1)
                merge_gates(L, "MA", 0)
                with act.Fori(0, 4) as i:
                    for s in range(4):
                        proj_wait(L, "FQ", i, s)
                        nc.scalar.activation(qk[:, s, :], bank[s][:, :], ACT.Copy,
                                             scale=FOX_D ** -0.5 if s % 2 == 0 else 1.0)\
                            .then_inc(drained_sem[s], 1)
                    n7 = 0
                    todo = []
                    for kind, u in fox_steps():
                        t, h = u % 4, u // 4
                        n = (t + 1) * P
                        if kind == "S":
                            todo.append(u)
                        if kind == "C":
                            act.wait_ge(filled[7].sem, filled[7].at(L, "FQ", i, n7 + 1))
                            nc.scalar.copy(cb[:, u % 2, :], bank[7][:, :]).then_inc(drained_sem[7], 1)
                            n7 += 1
                        if kind == "T":
                            act.wait_ge(filled[6].sem, filled[6].at(L, "FQ", i, u + 1))
                            nc.scalar.copy(pT[:, u % 2, 0:n], bank[6][:, 0:n]).then_inc(drained_sem[6], 1)
                        if kind == "V":
                            act.wait_ge(filled[7].sem, filled[7].at(L, "FQ", i, n7 + 1))
                            act.wait_ge(rinv_ready.sem, rinv_ready.at(L, "FQ", i, u + 1))
                            nc.scalar.activation(ytok[:, t, FOX_D * (h % 2):FOX_D * (h % 2) + FOX_D],
                                                 bank[7][:, 0:FOX_D], ACT.Copy, scale=rinv[:, u:u + 1])\
                                .then_inc(drained_sem[7], 1)
                            n7 += 1
                        if kind == "Y":
                            act.wait_ge(filled[7].sem, filled[7].at(L, "FQ", i, n7 + 1))
                            nc.scalar.copy(yT[:, 2 * i + u, :], bank[7][:, :]).then_inc(drained_sem[7], 1)
                            n7 += 1
                            act.wait_ge(drained_sem[7], drained[7].at(L, "FQ", i, n7))
                            nc.scalar.copy(y_hi[:, ds(2 * i + u, 1), :], yT[:, ds(2 * i + u, 1), :])\
                                .then_inc(y_hi_ready.sem, 1)
                        if todo and (kind == "V" or (kind == "T" and u == 0) or (kind == "S" and u < 2)):
                            e = todo.pop(0)
                            ne = (e % 4 + 1) * P
                            act.wait_ge(srow_ready.sem, srow_ready.at(L, "FQ", i, e + 1))
                            nc.scalar.activation(pr[:, e % 2, 0:ne], sc[:, e % 2, 0:ne], ACT.Exp,
                                                 bias=nmax[:, e:e + 1], accum_out=rsum[:, e:e + 1])\
                                .then_inc(prob_ready.sem, 1)
                    assert not todo
                values(L, "MV", 0)
                values(L, "MV", 1)
                merge_gates(L, "MB", 1)
                with act.Fori(0, 2) as i:
                    for s in range(4):
                        proj_wait(L, "MO", i, s)
                        nc.scalar.activation(og[:, 4 * i + s, :], bank[s][:, :], ACT.Tanh, scale=0.5)\
                            .then_inc(drained_sem[s], 1)
                with act.Fori(0, 4) as i:
                    def centred_square(p):
                        act.wait_ge(hc_ready.sem, hc_ready.at(L, "MQ", i, p + 1))
                        nc.scalar.activation(sq[:, p, :], hh[:, p, :], ACT.Square).then_inc(hsq_ready.sem, 1)

                    for s in range(4):
                        proj_wait(L, "MQ", i, s)
                        nc.scalar.activation(qk[:, s, :], bank[s][:, :], ACT.Copy,
                                             scale=ML_D ** -0.5 if s % 2 == 1 else 1.0)\
                            .then_inc(drained_sem[s], 1)
                        if s in (1, 2):
                            p = s - 1
                            act.wait_ge(filled[6].sem, filled[6].at(L, "MQ", i, p + 1))
                            if p == 1:
                                act.wait_ge(dec_ready.sem, dec_ready.at(L, "MQ", i, TT))
                            nc.scalar.copy(gb, bank[6][:, :]).then_inc(drained_sem[6], 1)
                            act.wait_ge(filled[7].sem, filled[7].at(L, "MQ", i, p + 1))
                            act.wait_ge(ml_y.sem, ml_y.at(L, "MQ", i, p) - 1)
                            nc.scalar.activation(em[:, p, :], bank[7][:, :], ACT.Exp, scale=-1.0)\
                                .then_inc(drained_sem[7], 1)
                            act.wait_ge(drained_sem[6], drained[6].at(L, "MQ", i, p + 1))
                            act.wait_ge(gdm_ready.sem, gdm_ready.at(L, "MQ", i, p + 1))
                            for k in range(TT):
                                gs = gcol[:, k, ds(2 * i + p, 1)]
                                if k < TT - 1:
                                    nc.scalar.activation(E[:, p, k, P:SEQ - k * P], gb[:, (k + 1) * P:], ACT.Exp,
                                                         scale=-1.0, bias=gs)
                                nc.scalar.activation(E[:, p, k, 0:P], gdm[:, k, :], ACT.Exp, scale=-1.0, bias=gs)\
                                    .then_inc(dec_ready.sem, 1)
                    for p in range(2):
                        act.wait_ge(filled[6].sem, filled[6].at(L, "MQ", i, 3 + 2 * p))
                        nc.scalar.copy(hh[:, p, :], bank[6][:, :]).then_inc(drained_sem[6], 1)
                        act.wait_ge(drained_sem[6], drained[6].at(L, "MQ", i, 3 + 2 * p))
                        act.sem_inc(h_ready.sem, 1)
                        act.wait_ge(drained_sem[7], drained[7].at(L, "MQ", i, 3 + p))
                        nc.scalar.activation(em[:, p, :], em[:, p, :], ACT.Square, scale=EPS ** 0.5)\
                            .then_inc(dsq_ready.sem, 1)
                        if p == 1:
                            centred_square(0)
                    centred_square(1)
                    for p in range(2):
                        act.wait_ge(drained_sem[7], drained[7].at(L, "MQ", i, 5 + p))
                        nc.scalar.activation(em[:, p, :], em[:, p, :], ACT.Sqrt).then_inc(dev_ready.sem, 1)
                    act.wait_ge(ml_y.sem, ml_y.at(L, "MQ", i, 2))
                    nc.scalar.copy(y_hi[:, ds(2 * i, 2), :], yT[:, ds(2 * i, 2), :]).then_inc(y_hi_ready.sem, 1)
                merge_gates(L, "MC", 2)
                evac_norm(L, "N2")
                with act.Fori(0, 4) as i:
                    for s in range(4):
                        proj_wait(L, "WQ", i, s)
                        nc.scalar.copy(qk[:, s, :], bank[s][:, :]).then_inc(drained_sem[s], 1)
                    for s in range(4):
                        act.wait_ge(filled[4 + s].sem, filled[4 + s].at(L, "WQ", i, 1))
                        if s == 0:
                            act.wait_ge(best_done.sem, best_done.at(L, "WQ", i, 0))
                        nc.scalar.copy(keys[:, 4 * s:4 * s + 4, :], bank[4 + s][:, :].rearrange("p (t n) -> p t n", t=TT))\
                            .then_inc(drained_sem[4 + s], 1)

                def soft(L, t):
                    act.wait_ge(wsm_in.sem, wsm_in.at(L, "T", t, 1))
                    nc.scalar.activation(wts, wts, ACT.Exp).then_inc(wsm_out.sem, 1)

                def gelu_tanh(L, t):
                    act.wait_ge(tanh_in.sem, tanh_in.at(L, "T", t, 1))
                    nc.scalar.activation(th, gin, ACT.Tanh).then_inc(tanh_out.sem, 1)

                soft(L, 0)
                with act.Fori(0, TT - 1) as t:
                    gelu_tanh(L, t)
                    soft(L, t + 1)
                gelu_tanh(L, TT - 1)
            act.wait_ge(ms_final, 1)
            nc.scalar.activation(stat[:, 2, :], stat[:, 1, :], ACT.Sqrt).then_inc(sd_final, 1)

        @block.vector
        def _(dve):
            V = nc.vector
            dve.sem_inc(proj_done, 4)
            for c in (layer_done, lru_done, ml_y, g_used, merged_ready, best_done):
                dve.sem_inc(c.sem, c.credit)
            V.memset(first_expert[:, :], 0.0).then_inc(final_step, 1)
            dve.wait_ge(final_step, 1)
            dve.wait_ge(x_loaded, 16)

            def square_sum(t):
                return V.scalar_tensor_tensor(out=hn[:, t, :], in0=x[:, t, :], scalar=1.0, in1=x[:, t, :],
                                              op0=ALU.mult, op1=ALU.mult, accum_out=stat[:, 0, ds(t, 1)])

            def mean_square():
                return V.tensor_scalar(stat[:, 1, :], stat[:, 0, :], 1.0 / D, EPS, ALU.mult, ALU.add)

            def scale_rows(t, w):
                return V.scalar_tensor_tensor(out=hn[:, t, :], in0=x[:, t, :], scalar=stat[:, 3, t:t + 1], in1=w,
                                              op0=ALU.mult, op1=ALU.mult)

            def norm(L, ph, a):
                c = Chain(dve, dve_step, L, ph, 0)
                if a == 0:
                    dve.wait_ge(square_done.sem, square_done.at(L, "T", 0, 0))
                else:
                    for t in range(TT):
                        c.step(square_sum(t))
                    c.wait()
                mean_square().then_inc(ms_ready.sem, 1)
                dve.wait_ge(sd_ready.sem, sd_ready.at(L, ph, 0, 1))
                c.step(V.reciprocal(stat[:, 3, :], stat[:, 2, :]))
                c.wait()
                dve.wait_ge(nw_loaded, 32 * L + 16 * (a + 1))
                for t in range(TT):
                    scale_rows(t, nwb[:, :]).then_inc(hn_ready.sem, 1)
                c.close()
                low = xl_peer if a else xl_mix
                for k in range(KC):
                    b = 4 + k % 4
                    dve.wait_ge(xh_ready.sem, xh_ready.at(L, ph, 0, k + 1))
                    V.tensor_tensor(low[:, :, k * P:(k + 1) * P], bank[b][:, :].rearrange("p (t n) -> p t n", t=TT),
                                    xT[:, k, :].bitcast(F32).rearrange("p (t n) -> p t n", t=TT), ALU.subtract)\
                        .then_inc(drained_sem[b], 1)

            def log1p(c, z, s, q, r):
                c.step(V.tensor_scalar(s, z, 2.0, None, ALU.add))
                c.wait()
                c.step(V.reciprocal(q, s))
                c.wait()
                c.step(V.tensor_tensor(s, z, q, ALU.mult))
                c.wait()
                c.step(V.tensor_tensor(q, s, s, ALU.mult))
                c.wait()
                c.step(V.tensor_scalar(r, q, 1.0 / 15, None, ALU.mult))
                c.wait()
                for k in (13, 11, 9, 7, 5, 3):
                    c.step(V.scalar_tensor_tensor(out=r, in0=r, scalar=1.0 / k, in1=q, op0=ALU.add, op1=ALU.mult))
                    c.wait()
                c.step(V.scalar_tensor_tensor(out=r, in0=r, scalar=1.0, in1=s, op0=ALU.add, op1=ALU.mult))
                c.wait()

            def merge(L, ph):
                with dve.Fori(0, 4) as i:
                    for j in range(2):
                        dve.wait_ge(proj_done, slots_done(L, ph, i, 3 + j))
                        dve.wait_ge(drained_sem[j], rnd(L, ph, i) + 2)
                        dst = merged[:, 2 * i + j, :]
                        to = dst if ph == "MA" else mtmp
                        if ph != "MA":
                            dve.wait_ge(merged_ready.sem, merged_ready.at(L, ph, i, j))
                        V.scalar_tensor_tensor(out=to, in0=gt[j], scalar=1.0, in1=bank[2 + j][:, :],
                                               op0=ALU.add, op1=ALU.mult).then_inc(drained_sem[2 + j], 1)
                        if ph != "MA":
                            dve.wait_ge(drained_sem[2 + j], rnd(L, ph, i) + 2)
                            V.tensor_tensor(dst, dst, mtmp, ALU.add).then_inc(merged_ready.sem, 1)
                    if ph == "MC":
                        low_part(L, ph, i, m_lo, merged, m_hi, 1)

            def low_part(L, ph, i, lo, src, hi, n):
                dve.wait_ge(y_hi_ready.sem, y_hi_ready.at(L, ph, i, n))
                V.tensor_tensor(lo[:, ds(2 * i, 2), :], src[:, ds(2 * i, 2), :], hi[:, ds(2 * i, 2), :].bitcast(F32),
                                ALU.subtract).then_inc(y_lo_ready.sem, 1)

            for t in range(TT):
                square_sum(t).then_inc(square_done.sem, 1)

            with dve.Fori(0, DEPTH) as L:
                norm(L, "N1", 0)
                c = Chain(dve, dve_step, L, "P", 0)
                dve.wait_ge(params_ready, 16 * L + 16)
                lam = pcol("lam", 0, KC)
                c.step(V.tensor_scalar(hb[:, :], pcol("ba", 0, 5 * KC), 0.5, None, ALU.mult))
                c.step(V.tensor_scalar(hnw[:, :], pcol("nw", 0, KC), 0.5, None, ALU.mult))
                c.step(V.tensor_scalar(nsp[:, :], lam, -1.0, None, ALU.mult))
                c.wait()
                V.tensor_tensor(lp[:, 0, :], lam, nsp[:, :], ALU.min).then_inc(zexp_in.sem, 1)
                dve.wait_ge(zexp_out.sem, zexp_out.at(L, "P", 0, 1))
                log1p(c, lp[:, 0, :], lp[:, 1, :], lp[:, 2, :], lp[:, 0, :])
                c.step(V.tensor_scalar(nsp[:, :], nsp[:, :], 0.0, -4.0, ALU.max, ALU.mult))
                c.wait()
                c.step(V.scalar_tensor_tensor(out=nsp[:, :], in0=lp[:, 0, :], scalar=-8.0, in1=nsp[:, :],
                                              op0=ALU.mult, op1=ALU.add))
                c.close()
                c = Chain(dve, dve_step, L, "G", 0)
                dve.wait_ge(filled[4].sem, filled[4].at(L, "G", 0, 1))
                c.step(V.tensor_scalar(rows[:, 0, :], bank[4][0:NROW, :], pcol("fbias", 0)[0:NROW, :], None, ALU.add))
                c.wait()
                V.tensor_scalar(rows[0:ML_H, 5, :], bank[4][I_ROW:GATES, :], pcol("ibias", 0)[0:ML_H, :], None, ALU.add)\
                    .then_inc(drained_sem[4], 1)
                c.step(V.tensor_scalar(rows[:, 1, :], rows[:, 0, :], -1.0, None, ALU.mult))
                c.wait()
                V.tensor_tensor(rows[:, 1, :], rows[:, 1, :], rows[:, 0, :], ALU.min).then_inc(zexp_in.sem, 1)
                dve.wait_ge(zexp_out.sem, zexp_out.at(L, "G", 0, 1))
                log1p(c, rows[:, 1, :], rows[:, 2, :], rows[:, 3, :], rows[:, 4, :])
                c.step(V.tensor_scalar(rows[:, 0, :], rows[:, 0, :], 0.0, None, ALU.min))
                c.wait()
                c.step(V.scalar_tensor_tensor(out=rows[:, 0, :], in0=rows[:, 4, :], scalar=-2.0, in1=rows[:, 0, :],
                                              op0=ALU.mult, op1=ALU.add))
                c.wait()
                c.step(V.tensor_tensor_scan(cum[:, :], ones[0:NROW, 0:1].to_broadcast([NROW, SEQ]), rows[:, 0, :], 0.0, ALU.mult, ALU.add))
                c.wait()
                dve.wait_ge(drained_sem[4], drained[4].at(L, "G", 0, 1))
                c.step(V.tensor_tensor(g_row[:, :], rows[0:ML_H, 5, :], cum[0:ML_H, :], ALU.subtract))
                c.wait()
                c.step(V.tensor_tensor_scan(G_row[:, :], g_row[:, :], g_row[:, :], 0.0, ALU.max, ALU.max))
                c.wait()
                c.step(V.tensor_tensor(m_row[:, :], G_row[:, :], cum[0:ML_H, :], ALU.add))
                c.wait()
                split_rows = ((0, NROW, cum), (G_AT, ML_H, G_row), (M_AT, ML_H, m_row))
                for at, n, row in split_rows:
                    c.step(V.tensor_copy(row_parts[at:at + n, 0, :], row))
                c.wait()
                for at, n, row in split_rows:
                    V.tensor_tensor(row_parts[at:at + n, 1, :], row, row_parts[at:at + n, 0, :].bitcast(F32), ALU.subtract)\
                        .then_inc(rows_ready.sem, 1)
                c.close()
                V.memset(xpad[:, :, 0:CONV - 1], 0.0).then_inc(pad_ready, 1)
                dve.wait_ge(pad_ready, L + 1)
                stand(dve)
                with dve.Fori(0, 2) as i:
                    c = Chain(dve, dve_step, L, "LRU", i)
                    for k in range(CONV):
                        for s in range(4):
                            if k == 0:
                                dve.wait_ge(drained_sem[s], rnd(L, "LRU", i) + 2)
                            w = dcol(pv, 4 * i + (PV_COLS["conv_w"][0] + k * KC + s))
                            src = xpad[:, ds(4 * i + s, 1), k:k + SEQ]
                            if k == 0:
                                c.step(V.tensor_scalar(xc[:, s, :], src, w, dcol(pv, 4 * i + (PV_COLS["conv_b"][0] + s)),
                                                       ALU.mult, ALU.add))
                            else:
                                ins = V.scalar_tensor_tensor(out=xc[:, s, :], in0=src, scalar=w, in1=xc[:, s, :],
                                                             op0=ALU.mult, op1=ALU.add)
                                if k == CONV - 1:
                                    ins.then_inc(conv_done.sem, 1)
                                else:
                                    c.step(ins)
                        if k < CONV - 1:
                            c.wait()
                    for s in range(4):
                        b = 4 + 2 * (s % 2)
                        dve.wait_ge(drained_sem[b], drained[b].at(L, "LRU", i, s // 2 + 1))
                        ins = V.tensor_scalar(R[:, s, :], R[:, s, :], 1.0, dcol(nsp, 4 * i + s), ALU.add, ALU.mult)
                        if s < 3:
                            c.step(ins)
                        else:
                            ins.then_inc(la_ready.sem, 1)
                    dve.wait_ge(drained_sem[5], drained[5].at(L, "LRU", i, 2))
                    dve.wait_ge(drained_sem[7], drained[7].at(L, "LRU", i, 2))
                    dve.wait_ge(conv_done.sem, conv_done.at(L, "LRU", i, 4))
                    c.step(V.scalar_tensor_tensor(out=TI, in0=TI, scalar=1.0, in1=xc, op0=ALU.add, op1=ALU.mult))
                    dve.wait_ge(ea_ready.sem, ea_ready.at(L, "LRU", i, 2))
                    c.step(V.tensor_tensor(R, A, A, ALU.mult))
                    c.wait()
                    V.scalar_tensor_tensor(out=TH[:, :, :], in0=R, scalar=1.0, in1=TH[:, :, :], op0=ALU.add, op1=ALU.mult)\
                        .then_inc(q_ready.sem, 1)
                    dve.wait_ge(sq_ready.sem, sq_ready.at(L, "LRU", i, 1))
                    c.step(V.tensor_tensor(TI, TI, TH[:, :, :], ALU.mult))
                    c.wait()
                    for s in range(4):
                        ins = V.tensor_tensor_scan(yT[:, 4 * i + s, :], A[:, s, :], TI[:, s, :], 0.0, ALU.mult, ALU.add)
                        if s < 3:
                            c.step(ins)
                        else:
                            ins.then_inc(lru_done.sem, 1)
                    c.close()
                dve.wait_ge(y_hi_ready.sem, y_hi_ready.at(L, "LRU", 1, 1))
                V.tensor_tensor(y_lo[:, :, :], yT, y_hi_lru[:, :, :].bitcast(F32), ALU.subtract).then_inc(y_lo_ready.sem, 1)
                merge(L, "MA")
                with dve.Fori(0, 4) as i:
                    c = Chain(dve, dve_step, L, "FQ", i)
                    cn = 0
                    n7 = {}
                    count = 0
                    for kind, u in fox_steps():
                        if kind in "CVY":
                            count += 1
                            n7[kind, u] = count
                    for u in range(17):
                        if u < 16:
                            t, h = u % 4, u // 4
                            b, n = 4 + u % 2, (u % 4 + 1) * P
                            if t == 0:
                                dve.wait_ge(drained_sem[7], drained[7].at(L, "FQ", i, n7["C", h]))
                                if u == 0:
                                    dve.wait_ge(drained_sem[6], drained[6].at(L, "COLS", 0, 1))
                            dve.wait_ge(filled[b].sem, filled[b].at(L, "FQ", i, u // 2 + 1))
                            dve.wait_ge(prob_ready.sem, prob_ready.at(L, "FQ", i, u) - 1)
                            V.scalar_tensor_tensor(out=sc[:, u % 2, 0:n], in0=bank[b][:, 0:n],
                                                   scalar=cumc[:, t, ds(4 * i + (ML_H + h), 1)],
                                                   in1=cb[:, h % 2, 0:n], op0=ALU.add, op1=ALU.subtract)\
                                .then_inc(drained_sem[b], 1)
                            dve.wait_ge(drained_sem[b], drained[b].at(L, "FQ", i, u // 2 + 1))
                            diag = sc[:, u % 2, n - P:n]
                            c.step(V.tensor_tensor(diag, diag, mask_q[:, :], ALU.add))
                            c.wait()
                            V.tensor_reduce(nmax[:, u:u + 1], sc[:, u % 2, 0:n], AX.X, ALU.max, negate=True)\
                                .then_inc(srow_ready.sem, 1)
                        if u >= 1:
                            dve.wait_ge(prob_ready.sem, prob_ready.at(L, "FQ", i, u))
                            V.reciprocal(rinv[:, u - 1:u], rsum[:, u - 1:u]).then_inc(rinv_ready.sem, 1)
                    low_part(L, "FQ", i, y_lo, yT, y_hi, 2)
                    c.close()
                merge(L, "MB")
                stand(dve)
                with dve.Fori(0, 2) as i:
                    for s in range(4):
                        dve.wait_ge(drained_sem[s], rnd(L, "MO", i) + 2)
                        V.tensor_scalar(og[:, 4 * i + s, :], og[:, 4 * i + s, :], 1.0, dcol(hnw, 4 * i + s),
                                        ALU.add, ALU.mult).then_inc(og_done.sem, 1)
                with dve.Fori(0, 4) as i:
                    c = Chain(dve, dve_step, L, "MQ", i)

                    def decay_mask(p):
                        dve.wait_ge(drained_sem[6], drained[6].at(L, "MQ", i, p + 1))
                        V.tensor_tensor(gdm, gb.rearrange("p (s n) -> p s n", s=4),
                                        mask_k[:, :].unsqueeze(1).to_broadcast([P, 4, P]), ALU.add)\
                            .then_inc(gdm_ready.sem, 1)

                    def weigh(p):
                        for s in range(TT):
                            b = 4 + s % 2
                            n = SEQ - s * P
                            dve.wait_ge(filled[b].sem, filled[b].at(L, "MQ", i, 2 * p + s // 2 + 1))
                            dve.wait_ge(dec_ready.sem, dec_ready.at(L, "MQ", i, 4 * p + s + 1))
                            V.tensor_tensor(E[:, p, s, 0:n], bank[b][:, 0:n], E[:, p, s, 0:n], ALU.mult)\
                                .then_inc(drained_sem[b], 1)
                            dve.wait_ge(drained_sem[b], drained[b].at(L, "MQ", i, 2 * p + s // 2 + 1))
                            dve.sem_inc(wts_ready.sem, 1)

                    def denominator(p):
                        dve.wait_ge(drained_sem[7], drained[7].at(L, "MQ", i, p + 1))
                        dve.wait_ge(filled[7].sem, filled[7].at(L, "MQ", i, 3 + p))
                        c.step(V.tensor_tensor(em[:, p, :], bank[7][:, :], em[:, p, :], ALU.max))
                        c.wait()
                        V.scalar_tensor_tensor(out=em[:, p, :], in0=bank[7][:, :], scalar=-1.0, in1=em[:, p, :],
                                               op0=ALU.mult, op1=ALU.max).then_inc(drained_sem[7], 1)

                    def centre(p):
                        n6 = 6 if p else 4
                        dve.wait_ge(filled[6].sem, filled[6].at(L, "MQ", i, n6))
                        V.tensor_tensor(hh[:, p, :], hh[:, p, :], bank[6][:, :], ALU.subtract)\
                            .then_inc(drained_sem[6], 1)
                        dve.wait_ge(drained_sem[6], drained[6].at(L, "MQ", i, n6))
                        dve.sem_inc(hc_ready.sem, 1)

                    decay_mask(0)
                    decay_mask(1)
                    weigh(0)
                    weigh(1)
                    denominator(0)
                    centre(0)
                    denominator(1)
                    centre(1)
                    for p in range(2):
                        dve.wait_ge(filled[7].sem, filled[7].at(L, "MQ", i, 5 + p))
                        dve.wait_ge(dsq_ready.sem, dsq_ready.at(L, "MQ", i, p + 1))
                        V.tensor_tensor(em[:, p, :], bank[7][:, :], em[:, p, :], ALU.add).then_inc(drained_sem[7], 1)
                    for p in range(2):
                        dve.wait_ge(dev_ready.sem, dev_ready.at(L, "MQ", i, p + 1))
                        c.step(V.reciprocal(em[:, p, :], em[:, p, :]))
                        c.wait()
                        c.step(V.tensor_tensor(hh[:, p, :], hh[:, p, :], em[:, p, :], ALU.mult))
                        c.wait()
                        V.tensor_tensor(yT[:, 2 * i + p, :], hh[:, p, :], og[:, 2 * i + p, :], ALU.mult)\
                            .then_inc(ml_y.sem, 1)
                    c.close()
                    low_part(L, "MQ", i, y_lo, yT, y_hi, 1)
                    c.close()
                merge(L, "MC")
                with dve.Fori(0, 2) as i:
                    dve.wait_ge(proj_done, slots_done(L, "OUT", i, 4))
                    for t in range(TT):
                        xs = x[:, t, ds(SEQ * i, SEQ)]
                        V.scalar_tensor_tensor(out=xs, in0=bank[t][:, :], scalar=0.5, in1=xs, op0=ALU.mult, op1=ALU.add)\
                            .then_inc(drained_sem[t], 1)
                for t in range(TT):
                    dve.wait_ge(drained_sem[t], drained[t].at(L, "OUT", 1, 1))
                norm(L, "N2", 1)

                def top16(c, src, val, idx, groups):
                    def step(what):
                        for g in groups:
                            c.step(what(g))
                        c.wait()
                        stand(dve)
                    yield step(lambda g: V.max(val[:, g, 0:8], src[:, g, :]))
                    yield step(lambda g: V.max_index(idx[:, g, 0:8], val[:, g, 0:8], src[:, g, :]))
                    yield step(lambda g: V.match_replace(src[:, g, :], val[:, g, 0:8], src[:, g, :], NEG * 1e8))
                    yield step(lambda g: V.max(val[:, g, 8:16], src[:, g, :]))
                    yield step(lambda g: V.max_index(idx[:, g, 8:16], val[:, g, 8:16], src[:, g, :]))

                def best_keys(c, i, t0, t1):
                    yield from top16(c, keys, kval, kidx, [TT * s + t for s in range(4) for t in range(t0, t1)])
                    for dst, src in ((vals, kval), (idxf, kidx)):
                        by_tile = src.rearrange("p (s t) n -> p t s n", t=TT)
                        c.step(V.tensor_copy(dst[:, t0:t1, ds(4 * i, 4), :],
                                             by_tile[:, t0:t1, :, :]))
                    c.wait()
                    stand(dve)
                    yield

                LAST = ROUNDS["WQ"] - 1

                def keys_wait(i):
                    for s in range(4):
                        dve.wait_ge(drained_sem[4 + s], drained[4 + s].at(L, "WQ", i, 1))
                    stand(dve)

                with dve.Fori(0, LAST) as i:
                    c = Chain(dve, dve_step, L, "WQ", i)
                    keys_wait(i)
                    for _ in best_keys(c, i, 0, TT):
                        pass
                    dve.sem_inc(best_done.sem, 1)
                    c.close()
                    stand(dve)

                def rest_of_keys():
                    c = Chain(dve, last_key_step, L, "REST", 0)
                    for t in range(1, TT):
                        yield from best_keys(c, LAST, t, t + 1)
                    dve.sem_inc(best_done.sem, 1)
                    c.close()

                c = Chain(dve, last_key_step, L, "FIRST", 0)
                keys_wait(LAST)
                for _ in best_keys(c, LAST, 0, 1):
                    pass
                c.close()
                stand(dve)

                w3 = wts.rearrange("p (h n) -> p h n", h=PEER_H)
                HH = PEER_H // 2
                HS = SLOTS // 2
                full = [P, HH, TOPK, TOPK]
                small = [P, PEER_H, TOPK]
                PIECES = 2 * 14 + 2
                REST_PIECES = 6 * (TT - 1)

                def choose(t):
                    c = Chain(dve, choose_step, L, "T", t)
                    v4 = vals[:, t, :, :].rearrange("p (h a) n -> p h a n", a=2)
                    i4 = idxf[:, t, :, :].rearrange("p (h a) n -> p h a n", a=2)
                    for part in range(2):
                        hs = slice(HH * part, HH * part + HH)
                        ks = slice(HS * part, HS * part + HS)
                        c.step(V.tensor_tensor(cand[:, hs, :].rearrange("p h (a b) -> p h a b", a=TOPK),
                                               v4[:, hs, 0, :].unsqueeze(3).to_broadcast(full),
                                               v4[:, hs, 1, :].unsqueeze(2).to_broadcast(full), ALU.add))
                        c.wait()
                        stand(dve)
                        yield
                        yield from top16(c, cand, tv, posu.rearrange("p (h n) -> p h n", h=PEER_H),
                                         range(HH * part, HH * part + HH))
                        c.step(V.tensor_scalar(posu2[:, 0, ks], posu[:, ks], 4, None, ALU.logical_shift_right))
                        c.step(V.tensor_scalar(posu2[:, 1, ks], posu[:, ks], 15, None, ALU.bitwise_and))
                        c.wait()
                        c.step(V.tensor_copy(posa[:, ks], posu2[:, 0, ks]))
                        c.step(V.tensor_copy(posb[:, ks], posu2[:, 1, ks]))
                        c.wait()
                        yield
                        for half, (pos, e) in enumerate(((posa, e1), (posb, e2))):
                            eq3 = eqb[:, 0:HS * TOPK].rearrange("p (k n) -> p k n", n=TOPK)
                            c.step(V.tensor_tensor(eq3, pos[:, ks].unsqueeze(2).to_broadcast([P, HS, TOPK]),
                                                   iota_f[:, :].unsqueeze(1).to_broadcast([P, HS, TOPK]), ALU.is_equal))
                            c.wait()
                            yield
                            eq4 = eqb[:, 0:HS * TOPK].rearrange("p (h k n) -> p h k n", h=HH, n=TOPK)
                            c.step(V.tensor_tensor(eq4, eq4, i4[:, hs, half, :].unsqueeze(2).to_broadcast(full), ALU.mult))
                            c.wait()
                            yield
                            c.step(V.tensor_reduce(e[:, ks], eq3, AX.X, ALU.add))
                            c.wait()
                            yield
                        c.step(V.tensor_scalar(e2[:, ks], e2[:, ks], first_expert[:, :], None, ALU.add))
                        c.wait()
                        V.scalar_tensor_tensor(out=eidx[:, t, ks], in0=e1[:, ks], scalar=float(N_KEYS), in1=e2[:, ks],
                                               op0=ALU.mult, op1=ALU.add).then_inc(eidx_ready.sem, 1)
                        yield
                    V.tensor_tensor(w3, tv, tv[:, :, 0:1].to_broadcast(small), ALU.subtract).then_inc(wsm_in.sem, 1)
                    yield
                    dve.wait_ge(wsm_out.sem, wsm_out.at(L, "T", t, 1))
                    c.step(V.tensor_reduce(ssum, w3, AX.X, ALU.add))
                    c.wait()
                    c.step(V.reciprocal(ssum, ssum))
                    c.wait()
                    c.step(V.tensor_tensor(w3, w3, ssum.unsqueeze(2).to_broadcast(small), ALU.mult))
                    c.wait()
                    c.close()

                def tile(t, pieces=iter(()), count=0, early=0):
                    turns = 2 * SLOTS // GR

                    def pieces_by(turn):
                        half = turns // 2
                        return early * turn // half if turn <= half else early + (count - early) * (turn - half) // half

                    stretch = 1 if count else turns // 2
                    for j0 in range(0, turns, stretch):
                        values = j0 >= turns // 2
                        if j0 == turns // 2:
                            dve.wait_ge(g_used.sem, g_used.at(L, "T", t, SLOTS))
                            c = Chain(dve, gelu_step, L, "T", t)
                            c.step(V.tensor_tensor(gin, actv, actv, ALU.mult))
                            c.wait()
                            c.step(V.tensor_scalar(gin, gin, 0.044715, 1.0, ALU.mult, ALU.add))
                            c.wait()
                            V.scalar_tensor_tensor(out=gin, in0=gin, scalar=0.7978845608028654, in1=actv,
                                                   op0=ALU.mult, op1=ALU.mult).then_inc(tanh_in.sem, 1)
                            c.step(V.scalar_tensor_tensor(out=coef, in0=actv, scalar=0.5, in1=wts, op0=ALU.mult, op1=ALU.mult))
                            c.wait()
                            dve.wait_ge(tanh_out.sem, tanh_out.at(L, "T", t, 1))
                            c.step(V.scalar_tensor_tensor(out=coef, in0=th, scalar=1.0, in1=coef, op0=ALU.add, op1=ALU.mult))
                            c.wait()
                            c.close()
                        stand(dve)
                        with dve.Fori(j0, j0 + stretch) as j:
                            for q in range(GR):
                                dve.wait_ge(g_ready[q], 16 * ((L * TT + t) * turns + j + 1))
                                if values:
                                    dve.wait_ge(g_used.sem, g_used.at(L, "T", t, q) + GR * j)
                                    V.scalar_tensor_tensor(out=x[:, t, :], in0=gring[:, q, :],
                                                           scalar=coef[:, ds(GR * j + (q - SLOTS), 1)],
                                                           in1=x[:, t, :], op0=ALU.mult, op1=ALU.add)\
                                        .then_inc(g_used.sem, 1)
                                else:
                                    V.scalar_tensor_tensor(out=gring[:, q, :], in0=gring[:, q, :], scalar=1.0,
                                                           in1=hn[:, t, :], op0=ALU.mult, op1=ALU.mult,
                                                           accum_out=actv[:, ds(GR * j + q, 1)]).then_inc(g_used.sem, 1)
                        for _ in range(pieces_by(j0 + stretch) - pieces_by(j0)):
                            next(pieces, None)
                    assert next(pieces, "end") == "end"
                    dve.wait_ge(g_used.sem, g_used.at(L, "T", t, 2 * SLOTS))
                    square_sum(t).then_inc(square_done.sem, 1)

                for _ in choose(0):
                    pass
                stand(dve)
                tile(0, chain(rest_of_keys(), choose(1)), REST_PIECES + PIECES, PIECES)
                stand(dve)
                with dve.Fori(1, TT - 1) as t:
                    tile(t, choose(t + 1), PIECES, PIECES - 3)
                tile(TT - 1)
                dve.wait_ge(g_used.sem, g_used.at(L, "T", TT - 1, 2 * SLOTS))
                V.tensor_scalar(first_expert[:, :], first_expert[:, :], float(N_KEYS * N_KEYS), None, ALU.add)\
                    .then_inc(layer_done.sem, 1)

            dve.wait_ge(square_done.sem, TT * DEPTH + TT)
            mean_square().then_inc(ms_final, 1)
            dve.wait_ge(sd_final, 1)
            V.reciprocal(stat[:, 3, :], stat[:, 2, :]).then_inc(final_step, 1)
            dve.wait_ge(final_step, 2)
            dve.wait_ge(fnw_loaded, 16)
            for t in range(TT):
                scale_rows(t, nwb[:, :]).then_inc(out_ready, 1)


def _rows_of(w, c0, n=P):
    return w[:, c0:c0 + n].reshape(KC, P, n).transpose(1, 0, 2).reshape(P, KC * n)


def _token_chunks(w, c0):
    return [w[2 * P * s:2 * P * (s + 1), c0:c0 + SEQ].reshape(2, P, SEQ).transpose(1, 0, 2).reshape(P, 2 * SEQ)
            for s in range(4)]


def _stream(w_in, w_lru, w_fox, w_ml, w_out, wq):
    chunks = []
    for i in range(2):
        chunks += [_rows_of(w_in, C_LRU + (4 * i + s) * P) for s in range(4)]
    for i in range(2):
        chunks += _token_chunks(w_in, C_FOX + 2 * D + i * SEQ)

    def merge(w, b):
        for j in range(0, KC, 2):
            chunks.extend(_rows_of(w_in, C_GATE + b * D + (j + n) * P) for n in range(2))
            chunks.extend(_rows_of(w, (j + n) * P) for n in range(2))

    def pairs(c0):
        for j in range(KC):
            chunks.append(_rows_of(w_in, c0 + j * P))
            chunks.append(_rows_of(w_in, c0 + D + j * P))

    merge(w_lru, 0)
    pairs(C_FOX)
    for i in range(2):
        chunks += _token_chunks(w_in, C_ML + 2 * D + i * SEQ)
    merge(w_fox, 1)
    for j in range(KC):
        chunks.append(_rows_of(w_in, C_O + j * P))
    pairs(C_ML)
    merge(w_ml, 2)
    for i in range(2):
        chunks += _token_chunks(w_out, i * SEQ)
    for j in range(2 * KC):
        chunks.append(_rows_of(wq, j * P))
    return chunks


def kernel(x, norm1_w, w_in, lru_conv_w, lru_conv_b, lru_wa, lru_ba, lru_wx, lru_bx, lru_lambda,
           fox_fgate_b, mlstm_igate_b, mlstm_fgate_b, mlstm_norm_w, merge_gate_b,
           w_br_lru, w_br_fox, w_br_mlstm, w_out, norm2_w,
           peer_wq, peer_subkeys1, peer_subkeys2, peer_u, peer_v, final_norm_w):
    import concourse.bacc as bacc
    from concourse.bass_utils import run_bass_kernel_spmd as run

    def column(v):
        return np.asarray(v).reshape(-1, P).T

    def column_of(v, n):
        c = np.zeros((P, 1), np.float32)
        c[0:n, 0] = v
        return c

    stream, pvs, lru = [], [], []
    for L in range(DEPTH):
        w = np.asarray(w_in[L])
        stream += _stream(w, np.asarray(w_br_lru[L]), np.asarray(w_br_fox[L]), np.asarray(w_br_mlstm[L]),
                          np.asarray(w_out[L]), np.asarray(peer_wq[L]))
        wgate = np.concatenate([w[:, C_MLF:C_MLF + ML_H], w[:, C_FOXF:C_FOXF + FOX_H],
                                np.zeros((D, I_ROW - NROW), np.float32), w[:, C_MLI:C_MLI + ML_H]], axis=1)
        fb = np.concatenate([np.asarray(mlstm_fgate_b[L]), np.asarray(fox_fgate_b[L])])
        pvs.append(np.concatenate([
            column(lru_conv_w[L]), column(lru_conv_b[L]), column(lru_ba[L]), column(lru_bx[L]),
            column(merge_gate_b[L]), column(lru_lambda[L]), column(mlstm_norm_w[L]),
            column_of(fb, NROW), column_of(np.asarray(mlstm_igate_b[L]), ML_H),
            np.asarray(peer_subkeys1[L]).T, np.asarray(peer_subkeys2[L]).T, _rows_of(wgate, 0, GATES)], axis=1))
        both = np.stack([np.asarray(lru_wa[L]), np.asarray(lru_wx[L])], axis=1)
        lru.append(both.reshape(2, 4, 2, P, P).transpose(0, 3, 1, 2, 4).reshape(2, P, D))
    arrays = {
        "x_in": np.ascontiguousarray(np.asarray(x)[0]),
        "w_stream": np.stack(stream),
        "w_lru": np.concatenate(lru),
        "pvec": np.stack(pvs),
        "nrows": np.stack([np.asarray(a) for L in range(DEPTH) for a in (norm1_w[L], norm2_w[L])]),
        "fnorm": np.asarray(final_norm_w),
        "u_tab": np.asarray(peer_u).reshape(-1, D),
        "v_tab": np.asarray(peer_v).reshape(-1, D),
    }
    nc = bacc.Bacc("TRN2", target_bir_lowering=False, num_devices=1)
    args = [nc.dram_tensor(n, a.shape, mybir.dt.from_np(a.dtype), kind="ExternalInput").ap() for n, a in arrays.items()]
    out = nc.dram_tensor("out", (SEQ, D), F32, kind="ExternalOutput").ap()
    build(nc, *args, out)
    r = run(nc, [arrays], core_ids=[0])
    return r.results[0]["out"].reshape(1, SEQ, D)
```
